# Optimizing a Trainium2 kernel written in Bass

```python
import jax, jax.numpy as jnp
from jax import lax
import numpy as np
import math

D_MODEL = 1024
BATCH = 1
SEQ = 512
DEPTH = 1

D_CONV = D_MODEL // 2
CONV_WIDTH = 31
M_INNER = D_MODEL // 2
M_HEADS = 4
M_HEAD_DIM = M_INNER // M_HEADS
QK_CONV_WIDTH = 4
CHUNK = 64
N_GROUPS = 4
E_PER_GROUP = 8
N_EXPERTS = N_GROUPS * E_PER_GROUP
TOP_K = 2
D_EXPERT = D_MODEL // 2
EXPERT_ROWS = 128
RMS_EPS = 1e-6
LN_EPS = 1e-5
IN_WIDTHS = (D_CONV, D_CONV, M_INNER, M_INNER, M_INNER, M_INNER, M_HEADS, M_HEADS, D_MODEL, D_MODEL)
D_IN = 2 * D_CONV + 4 * M_INNER + 2 * M_HEADS + 2 * D_MODEL


def rmsnorm(x, g):
    xf = x.astype(jnp.float32)
    y = xf * lax.rsqrt(jnp.mean(xf * xf, axis=-1, keepdims=True) + RMS_EPS)
    return (y * g.astype(jnp.float32)).astype(x.dtype)

def layernorm(x, g, b):
    xf = x.astype(jnp.float32)
    mu = jnp.mean(xf, axis=-1, keepdims=True)
    var = jnp.mean(jnp.square(xf - mu), axis=-1, keepdims=True)
    y = (xf - mu) * lax.rsqrt(var + LN_EPS)
    return (y * g.astype(jnp.float32) + b.astype(jnp.float32)).astype(x.dtype)

def modulate(h, shift, scale):
    return h * (1 + scale[:, None, :]) + shift[:, None, :]

def causal_dwconv(u, w, b):
    width = w.shape[0]
    y = lax.conv_general_dilated(
        u, w.astype(u.dtype)[:, None, :], window_strides=(1,), padding=[(width - 1, 0)],
        dimension_numbers=("NWC", "WIO", "NWC"), feature_group_count=u.shape[-1])
    return y + b.astype(u.dtype)

def mlstm_chunkwise(q, k, v, i_pre, f_pre):
    B, S, NH, DH = q.shape
    NC = S // CHUNK
    q = q * (DH ** -0.5)
    lf = jax.nn.log_sigmoid(f_pre)
    li = i_pre

    def to_chunks(a):
        return a.reshape(B, NC, CHUNK, NH, DH).transpose(1, 0, 3, 2, 4)

    def gates_to_chunks(a):
        return a.reshape(B, NC, CHUNK, NH).transpose(1, 0, 3, 2)

    causal = jnp.tril(jnp.ones((CHUNK, CHUNK), dtype=bool))

    def step(carry, xs):
        C, n, m = carry
        qc, kc, vc, lic, lfc = xs
        bcum = jnp.cumsum(lfc, axis=-1)
        dmat = bcum[..., :, None] - bcum[..., None, :] + lic[..., None, :]
        dmat = jnp.where(causal, dmat, -jnp.inf)
        inter = bcum + m[..., None]
        m_t = jnp.maximum(jnp.max(dmat, axis=-1), inter)
        wts = jnp.exp(dmat - m_t[..., None])
        s_inter = jnp.exp(inter - m_t)
        qk = jnp.einsum("bhtd,bhsd->bhts", qc, kc) * wts
        num = jnp.einsum("bhts,bhsd->bhtd", qk, vc) + s_inter[..., None] * jnp.einsum("bhtd,bhde->bhte", qc, C)
        den = jnp.sum(qk, axis=-1) + s_inter * jnp.einsum("bhtd,bhd->bht", qc, n)
        h = num / jnp.maximum(jnp.abs(den), jnp.exp(-m_t))[..., None]
        b_last = bcum[..., -1]
        a = b_last[..., None] - bcum + lic
        m_new = jnp.maximum(b_last + m, jnp.max(a, axis=-1))
        wk = jnp.exp(a - m_new[..., None])
        sc = jnp.exp(b_last + m - m_new)
        C_new = sc[..., None, None] * C + jnp.einsum("bhs,bhsd,bhse->bhde", wk, kc, vc)
        n_new = sc[..., None] * n + jnp.einsum("bhs,bhsd->bhd", wk, kc)
        return (C_new, n_new, m_new), h

    init = (jnp.zeros((B, NH, DH, DH), jnp.float32),
            jnp.zeros((B, NH, DH), jnp.float32),
            jnp.zeros((B, NH), jnp.float32))
    xs = (to_chunks(q), to_chunks(k), to_chunks(v), gates_to_chunks(li), gates_to_chunks(lf))
    _, h = lax.scan(step, init, xs)
    return h.transpose(1, 0, 3, 2, 4).reshape(B, S, NH, DH)

def hybrid_mixer(h, w_in, b_if, conv_dw_w, conv_dw_b, conv_ln_g, conv_ln_b, w_conv_out,
                 qk_conv_w, qk_conv_b, m_norm_g, w_m_out, w_out):
    B, S, _ = h.shape
    z = h @ w_in
    offs = np.cumsum(IN_WIDTHS)[:-1].tolist()
    glu_a, glu_b, q, k, v, o, i_pre, f_pre, g_a, g_b = jnp.split(z, offs, axis=-1)

    u = glu_a * jax.nn.sigmoid(glu_b)
    u = causal_dwconv(u, conv_dw_w, conv_dw_b)
    u = jax.nn.silu(layernorm(u, conv_ln_g, conv_ln_b))
    y_a = u @ w_conv_out

    qk = jax.nn.silu(causal_dwconv(jnp.concatenate([q, k], axis=-1), qk_conv_w, qk_conv_b))
    q, k = jnp.split(qk, 2, axis=-1)
    heads = lambda a: a.astype(jnp.float32).reshape(B, S, M_HEADS, M_HEAD_DIM)
    bif = b_if.astype(jnp.float32)
    i_g = i_pre.astype(jnp.float32) + bif[:M_HEADS]
    f_g = f_pre.astype(jnp.float32) + bif[M_HEADS:]
    hm = mlstm_chunkwise(heads(q), heads(k), heads(v), i_g, f_g)
    mu = jnp.mean(hm, axis=-1, keepdims=True)
    var = jnp.mean(jnp.square(hm - mu), axis=-1, keepdims=True)
    hm = (hm - mu) * lax.rsqrt(var + LN_EPS) * m_norm_g.astype(jnp.float32).reshape(M_HEADS, M_HEAD_DIM)
    hm = hm * jax.nn.sigmoid(heads(o))
    y_b = hm.reshape(B, S, M_INNER).astype(h.dtype) @ w_m_out

    merged = jax.nn.sigmoid(g_a) * y_a + jax.nn.sigmoid(g_b) * y_b
    return merged @ w_out

def hierarchical_moe(h, w_rg, b_rg, w_re, b_re, w_e_gate, w_e_up, w_e_down):
    T, D = h.shape
    hf = h.astype(jnp.float32)
    p_grp = jax.nn.softmax(hf @ w_rg.astype(jnp.float32) + b_rg.astype(jnp.float32), axis=-1)
    g_sel = jnp.argmax(p_grp, axis=-1)
    p_g = jnp.take_along_axis(p_grp, g_sel[:, None], axis=-1)
    le = (hf @ w_re.astype(jnp.float32) + b_re.astype(jnp.float32)).reshape(T, N_GROUPS, E_PER_GROUP)
    le_sel = jnp.take_along_axis(le, g_sel[:, None, None], axis=1)[:, 0]
    top_p, top_e = lax.top_k(jax.nn.softmax(le_sel, axis=-1), TOP_K)
    w_tok = p_g * top_p / jnp.sum(top_p, axis=-1, keepdims=True)
    e_idx = g_sel[:, None] * E_PER_GROUP + top_e

    A = T * TOP_K
    e_flat = e_idx.reshape(A).astype(jnp.int32)
    w_flat = w_tok.reshape(A)
    tok = jnp.arange(A, dtype=jnp.int32) // TOP_K
    order = jnp.argsort(e_flat)
    e_sorted = e_flat[order]
    tok_sorted = tok[order]
    counts = jnp.bincount(e_flat, length=N_EXPERTS)
    padded = (counts + EXPERT_ROWS - 1) // EXPERT_ROWS * EXPERT_ROWS
    starts = jnp.cumsum(counts) - counts
    pends = jnp.cumsum(padded)
    pstarts = pends - padded
    dest = pstarts[e_sorted] + jnp.arange(A, dtype=jnp.int32) - starts[e_sorted]
    n_groups_rows = -(-(A + N_EXPERTS * (EXPERT_ROWS - 1)) // EXPERT_ROWS)
    P = n_groups_rows * EXPERT_ROWS
    xs = jnp.zeros((P, D), h.dtype).at[dest].set(h[tok_sorted])
    grp_e = jnp.minimum(jnp.searchsorted(pends, jnp.arange(n_groups_rows) * EXPERT_ROWS, side="right"),
                        N_EXPERTS - 1)

    def expert_rows(args):
        xb, e = args
        return (jax.nn.silu(xb @ w_e_gate[e]) * (xb @ w_e_up[e])) @ w_e_down[e]

    ys = lax.map(expert_rows, (xs.reshape(n_groups_rows, EXPERT_ROWS, D), grp_e)).reshape(P, D)
    contrib = ys[dest].astype(jnp.float32) * w_flat[order][:, None]
    return jax.ops.segment_sum(contrib, tok_sorted, num_segments=T).astype(h.dtype)

def first_inputs(seed: int = 0) -> dict:
    key = jax.random.key(seed)
    ks = jax.random.split(key, 32)
    L, D = DEPTH, D_MODEL

    def nrm(k, shape, scale):
        return jax.random.normal(k, shape, jnp.float32) * scale

    b_if = jnp.concatenate([
        nrm(ks[6], (L, M_HEADS), 0.1),
        jnp.linspace(3.0, 6.0, M_HEADS, dtype=jnp.float32)[None, :] + nrm(ks[7], (L, M_HEADS), 0.1)], axis=-1)
    return {
        "x": nrm(ks[0], (BATCH, SEQ, D), 1.0),
        "c": nrm(ks[1], (BATCH, D), 1.0),
        "w_ada": nrm(ks[2], (L, D, 6 * D), 0.5 * D ** -0.5),
        "b_ada": nrm(ks[3], (L, 6 * D), 0.02),
        "g_norm1": 1.0 + nrm(ks[4], (L, D), 0.02),
        "w_in": nrm(ks[5], (L, D, D_IN), D ** -0.5),
        "b_if": b_if,
        "conv_dw_w": nrm(ks[8], (L, CONV_WIDTH, D_CONV), CONV_WIDTH ** -0.5),
        "conv_dw_b": nrm(ks[9], (L, D_CONV), 0.02),
        "conv_ln_g": 1.0 + nrm(ks[10], (L, D_CONV), 0.02),
        "conv_ln_b": nrm(ks[11], (L, D_CONV), 0.02),
        "w_conv_out": nrm(ks[12], (L, D_CONV, D), D_CONV ** -0.5),
        "qk_conv_w": nrm(ks[13], (L, QK_CONV_WIDTH, 2 * M_INNER), QK_CONV_WIDTH ** -0.5),
        "qk_conv_b": nrm(ks[14], (L, 2 * M_INNER), 0.02),
        "m_norm_g": 1.0 + nrm(ks[15], (L, M_INNER), 0.02),
        "w_m_out": nrm(ks[16], (L, M_INNER, D), M_INNER ** -0.5),
        "w_out": nrm(ks[17], (L, D, D), D ** -0.5),
        "g_norm2": 1.0 + nrm(ks[18], (L, D), 0.02),
        "w_rg": nrm(ks[19], (L, D, N_GROUPS), D ** -0.5),
        "b_rg": nrm(ks[20], (L, N_GROUPS), 0.01),
        "w_re": nrm(ks[21], (L, D, N_EXPERTS), D ** -0.5),
        "b_re": nrm(ks[22], (L, N_EXPERTS), 0.01),
        "w_e_gate": nrm(ks[23], (L, N_EXPERTS, D, D_EXPERT), D ** -0.5),
        "w_e_up": nrm(ks[24], (L, N_EXPERTS, D, D_EXPERT), D ** -0.5),
        "w_e_down": nrm(ks[25], (L, N_EXPERTS, D_EXPERT, D), D_EXPERT ** -0.5),
        "g_final": 1.0 + nrm(ks[26], (D,), 0.02),
    }

def first_block(x, c, w_ada, b_ada, g_norm1, w_in, b_if, conv_dw_w, conv_dw_b, conv_ln_g, conv_ln_b,
              w_conv_out, qk_conv_w, qk_conv_b, m_norm_g, w_m_out, w_out, g_norm2, w_rg, b_rg,
              w_re, b_re, w_e_gate, w_e_up, w_e_down, g_final):
    B, S, D = x.shape
    for l in range(DEPTH):
        mod = jax.nn.silu(c) @ w_ada[l] + b_ada[l]
        sh1, sc1, gt1, sh2, sc2, gt2 = jnp.split(mod, 6, axis=-1)
        h = modulate(rmsnorm(x, g_norm1[l]), sh1, sc1)
        y = hybrid_mixer(h, w_in[l], b_if[l], conv_dw_w[l], conv_dw_b[l], conv_ln_g[l], conv_ln_b[l],
                         w_conv_out[l], qk_conv_w[l], qk_conv_b[l], m_norm_g[l], w_m_out[l], w_out[l])
        x = x + gt1[:, None, :] * y
        h = modulate(rmsnorm(x, g_norm2[l]), sh2, sc2)
        y = hierarchical_moe(h.reshape(B * S, D), w_rg[l], b_rg[l], w_re[l], b_re[l],
                             w_e_gate[l], w_e_up[l], w_e_down[l]).reshape(B, S, D)
        x = x + gt2[:, None, :] * y
    return rmsnorm(x, g_final)


DEPTH_2 = 2

N_A_LAYERS = DEPTH_2 // 2
N_B_LAYERS = DEPTH_2 - N_A_LAYERS

A_HEADS = 8
A_DK = 128
A_DV = 128
A_CONV = 4
A_CHUNK = 64
A_QK = A_HEADS * A_DK
A_V = A_HEADS * A_DV
A_IN = 2 * A_QK + 2 * A_V + 2 * A_HEADS

B_HEADS = 16
B_KV_HEADS = 4
B_GROUP = B_HEADS // B_KV_HEADS
B_DH = 64
B_WINDOW = 128
B_BLOCK = 128

FFN_DIM = 2816
FFN_CONV = 3

EPS = 1e-6


def rmsnorm_2(x, g):
    xf = x.astype(jnp.float32)
    y = xf * lax.rsqrt(jnp.mean(xf * xf, axis=-1, keepdims=True) + EPS)
    return (y * g.astype(jnp.float32)).astype(x.dtype)

def l2norm(x):
    return x * lax.rsqrt(jnp.sum(x * x, axis=-1, keepdims=True) + EPS)

def causal_dwconv_2(x, w):
    K = w.shape[0]
    S = x.shape[1]
    xp = jnp.pad(x, ((0, 0), (K - 1, 0), (0, 0)))
    y = xp[:, K - 1:K - 1 + S] * w[K - 1]
    for j in range(K - 1):
        y = y + xp[:, j:j + S] * w[j]
    return y

def gated_delta_rule_chunked(q, k, v, beta, g):
    Bsz, S, H, DK = q.shape
    DV = v.shape[-1]
    C = A_CHUNK
    N = S // C

    def chunk(t):
        t = t.reshape((Bsz, N, C, H) + t.shape[3:])
        return jnp.moveaxis(t, 3, 1)

    q, k, v, beta, g = chunk(q), chunk(k), chunk(v), chunk(beta), chunk(g)
    gc = jnp.cumsum(g, axis=-1)
    idx = jnp.arange(C)
    strict = idx[:, None] > idx[None, :]
    incl = idx[:, None] >= idx[None, :]
    diff = gc[..., :, None] - gc[..., None, :]
    decay = jnp.exp(jnp.where(incl, diff, -jnp.inf))
    kb = k * beta[..., None]
    Lmat = jnp.where(strict, jnp.einsum('bhnid,bhnjd->bhnij', kb, k) * decay, 0.0)
    eye = jnp.eye(C, dtype=Lmat.dtype)
    rhs = jnp.concatenate([v * beta[..., None], kb * jnp.exp(gc)[..., None]], axis=-1)
    sol = lax.linalg.triangular_solve(eye + Lmat, rhs, left_side=True, lower=True, unit_diagonal=True)
    value, k_cumdecay = sol[..., :DV], sol[..., DV:]
    attn_intra = jnp.einsum('bhnid,bhnjd->bhnij', q, k) * decay
    q_dec = q * jnp.exp(gc)[..., None]
    k_dec = k * jnp.exp(gc[..., -1:] - gc)[..., None]
    g_last = jnp.exp(gc[..., -1])

    def step(state, xs):
        a_c, qd, kd, val, kcd, gl = xs
        v_new = val - jnp.einsum('bhcd,bhde->bhce', kcd, state)
        o = jnp.einsum('bhcd,bhde->bhce', qd, state) + jnp.einsum('bhij,bhje->bhie', a_c, v_new)
        state = state * gl[..., None, None] + jnp.einsum('bhcd,bhce->bhde', kd, v_new)
        return state, o

    xs = tuple(jnp.moveaxis(t, 2, 0) for t in (attn_intra, q_dec, k_dec, value, k_cumdecay, g_last))
    state0 = jnp.zeros((Bsz, H, DK, DV), jnp.float32)
    _, o = lax.scan(step, state0, xs)
    o = jnp.moveaxis(jnp.moveaxis(o, 0, 2), 1, 3)
    return o.reshape(Bsz, S, H, DV)

def deltanet_mixer(h, w_in, conv_w, A_log, dt_bias, onorm_g, w_out):
    Bsz, S, _ = h.shape
    f32 = jnp.float32
    p = h @ w_in
    qkv, gate, b_raw, a_raw = jnp.split(p, [2 * A_QK + A_V, 2 * A_QK + 2 * A_V, 2 * A_QK + 2 * A_V + A_HEADS], axis=-1)
    qkv = jax.nn.silu(causal_dwconv_2(qkv, conv_w))
    q, k, v = jnp.split(qkv, [A_QK, 2 * A_QK], axis=-1)
    q = l2norm(q.reshape(Bsz, S, A_HEADS, A_DK).astype(f32)) * (A_DK ** -0.5)
    k = l2norm(k.reshape(Bsz, S, A_HEADS, A_DK).astype(f32))
    v = v.reshape(Bsz, S, A_HEADS, A_DV).astype(f32)
    beta = jax.nn.sigmoid(b_raw.astype(f32))
    g = -jnp.exp(A_log.astype(f32)) * jax.nn.softplus(a_raw.astype(f32) + dt_bias.astype(f32))
    o = gated_delta_rule_chunked(q, k, v, beta, g)
    o = rmsnorm_2(o, onorm_g) * jax.nn.silu(gate.reshape(Bsz, S, A_HEADS, A_DV).astype(f32))
    return o.reshape(Bsz, S, A_V).astype(h.dtype) @ w_out

def swa_sink_attention(h, k_sh, v_sh, w_q, b_q, sinks, w_o, b_o):
    Bsz, S, _ = h.shape
    f32 = jnp.float32
    NB = S // B_BLOCK
    q = (h @ w_q + b_q).astype(f32) * (B_DH ** -0.5)
    q = q.reshape(Bsz, NB, B_BLOCK, B_KV_HEADS, B_GROUP, B_DH)

    def with_prev(t):
        t = t.astype(f32).reshape(Bsz, NB, B_BLOCK, B_KV_HEADS, B_DH)
        prev = jnp.pad(t, ((0, 0), (1, 0), (0, 0), (0, 0), (0, 0)))[:, :-1]
        return jnp.concatenate([prev, t], axis=2)

    kb, vb = with_prev(k_sh), with_prev(v_sh)
    slopes = (2.0 ** (-8.0 * jnp.arange(1, B_HEADS + 1, dtype=f32) / B_HEADS)).reshape(B_KV_HEADS, B_GROUP)
    qi = jnp.arange(B_BLOCK)[:, None]
    kj = jnp.arange(2 * B_BLOCK)[None, :]
    dist = qi + B_BLOCK - kj
    band = (dist >= 0) & (dist < B_WINDOW)
    bias = -slopes[:, :, None, None] * dist.astype(f32)
    sink = sinks.astype(f32).reshape(B_KV_HEADS, B_GROUP)[None, :, :, None]

    def block_attn(args):
        qb, kk, vv, blk = args
        s = jnp.einsum('bqkgd,bskd->bkgqs', qb, kk) + bias
        valid = band & ((blk > 0) | (kj >= B_BLOCK))
        s = jnp.where(valid, s, -jnp.inf)
        m = jnp.maximum(jnp.max(s, axis=-1), sink)
        p = jnp.exp(s - m[..., None])
        denom = jnp.sum(p, axis=-1) + jnp.exp(sink - m)
        o = jnp.einsum('bkgqs,bskd->bqkgd', p, vv)
        return o / jnp.transpose(denom, (0, 3, 1, 2))[..., None]

    xs = (jnp.moveaxis(q, 1, 0), jnp.moveaxis(kb, 1, 0), jnp.moveaxis(vb, 1, 0), jnp.arange(NB, dtype=jnp.int32))
    o = lax.map(block_attn, xs)
    o = jnp.moveaxis(o, 0, 1).reshape(Bsz, S, B_HEADS * B_DH)
    return o.astype(h.dtype) @ w_o + b_o

def conv_ffn(h, w_up, conv_w, conv_b, w_down):
    u = causal_dwconv_2(h @ w_up, conv_w) + conv_b
    gate, up = jnp.split(u, 2, axis=-1)
    return (jax.nn.silu(gate) * up) @ w_down

def second_inputs(seed: int = 0) -> dict:
    key = jax.random.key(seed)
    ks = jax.random.split(key, 24)
    f32 = jnp.float32

    def nrm(k, shape, fan_in):
        return jax.random.normal(k, shape, f32) * (fan_in ** -0.5)

    def gain(k, shape):
        return 1.0 + 0.05 * jax.random.normal(k, shape, f32)

    def small(k, shape):
        return 0.02 * jax.random.normal(k, shape, f32)

    x = jax.random.normal(ks[0], (BATCH, SEQ, D_MODEL), f32)
    a_norm = gain(ks[1], (N_A_LAYERS, D_MODEL))
    a_w_in = nrm(ks[2], (N_A_LAYERS, D_MODEL, A_IN), D_MODEL)
    a_conv_w = nrm(ks[3], (N_A_LAYERS, A_CONV, 2 * A_QK + A_V), A_CONV)
    a_A_log = jnp.log(jax.random.uniform(ks[4], (N_A_LAYERS, A_HEADS), f32, 1.0, 16.0))
    dt = jnp.exp(jax.random.uniform(ks[5], (N_A_LAYERS, A_HEADS), f32, math.log(1e-3), math.log(1e-1)))
    a_dt_bias = dt + jnp.log(-jnp.expm1(-dt))
    a_onorm = gain(ks[6], (N_A_LAYERS, A_DV))
    a_w_out = nrm(ks[7], (N_A_LAYERS, A_V, D_MODEL), A_V)
    kv_norm = gain(ks[8], (D_MODEL,))
    kv_w = nrm(ks[9], (D_MODEL, 2 * B_KV_HEADS * B_DH), D_MODEL)
    kv_b = small(ks[10], (2 * B_KV_HEADS * B_DH,))
    b_norm = gain(ks[11], (N_B_LAYERS, D_MODEL))
    b_w_q = nrm(ks[12], (N_B_LAYERS, D_MODEL, B_HEADS * B_DH), D_MODEL)
    b_b_q = small(ks[13], (N_B_LAYERS, B_HEADS * B_DH))
    b_sinks = jax.random.normal(ks[14], (N_B_LAYERS, B_HEADS), f32)
    b_w_o = nrm(ks[15], (N_B_LAYERS, B_HEADS * B_DH, D_MODEL), B_HEADS * B_DH)
    b_b_o = small(ks[16], (N_B_LAYERS, D_MODEL))
    f_norm = gain(ks[17], (DEPTH_2, D_MODEL))
    f_w_up = nrm(ks[18], (DEPTH_2, D_MODEL, 2 * FFN_DIM), D_MODEL)
    f_conv_w = nrm(ks[19], (DEPTH_2, FFN_CONV, 2 * FFN_DIM), FFN_CONV)
    f_conv_b = small(ks[20], (DEPTH_2, 2 * FFN_DIM))
    f_w_down = nrm(ks[21], (DEPTH_2, FFN_DIM, D_MODEL), FFN_DIM)
    final_norm = gain(ks[22], (D_MODEL,))
    return {'x': x, 'a_norm': a_norm, 'a_w_in': a_w_in, 'a_conv_w': a_conv_w, 'a_A_log': a_A_log,
            'a_dt_bias': a_dt_bias, 'a_onorm': a_onorm, 'a_w_out': a_w_out,
            'kv_norm': kv_norm, 'kv_w': kv_w, 'kv_b': kv_b,
            'b_norm': b_norm, 'b_w_q': b_w_q, 'b_b_q': b_b_q, 'b_sinks': b_sinks, 'b_w_o': b_w_o, 'b_b_o': b_b_o,
            'f_norm': f_norm, 'f_w_up': f_w_up, 'f_conv_w': f_conv_w, 'f_conv_b': f_conv_b, 'f_w_down': f_w_down,
            'final_norm': final_norm}

def second_block(x, a_norm, a_w_in, a_conv_w, a_A_log, a_dt_bias, a_onorm, a_w_out,
              kv_norm, kv_w, kv_b,
              b_norm, b_w_q, b_b_q, b_sinks, b_w_o, b_b_o,
              f_norm, f_w_up, f_conv_w, f_conv_b, f_w_down, final_norm):
    Bsz, S, _ = x.shape
    h = x
    k_sh = None
    v_sh = None
    for layer in range(DEPTH_2):
        if layer < N_A_LAYERS:
            i = layer
            h = h + deltanet_mixer(rmsnorm_2(h, a_norm[i]), a_w_in[i], a_conv_w[i], a_A_log[i],
                                   a_dt_bias[i], a_onorm[i], a_w_out[i])
        else:
            i = layer - N_A_LAYERS
            if i == 0:
                kv = rmsnorm_2(h, kv_norm) @ kv_w + kv_b
                k_sh, v_sh = jnp.split(kv, 2, axis=-1)
                k_sh = k_sh.reshape(Bsz, S, B_KV_HEADS, B_DH)
                v_sh = v_sh.reshape(Bsz, S, B_KV_HEADS, B_DH)
            h = h + swa_sink_attention(rmsnorm_2(h, b_norm[i]), k_sh, v_sh, b_w_q[i], b_b_q[i],
                                       b_sinks[i], b_w_o[i], b_b_o[i])
        h = h + conv_ffn(rmsnorm_2(h, f_norm[layer]), f_w_up[layer], f_conv_w[layer],
                         f_conv_b[layer], f_w_down[layer])
    return rmsnorm_2(h, final_norm)


def setup_inputs(seed=0):
    out = dict(first_inputs(seed))
    for name, value in second_inputs(seed + 1).items():
        if name != "x":
            out[name + "_2"] = value
    return out


def reference(
    x, c, w_ada, b_ada, g_norm1, w_in, b_if, conv_dw_w, conv_dw_b, conv_ln_g, conv_ln_b,
    w_conv_out, qk_conv_w, qk_conv_b, m_norm_g, w_m_out, w_out, g_norm2, w_rg, b_rg, w_re, b_re,
    w_e_gate, w_e_up, w_e_down, g_final, a_norm_2, a_w_in_2, a_conv_w_2, a_A_log_2, a_dt_bias_2,
    a_onorm_2, a_w_out_2, kv_norm_2, kv_w_2, kv_b_2, b_norm_2, b_w_q_2, b_b_q_2, b_sinks_2,
    b_w_o_2, b_b_o_2, f_norm_2, f_w_up_2, f_conv_w_2, f_conv_b_2, f_w_down_2, final_norm_2,
):
    x = first_block(
        x, c, w_ada, b_ada, g_norm1, w_in, b_if, conv_dw_w, conv_dw_b, conv_ln_g, conv_ln_b,
        w_conv_out, qk_conv_w, qk_conv_b, m_norm_g, w_m_out, w_out, g_norm2, w_rg, b_rg, w_re,
        b_re, w_e_gate, w_e_up, w_e_down, g_final,
    )
    return second_block(
        x, a_norm_2, a_w_in_2, a_conv_w_2, a_A_log_2, a_dt_bias_2, a_onorm_2, a_w_out_2,
        kv_norm_2, kv_w_2, kv_b_2, b_norm_2, b_w_q_2, b_b_q_2, b_sinks_2, b_w_o_2, b_b_o_2,
        f_norm_2, f_w_up_2, f_conv_w_2, f_conv_b_2, f_w_down_2, final_norm_2,
    )


_drawn_inputs = setup_inputs


def setup_inputs(seed=0):
    import zlib

    import numpy as np

    out = dict(_drawn_inputs(seed))
    spreads = {}
    factors = {'g_norm1': 6.671,
     'conv_dw_b': 5.256,
     'conv_ln_g': 8.0,
     'conv_ln_b': 6.669,
     'qk_conv_b': 7.338,
     'm_norm_g': 8.0,
     'g_norm2': 3.239,
     'b_rg': 8.0,
     'b_re': 8.0,
     'kv_norm_2': 3.631,
     'kv_b_2': 3.668,
     'b_norm_2': 6.147,
     'b_b_q_2': 8.0,
     'b_b_o_2': 9.834,
     'f_conv_b_2': 2.992,
     'b_sinks_2': 7.7}
    for name, (base, spread) in spreads.items():
        noise = np.random.default_rng([zlib.crc32(name.encode()), seed]).standard_normal(out[name].shape)
        drawn = base * np.exp(spread * noise) if base else spread * noise
        out[name] = __import__('jax').numpy.asarray(drawn.astype(out[name].dtype))
    for name, factor in factors.items():
        out[name] = (out[name] * factor).astype(out[name].dtype)
    return out
```

```python
from contextlib import ExitStack

import numpy as np

import concourse.bass as bass
from concourse import mybir

ALU = mybir.AluOpType
ACT = mybir.ActivationFunctionType
AX = mybir.AxisListType.X
F32 = mybir.dt.float32
I32 = mybir.dt.int32

P = 128
D = 1024
T = 512
KD = D // P
NT = T // P
NEG = -1.0e30

DC = 512
CT = DC // P
TAPS = 31
QTAPS = 4
MH = 4
E = 32
NG = 4
EPG = 8
NB = 2 * T // P + E
DH = 8
LEVELS = 7
AH = 16
HD = 64
KVH = 4
FF = 2816
FT = FF // P
FU = 11

VECS = [("c", 8), ("b_ada", 48), ("g_norm1", 8), ("conv_dw_w", TAPS * 4), ("conv_dw_b", 4), ("conv_ln_g", 4),
        ("conv_ln_b", 4), ("qk_conv_w", 32), ("qk_conv_b", 8), ("m_norm_g", 4), ("g_norm2", 8), ("g_final", 8),
        ("a_norm", 8), ("a_conv_w", 96), ("a_onorm", 1), ("kv_norm", 8), ("kv_b", 2), ("b_norm", 8), ("b_b_q", 8),
        ("b_b_o", 8), ("f_norm", 16), ("f_conv_w", 2 * 3 * 44), ("f_conv_b", 2 * 44), ("final_norm", 8)]
VOFF, NVEC = {}, 0
for _n, _w in VECS:
    VOFF[_n] = NVEC
    NVEC += _w
ROWS = [("b_router", NG + E), ("a_gate", 2 * DH), ("kv_b_v", 256), ("sinks", AH)]
ROFF, NROW = {}, 0
for _n, _w in ROWS:
    ROFF[_n] = NROW
    NROW += _w
CONSTS = [("ident", P), ("ones", P), ("after", P), ("tri_strict", P), ("tri_incl", P),
          ("iota4", NG), ("iota8", EPG), ("iotab", NB)]
COFF, NCST = {}, 0
for _n, _w in CONSTS:
    COFF[_n] = NCST
    NCST += _w

UNITS1 = (["ada0", "ada1", "ada2", "ada3", "in0", "in1", "ada4", "in2", "ada5", "in3", "ada6", "in4", "ada7", "in5",
           "ada8", "in6", "ada9", "in7", "ada10", "in8", "ada11", "in9", "conv_out", "m_out", "w_out0", "w_out1"])
UNITS2 = ([f"a_in{i}" for i in range(8)] + ["a_out0", "a_out1"] + [f"up0_{i}" for i in range(FU)]
          + [f"down0_{i}" for i in range(6)] + ["kv", "w_q0", "w_q1", "w_o0", "w_o1"]
          + [f"up1_{i}" for i in range(FU)] + [f"down1_{i}" for i in range(6)])
UNITS = UNITS1 + UNITS2
NU1, NU = len(UNITS1), len(UNITS)
UIDX = {n: i for i, n in enumerate(UNITS)}

GROUPS = ([([f"in{i}"], "A") for i in range(10)] + [(["conv_out"], "D")] * 2 + [(["m_out"], "D")] * 2
          + [(["w_out0"], "X"), (["w_out1"], "X")]
          + [([f"a_in{i}"], "D" if i < 6 else "A") for i in range(8)] + [(["a_out0"], "X"), (["a_out1"], "X")]
          + [([f"up0_{i}"], "D") for i in range(FU)] + [([f"down0_{3 * m + i}" for i in range(3)], "X") for m in range(2)]
          + [(["kv"], "D"), (["w_q0"], "D"), (["w_q1"], "D"), (["w_o0"], "X"), (["w_o1"], "X")]
          + [([f"up1_{i}"], "D") for i in range(FU)] + [([f"down1_{3 * m + i}" for i in range(3)], "X") for m in range(2)])
G_CONV, G_MOUT, G_WOUT, G_AIN, G_AOUT, G_UP0, G_DN0, G_KV, G_WQ, G_WO, G_UP1, G_DN1 = 10, 12, 14, 16, 24, 26, 37, 39, 40, 42, 44, 55
TILE_DONE, UNIT_USED, EMPTIED = [], {}, []
_mm, _ev = 0, {"A": 0, "D": 0, "X": 0}
for _us, _e in GROUPS:
    if _us[0] == "a_out0":
        _ev["X"] += 2 * KD
    for _u in _us[:-1]:
        _mm += 1
        UNIT_USED[_u] = _mm
    TILE_DONE.append([_mm + j + 1 for j in range(4)])
    _mm += 4
    UNIT_USED[_us[-1]] = _mm
    _ev[_e] += 4
    EMPTIED.append((_e, _ev[_e]))


def build(nc, xt_in, wall, wexp, w_if, w_router, w_ab, vecs, rows, b_if, cst_in, ints, att_bias, levels_in, out_t):
    f_tok = nc.dram_tensor("h2_tokens", [T, D], F32, kind="Internal").ap()
    y_asg = nc.dram_tensor("y_assignments", [2 * T, D], F32, kind="Internal").ap()
    slots = nc.dram_tensor("slot_table", [(NB + 2) * P, 2], I32, kind="Internal").ap()

    ctx = ExitStack()
    with ctx:
        def sb(name, shape, dt=F32):
            return ctx.enter_context(nc.sbuf_tensor(name, shape, dt))

        sems = {}

        def S(name):
            if name not in sems:
                sems[name] = ctx.enter_context(nc.semaphore(name))
            return sems[name]

        PS = ctx.enter_context(nc.psum_tensor("PS", [P, 8, 512], F32))
        x = sb("x", [P, KD, T])
        h = sb("h", [P, KD, T])
        ring = sb("ring", [P, 2, 8, 512])
        A = sb("A", [P, 59, 512])
        sq = sb("sq", [P, 2, T])
        rstd = sb("rstd", [P, T])
        vec = sb("vec", [P, NVEC])
        row = sb("row", [P, NROW])
        cst = sb("cst", [P, NCST])
        eps = sb("eps", [P, 4])
        mod = sb("mod", [P, 48])
        gm = sb("gm", [P, 2, KD])
        silc = sb("silc", [P, KD])

        def V(name, i=0, n=1):
            return vec[:, VOFF[name] + i:VOFF[name] + i + n]

        def C(name):
            w = dict(CONSTS)[name]
            return cst[:, COFF[name]:COFF[name] + w]

        def R(name):
            w = dict(ROWS)[name]
            return row[:, ROFF[name]:ROFF[name] + w]

        ident, ones = C("ident"), C("ones")

        wif = sb("wif", [P, KD, 64])
        bif = sb("bif", [64, 1])
        gr = [A[0:4, u, :] for u in (44, 45, 46, 47, 48, 56, 57, 58)]
        gT = sb("gT", [P, NT, MH])
        wrt = sb("wrt", [P, KD, NG + E])
        tok = sb("tok", [P, 8, 2], I32)
        idx = sb("idx", [P, 2, 2], I32)
        sidx = sb("sidx", [P, 2, 2], I32)
        wtok = sb("wtok", [P, 2, NT])
        blki = sb("blki", [1, NB + 2], I32)

        used_r = [0]

        def carve(*dims):
            n = int(np.prod(dims))
            v = A[:, 48:59, :].rearrange("p a b -> p (a b)")[:, used_r[0]:used_r[0] + n]
            used_r[0] += n
            if len(dims) == 2:
                return v.rearrange("p (a b) -> p a b", b=dims[1])
            if len(dims) == 3:
                return v.rearrange("p (a b c) -> p a b c", b=dims[1], c=dims[2])
            return v

        lg = carve(NT, NG + E)
        rs = [carve(NT) for _ in range(14)]
        r4 = [carve(NT, NG) for _ in range(3)]
        r8 = [carve(NT, EPG) for _ in range(5)]
        asg = [carve(NT, E) for _ in range(5)]
        er = [carve(E) for _ in range(6)]
        blk = carve(NB, E)
        blkf = carve(NB + 2)
        assert used_r[0] <= 11 * 512
        posi = sb("posi", [P, 2, NT], I32)
        wab = sb("wab", [P, KD, 2 * DH])
        levels = sb("levels", [P, LEVELS, P])
        ab = sb("ab", [P, NT, 2 * DH])
        dl = [sb(f"dl{i}", [P, NT, DH]) for i in range(6)]
        glast = sb("glast", [P, DH])
        sm = [sb(f"sm{i}", [P, 2, 8]) for i in range(4)]

        moe_w = [[ring[:, 0], ring[:, 1], A[:, 0:8]], [A[:, 8:16], A[:, 16:24], A[:, 24:32]]]
        xg = [A[:, 32 + 2 * j:34 + 2 * j, :] for j in range(2)]
        xgT = [A[:, 36 + 2 * j:38 + 2 * j, :] for j in range(2)]
        hid = [A[:, 40 + j, :] for j in range(2)]
        hidT = [A[:, 42 + j, :] for j in range(2)]
        yb = [A[:, 44 + 2 * j:46 + 2 * j, :] for j in range(2)]
        PAIRS_MIN = 2 * T // T * (T // P) // 2
        PAIRS_MAX = NB // 2

        def last1(ap, shape):
            return ap.broadcast_to(shape)

        def rwait(eng, sem, value):
            eng.wait_ge(sem, value)
            eng.sem_inc(S("waits"), 1)

        def pairs(eng):
            eng.wait_ge(S("blocks"), 1)
            return eng.value_load(blki[0:1, NB:NB + 1], min_val=PAIRS_MIN, max_val=PAIRS_MAX)

        block = ctx.enter_context(nc.Block())

        def freed(eng, g):
            if g >= 0:
                e, n = EMPTIED[g]
                eng.wait_ge(S({"A": "ev_act", "D": "ev_dve", "X": "xt"}[e]), n)

        def unit_slot(name):
            return UIDX[name] % 2

        def unit_here(eng, name):
            u = UIDX[name]
            eng.wait_ge(S(f"unit{u % 2}"), 16 * (u // 2 + 1))

        @block.sync
        def _(sp):
            sp.dma_start(vec[:], vecs).then_inc(S("small"), 16)
            sp.dma_start(cst[:], cst_in).then_inc(S("small"), 16)
            sp.dma_start(bif[0:4], b_if[0:4]).then_inc(S("small"), 16)
            sp.dma_start(bif[32:36], b_if[4:8]).then_inc(S("small"), 16)
            sp.dma_start(row[:], rows.partition_broadcast(P)).then_inc(S("small"), 16)
            sp.dma_start(x[:], xt_in).then_inc(S("x_in"), 16)
            sp.dma_start(wif[:], w_if).then_inc(S("small2"), 16)
            sp.dma_start(wrt[:], w_router).then_inc(S("small2"), 16)
            sp.dma_start(tok[:], ints[:, 0:16].rearrange("p (a b) -> p a b", b=2)).then_inc(S("small2"), 16)
            sp.dma_start(slots.rearrange("(p a) b -> p (a b)", p=P), ints[:, 16:16 + 2 * (NB + 2)]).then_inc(S("slots0"), 16)
            for u in range(NU1):
                if u >= 2:
                    name = UNITS[u - 2]
                    if name.startswith("ada"):
                        sp.wait_ge(S("ada_used"), int(name[3:]) + 1)
                    else:
                        sp.wait_ge(S("mm"), UNIT_USED[name])
                sp.dma_start(ring[:, u % 2], wall[u]).then_inc(S(f"unit{u % 2}"), 16)

            for t in range(NT):
                sp.wait_ge(S("ht_ev"), t + 1)
                sp.dma_start(f_tok[t * P:(t + 1) * P, :], A[:, 2 * t:2 * t + 2, :].rearrange("p a b -> p (a b)")).then_inc(S("f_tok"), 16)
            n = pairs(sp)
            sp.wait_ge(S("f_tok"), 16 * NT)

            def expert(b, j, part):
                e = sp.value_load(blki[0:1, bass.ds(b, 1)], min_val=0, max_val=E - 1)
                return wexp[bass.ds(e, 1), part].rearrange("a p k n -> p (a k) n")

            order = [(0, 0), (0, 1), (1, 0), (1, 1), (0, 2), (1, 2)]
            for j, part in order:
                sp.dma_start(moe_w[j][part], expert(j, j, part)).then_inc(S(f"w{j}{part}"), 16)
            with sp.Fori(1, n) as i:
                for j, part in order:
                    rwait(sp, S("m_dn" if part == 2 else "m_gu"), 2 * i + j - 1)
                    sp.dma_start(moe_w[j][part], expert(2 * i + j, j, part)).then_inc(S(f"w{j}{part}"), 16)
            for j in range(2):
                rwait(sp, S(f"sc{j}"), 16 * n + 16 * NT)
            rwait(sp, S("m_dn"), 2 * n)
            for u in range(NU1, NU1 + 2):
                sp.dma_start(ring[:, u % 2], wall[u]).then_inc(S(f"unit{u % 2}"), 16)
            for t in range(NT):
                sp.dma_start(A[:, 4 * t:4 * t + 4, :], y_asg.rearrange("(t p c) d -> t p (c d)", p=P, c=2)[t]).then_inc(S("y2"), 16)

            sp.dma_start(wab[:], w_ab).then_inc(S("small3"), 16)
            sp.dma_start(levels[:], levels_in.rearrange("p (l f) -> p l f", f=P)).then_inc(S("small3"), 16)

            def load(u):
                sp.wait_ge(S("mm"), UNIT_USED[UNITS[u - 2]])
                sp.dma_start(ring[:, u % 2], wall[u]).then_inc(S(f"unit{u % 2}"), 16)

            def load_up(layer):
                u0 = UIDX[f"up{layer}_0"]
                load(u0)
                load(u0 + 1)
                with sp.Fori(0, (FU - 3) // 2) as i:
                    for j in range(2):
                        sp.wait_ge(S("mm"), 8 * i + UNIT_USED[UNITS[u0 + j]])
                        sp.dma_start(ring[:, (u0 + j) % 2], wall[bass.ds(2 * i + u0 + 2 + j, 1)].rearrange("a p k n -> p (a k) n")).then_inc(S(f"unit{(u0 + j) % 2}"), 16)
                load(u0 + FU - 1)

            for u in range(NU1 + 2, UIDX["up0_0"]):
                load(u)
            load_up(0)
            for u in range(UIDX["down0_0"], UIDX["w_q1"] + 1):
                load(u)
            sp.wait_ge(S("xt"), 40)
            sp.dma_start(A[:, 12:20, :], att_bias.rearrange("p a b -> p (a b)").rearrange("p (a b) -> p a b", b=512)).then_inc(S("bias"), 16)
            for u in range(UIDX["w_q1"] + 1, UIDX["up1_0"]):
                load(u)
            load_up(1)
            for u in range(UIDX["down1_0"], NU):
                load(u)
            sp.wait_ge(S("h"), 56)
            sp.dma_start(out_t, h[:]).then_inc(S("out"), 16)
            sp.wait_ge(S("out"), 16)

        @block.tensor
        def _(pe):
            mm = nc.tensor.matmul

            def group(g, k_tiles, rhs, lhs=None, k0=0):
                name = GROUPS[g][0][0]
                unit_here(pe, name)
                freed(pe, g - 2)
                if 3 <= g <= 9:
                    ada(g + 1, 4 * (g % 2) + 3)
                w = ring[:, unit_slot(name)]
                for j in range(4):
                    if 3 <= g <= 9 and j == 3:
                        pe.wait_ge(S("mod_ev"), g + 2)
                    for k in range(k_tiles):
                        last = mm(PS[:, 4 * (g % 2) + j, :], w[:, k0 + k, j * P:(j + 1) * P] if lhs is None else lhs(j, k, w),
                                  rhs(k) if lhs is None else rhs(k, w), start=k == 0, stop=k == k_tiles - 1)
                    last.then_inc(S("mm"), 1)

            def wait_h(n):
                pe.wait_ge(S("h"), KD * (n + 1))

            def norm(n, bank):
                for k in range(KD):
                    pe.wait_ge(S("sq"), KD * n + k + 1)
                    mm(PS[:, bank, :], ones, sq[:, k % 2, :], start=k == 0, stop=k == KD - 1).then_inc(S("sq_used"), 1)

            pe.wait_ge(S("small"), 80)
            norm(0, 0)

            def ada(a, bank):
                pe.wait_ge(S("ada_used"), a + 1)
                for j in range(4):
                    last = mm(PS[:, bank, j:j + 1], A[:, 52 + a % 2, j * P:(j + 1) * P], ones[:, 0:1], start=True, stop=True)
                last.then_inc(S("ada_sum"), 1)

            for a in range(4):
                ada(a, 1 + a)
            wait_h(0)
            pe.wait_ge(S("small2"), 48)
            for k in range(KD):
                last = mm(PS[0:64, 4, :], wif[:, k, :], h[:, k, :], start=k == 0, stop=k == KD - 1)
            last.then_inc(S("if_mm"), 1)
            for g in range(10):
                if g == 1:
                    pe.wait_ge(S("if_ev"), 2)
                if g == 4:
                    group(g, KD, lambda k, w: w[:, k, :], lambda j, k, w: h[:, k, j * P:(j + 1) * P])
                else:
                    group(g, KD, lambda k: h[:, k, :])

            freed(pe, 8)
            pe.wait_ge(S("cv"), CT)
            for i in range(CT):
                last = mm(PS[:, 0, :], ones, A[:, 40 + i, :], start=i == 0, stop=i == CT - 1)
            last.then_inc(S("cl_mm"), 1)
            ada(11, 1)
            for i in range(CT):
                pe.wait_ge(S("cl_sq"), i + 1)
                last = mm(PS[:, 2, :], ones, A[:, 4 + i, :], start=i == 0, stop=i == CT - 1)
            last.then_inc(S("cl_mm"), 1)
            pe.wait_ge(S("g_rows"), 1)
            for t in range(NT):
                last = nc.tensor.transpose(PS[:, 3, 4 * t:4 * t + 4], gr[5][:, t * P:(t + 1) * P], ident[0:4, 0:4])
            last.then_inc(S("gT_mm"), 1)

            pe.wait_ge(S("qk"), 8)
            freed(pe, 9)
            pe.wait_ge(S("mod_ev"), 12)
            pe.wait_ge(S("gT_ev"), 1)
            pe.wait_ge(S("cl_ev"), 1)
            pe.wait_ge(S("em"), 1)
            for hd in range(MH):
                if hd:
                    pe.wait_ge(S("ml_h"), hd)
                for s in range(NT):
                    mm(PS[:, s, 0:T - s * P], A[:, 48 + hd, s * P:(s + 1) * P], A[:, 44 + hd, s * P:T], start=True, stop=True)
                sel = ident[0:4, hd:hd + 1].broadcast_to([4, P])
                mm(PS[:, 4, :], sel, gr[6], start=True, stop=True)
                mm(PS[:, 5, :], sel, gr[7], start=True, stop=True).then_inc(S("ml_s"), 1)
                for s in range(NT):
                    pe.wait_ge(S("ml_p"), NT * hd + s + 1)
                    mm(PS[:, 6, s * P:T], A[:, 16 + s, hd * P:(hd + 1) * P], A[:, 52 + s, s * P:T], start=s == 0,
                       stop=s == NT - 1)
                    last = mm(PS[:, 7, s * P:T], ones, A[:, 52 + s, s * P:T], start=s == 0, stop=s == NT - 1)
                last.then_inc(S("ml_n"), 1)
            pe.wait_ge(S("ml_h"), MH)
            for hd in range(MH):
                mm(PS[:, hd, :], ones, A[:, 8 + hd, :], start=True, stop=True).then_inc(S("ml_mu"), 1)
            for hd in range(MH):
                pe.wait_ge(S("ml_sq"), hd + 1)
                mm(PS[:, 4 + hd, :], ones, A[:, 12 + hd, :], start=True, stop=True).then_inc(S("ml_var"), 1)
            pe.wait_ge(S("ya_in"), CT)
            pe.wait_ge(S("ml_std"), MH)
            for m in range(2):
                group(G_CONV + m, CT, lambda k: A[:, 40 + k, :], k0=0 if m == 0 else 4)
            pe.wait_ge(S("hm"), MH)
            for m in range(2):
                group(G_MOUT + m, CT, lambda k: A[:, 8 + k, :], k0=0 if m == 0 else 4)
            for m in range(2):
                pe.wait_ge(S("merged"), KD)
                group(G_WOUT + m, KD, lambda k: A[:, 24 + k, :])
            norm(1, 4 * (G_WOUT % 2))
            wait_h(1)
            freed(pe, 15)
            for t in range(NT):
                for k in range(KD):
                    last = mm(PS[:, 0, 64 * t:64 * t + NG + E], h[:, k, t * P:(t + 1) * P], wrt[:, k, :], start=k == 0, stop=k == KD - 1)
            last.then_inc(S("logits"), 1)
            for t in range(NT):
                if t >= 2:
                    pe.wait_ge(S("ht_ev"), t - 1)
                for k in range(KD):
                    last = nc.tensor.transpose(PS[:, 2 + 2 * (t % 2) + k // 4, (k % 4) * P:(k % 4 + 1) * P], h[:, k, t * P:(t + 1) * P], ident)
                last.then_inc(S("ht_mm"), 1)
            pe.wait_ge(S("asg"), 1)
            for t in range(NT):
                for u in range(t + 1):
                    mm(PS[:, 6, t * E:(t + 1) * E], C("tri_strict") if u == t else ones, asg[2][:, u, :], start=u == 0, stop=u == t)
            for u in range(NT):
                last = mm(PS[:, 7, 0:E], ones, asg[2][:, u, :], start=u == 0, stop=u == NT - 1)
            last.then_inc(S("rank"), 1)
            n = pairs(pe)
            pe.wait_ge(S("ht_ev"), NT)
            with pe.Fori(0, n) as i:
                for j in range(2):
                    pe.wait_ge(S(f"xg{j}"), 16 * i + 16)
                    for k in range(KD):
                        last = nc.tensor.transpose(PS[:, k // 4, (k % 4) * P:(k % 4 + 1) * P], xg[j][:, k // 4, (k % 4) * P:(k % 4 + 1) * P], ident)
                    last.then_inc(S("m_tr"), 1)
                    pe.wait_ge(S("m_xT"), 2 * i + j + 1)
                    for part in range(2):
                        pe.wait_ge(S(f"w{j}{part}"), 16 * i + 16)
                        for k in range(KD):
                            last = mm(PS[:, 2 + 2 * j + part, :], xgT[j][:, k // 4, (k % 4) * P:(k % 4 + 1) * P], moe_w[j][part][:, k, :],
                                      start=k == 0, stop=k == KD - 1)
                    last.then_inc(S("m_gu"), 1)
                for j in range(2):
                    pe.wait_ge(S("m_h"), 2 * i + j + 1)
                    for k in range(4):
                        last = nc.tensor.transpose(PS[:, 0, k * P:(k + 1) * P], hid[j][:, k * P:(k + 1) * P], ident)
                    last.then_inc(S("m_ht"), 1)
                    pe.wait_ge(S("m_hT"), 2 * i + j + 1)
                    pe.wait_ge(S(f"w{j}2"), 16 * i + 16)
                    pe.wait_ge(S("m_y"), 2 * i + j + 1)
                    for m in range(2):
                        for k in range(4):
                            last = mm(PS[:, 6 + m, :], hidT[j][:, k * P:(k + 1) * P], moe_w[j][2][:, 4 * m + k, :], start=k == 0, stop=k == 3)
                    last.then_inc(S("m_dn"), 1)
            for t in range(NT):
                pe.wait_ge(S("y_sum"), t + 1)
            for k in range(KD):
                for t in range(NT):
                    last = nc.tensor.transpose(PS[:, k, t * P:(t + 1) * P], A[:, 16 + 2 * t + k // 4, (k % 4) * P:(k % 4 + 1) * P], ident)
                last.then_inc(S("yT"), 1)
            norm(2, 0)

            norm(3, 0)
            wait_h(2)
            pe.wait_ge(S("small3"), 32)
            for t in range(NT):
                for k in range(KD):
                    last = mm(PS[:, 4, 16 * t:16 * t + 16], h[:, k, t * P:(t + 1) * P], wab[:, k, :], start=k == 0, stop=k == KD - 1)
            last.then_inc(S("ab_mm"), 1)
            for g in range(8):
                if g == 1:
                    pe.wait_ge(S("ab_ev"), 1)
                group(G_AIN + g, KD, lambda k: h[:, k, :])
            freed(pe, G_AIN + 6)
            freed(pe, G_AIN + 7)
            for m in range(16):
                pe.wait_ge(S("l_sq"), m + 1)
                if m >= 8:
                    pe.wait_ge(S("l_r"), m - 7)
                mm(PS[:, m % 8, :], ones, sq[:, m % 2, :], start=True, stop=True).then_inc(S("l_mm"), 1)
            pe.wait_ge(S("l_r"), 16)
            for t in range(NT):
                for which in range(2):
                    if which == 0:
                        pe.wait_ge(S("a_silu"), 24)
                        if t >= 2:
                            pe.wait_ge(S("vt"), t - 1)
                    else:
                        pe.wait_ge(S("l_n"), 16)
                        if t >= 2:
                            pe.wait_ge(S("kt"), t - 1)
                    b = 4 * (t % 2) + 2 * which
                    for hd in range(DH):
                        last = nc.tensor.transpose(PS[:, b + hd // 4, (hd % 4) * P:(hd % 4 + 1) * P], A[:, (8 if which else 40) + hd, t * P:(t + 1) * P], ident)
                    last.then_inc(S("vk_mm"), 1)
            pe.wait_ge(S("g"), 1)
            pe.wait_ge(S("vt"), NT)
            for c in range(NT):
                last = mm(PS[:, 0, 8 * c:8 * c + 8], C("tri_incl"), dl[1][:, c, :], start=True, stop=True)
            last.then_inc(S("gc_mm"), 1)
            pe.wait_ge(S("kt"), NT)
            pe.wait_ge(S("gc"), 1)

            def heads(bank, lhs, rhs, sets=(0, 1)):
                for hd in range(4 * sets[0], 4 * sets[-1] + 4):
                    last = mm(PS[:, bank + hd // 4, (hd % 4) * P:(hd % 4 + 1) * P], lhs(hd), rhs(hd), start=True, stop=True)
                return last

            def hv(u):
                return lambda hd: A[:, u + hd // 4, (hd % 4) * P:(hd % 4 + 1) * P]

            def identity(hd):
                return ident

            for c in range(NT):
                cols = slice(c * P, (c + 1) * P)

                def qT(hd):
                    return A[:, hd, cols]

                def kT(hd):
                    return A[:, 8 + hd, cols]

                if c:
                    pe.wait_ge(S("d_S"), 2 * c)
                    pe.wait_ge(S("d_o"), 2 * c)
                heads(0, lambda hd: dl[1][:, c, hd:hd + 1].broadcast_to([P, P]), lambda hd: C("tri_incl")).then_inc(S("d_mm"), 1)
                heads(6, lambda hd: dl[0][:, c, hd:hd + 1].broadcast_to([P, P]), identity)
                heads(2, kT, kT).then_inc(S("d_mm"), 1)
                heads(4, kT, qT).then_inc(S("d_mm"), 1)
                pe.wait_ge(S("d_pre"), c + 1)
                for l in range(LEVELS):
                    n = LEVELS * c + l
                    for s in range(2):
                        pe.wait_ge(S(f"d_nl{s}"), n + 1)
                        if l:
                            pe.wait_ge(S(f"d_X{s}"), n)
                        heads(0, hv(48), identity if l == 0 else hv(52), (s,)).then_inc(S(f"d_p{s}"), 1)
                    if l:
                        for s in range(2):
                            pe.wait_ge(S(f"d_p1{s}"), c * (LEVELS - 1) + l)
                            if l < LEVELS - 1:
                                heads(2, hv(50), hv(54), (s,))
                            heads(4, hv(54), hv(50), (s,)).then_inc(S(f"d_dx{s}"), 1)
                if c:
                    for s in range(2):
                        heads(0, kT, hv(56), (s,)).then_inc(S("d_ks"), 1)
                for s in range(2):
                    pe.wait_ge(S(f"d_X{s}"), LEVELS * (c + 1))
                    if c:
                        pe.wait_ge(S("d_R"), 2 * (c - 1) + s + 1)
                    heads(2, hv(50), hv(54) if c else hv(24), (s,)).then_inc(S("d_vn"), 1)
                for s in range(2):
                    pe.wait_ge(S("d_vs"), 2 * c + s + 1)
                    for hd in range(4 * s, 4 * s + 4):
                        o = PS[:, 4 + s, (hd % 4) * P:(hd % 4 + 1) * P]
                        if c:
                            mm(o, hv(56)(hd), qT(hd), start=True, stop=False)
                        last = mm(o, hv(40)(hd), hv(44)(hd), start=not c, stop=True)
                    last.then_inc(S("d_om"), 1)
                    heads(6, hv(32 + 2 * c), hv(40), (s,)).then_inc(S("d_sm"), 1)
            pe.wait_ge(S("d_o"), 2 * NT)
            pe.wait_ge(S("d_S"), 2 * NT)
            for hd in range(DH):
                pe.wait_ge(S("o_sq"), hd + 1)
                mm(PS[:, hd, :], ones, sq[:, hd % 2, :], start=True, stop=True).then_inc(S("o_mm"), 1)
            pe.wait_ge(S("o"), DH)
            for m in range(2):
                group(G_AOUT + m, KD, lambda k: h[:, k, :])

            def ffn(layer, g_up, g_dn):
                u0 = UIDX[f"up{layer}_0"]

                def up(j, unit_count, free_count):
                    pe.wait_ge(S(f"unit{(u0 + j) % 2}"), unit_count)
                    pe.wait_ge(S("ev_dve"), free_count)
                    for t in range(4):
                        for k in range(KD):
                            last = mm(PS[:, 4 * ((g_up + j) % 2) + t, :], ring[:, (u0 + j) % 2, k, t * P:(t + 1) * P], h[:, k, :], start=k == 0, stop=k == KD - 1)
                        last.then_inc(S("mm"), 1)

                for j in range(2):
                    group(g_up + j, KD, lambda k: h[:, k, :])
                with pe.Fori(0, (FU - 3) // 2) as i:
                    for j in range(2):
                        up(j, 16 * i + 16 * ((u0 + 2 + j) // 2 + 1), 8 * i + EMPTIED[g_up + j][1])
                group(g_up + FU - 1, KD, lambda k: h[:, k, :])
                for m in range(2):
                    g = g_dn + m
                    freed(pe, g - 2)
                    for ui in range(3):
                        name = f"down{layer}_{3 * m + ui}"
                        unit_here(pe, name)
                        nk = 8 if ui < 2 else FT - 16
                        if m == 0:
                            pe.wait_ge(S("f_hid"), FT * layer + 8 * ui + nk)
                        for j in range(4):
                            for k in range(nk):
                                last = mm(PS[:, 4 * (g % 2) + j, :], ring[:, unit_slot(name), k, j * P:(j + 1) * P], A[:, 8 * ui + k, :],
                                          start=ui == 0 and k == 0, stop=ui == 2 and k == nk - 1)
                            if ui == 2 or j == 3:
                                last.then_inc(S("mm"), 1)

            norm(4, NORM_BANK[4])
            wait_h(3)
            ffn(0, G_UP0, G_DN0)

            norm(5, NORM_BANK[5])
            wait_h(4)
            g = G_KV
            unit_here(pe, "kv")
            freed(pe, g - 2)
            w = ring[:, unit_slot("kv")]
            for j in range(2):
                for k in range(KD):
                    last = mm(PS[:, 4 * (g % 2) + j, :], w[:, k, j * P:(j + 1) * P], h[:, k, :], start=k == 0, stop=k == KD - 1)
                last.then_inc(S("mm"), 1)
            for j in range(2):
                for t in range(2 * j, 2 * j + 2):
                    for k in range(KD):
                        last = mm(PS[:, 4 * (g % 2) + 2 + j, 256 * (t % 2):256 * (t % 2) + 256], h[:, k, t * P:(t + 1) * P], w[:, k, 256:512],
                                  start=k == 0, stop=k == KD - 1)
                last.then_inc(S("mm"), 1)
            pe.wait_ge(S("hb"), KD)
            for m in range(2):
                group(G_WQ + m, KD, lambda k: A[:, 40 + k, :])

            def scores(n):
                b, m = n // 2, n % 2
                if n >= 2:
                    pe.wait_ge(S("at_o"), n - 1)
                k0 = max(b - 1, 0) * P
                for hh in range(8):
                    base = 64 * (hh // 4)
                    last = mm(PS[:, 4 * m + hh // 2, (hh % 2) * 256 + (0 if b else P):(hh % 2) * 256 + 256],
                              A[base:base + HD, 4 * m + hh % 4, b * P:(b + 1) * P], A[base:base + HD, 8 + m, k0:(b + 1) * P], start=True, stop=True)
                last.then_inc(S("at_s"), 1)

            freed(pe, G_WQ)
            freed(pe, G_WQ + 1)
            scores(0)
            scores(1)
            for n in range(2 * NT):
                b, m = n // 2, n % 2
                pe.wait_ge(S("at_pn"), n + 1)
                for hh in range(8):
                    for kk in range(0 if b else 1, 2):
                        i = 2 * hh + kk
                        last = nc.tensor.transpose(PS[:, 4 * m + i // 4, (i % 4) * P:(i % 4 + 1) * P], A[:, 20 + 4 * m + i // 4, (i % 4) * P:(i % 4 + 1) * P], ident)
                last.then_inc(S("at_t"), 1)
                pe.wait_ge(S("at_pt"), n + 1)
                for hh in range(8):
                    kv = 2 * m + hh // 4
                    for kk in range(0 if b else 1, 2):
                        i, t = 2 * hh + kk, b - 1 + kk
                        last = mm(PS[64 * (hh % 2):64 * (hh % 2) + HD, 4 * m, (hh // 2) * P:(hh // 2 + 1) * P],
                                  A[:, 10 + t // 2, 256 * (t % 2) + kv * HD:256 * (t % 2) + (kv + 1) * HD],
                                  A[:, 28 + 4 * m + i // 4, (i % 4) * P:(i % 4 + 1) * P], start=kk == 0 or not b, stop=kk == 1)
                last.then_inc(S("at_pv"), 1)
                if n + 2 < 2 * NT:
                    scores(n + 2)
            pe.wait_ge(S("at_o"), 2 * NT)
            for m in range(2):
                group(G_WO + m, KD, lambda k: h[:, k, :])
            norm(6, NORM_BANK[6])
            wait_h(5)
            ffn(1, G_UP1, G_DN1)
            norm(7, NORM_BANK[7])

        @block.scalar
        def _(act):
            a_ = nc.scalar.activation
            chain = [0]

            def link(ins):
                chain[0] += 1
                ins.then_inc(S("act"), 1)
                act.wait_ge(S("act"), chain[0])

            def inv_sqrt(dst, src, e, scale):
                link(a_(dst, src, ACT.Ln, bias=eps[:, e:e + 1], scale=scale))
                return a_(dst, dst, ACT.Exp, scale=-0.5)

            def norm(n):
                for k in range(KD):
                    if n == 0:
                        act.wait_ge(S("x_in"), 16)
                    else:
                        act.wait_ge(S("xt"), KD * (n - 1) + k + 1)
                    if KD * n + k >= 2:
                        act.wait_ge(S("sq_used"), KD * n + k - 1)
                    a_(sq[:, k % 2, :], x[:, k, :], ACT.Square).then_inc(S("sq"), 1)
                act.wait_ge(S("sq_used"), KD * (n + 1))
                bank = NORM_BANK[n]
                inv_sqrt(rstd[:], PS[:, bank, :], 0, 1.0 / D).then_inc(S("std"), 1)

            act.wait_ge(S("small"), 80)
            a_(silc[:], V("c", 0, KD), ACT.Silu).then_inc(S("silc"), 1)
            act.wait_ge(S("eps"), 4)
            norm(0)
            for k in range(KD):
                act.wait_ge(S("h_pre"), k + 1)
                a_(h[:, k, :], h[:, k, :], ACT.Identity, bias=mod[:, k:k + 1]).then_inc(S("h"), 1)
            act.wait_ge(S("if_ev"), 2)
            a_(gr[2], gr[1], ACT.Abs).then_inc(S("ga"), 1)
            act.wait_ge(S("ga"), 1)
            a_(gr[2], gr[2], ACT.Exp, scale=-1.0).then_inc(S("ga"), 1)
            act.wait_ge(S("ga"), 2)
            a_(gr[2], gr[2], ACT.Ln, bias=eps[0:4, 2:3]).then_inc(S("ga"), 1)

            for g in range(10):
                for j in range(4):
                    act.wait_ge(S("mm"), TILE_DONE[g][j])
                    a_(A[:, 4 * g + j, :], PS[:, 4 * (g % 2) + j, :], ACT.Copy if g in (0, 2, 3, 4) else ACT.Sigmoid).then_inc(S("ev_act"), 1)
                if g == 0:
                    act.wait_ge(S("g_rows"), 2)
                    a_(gr[7], gr[7], ACT.Exp).then_inc(S("em"), 1)
            for m in range(8):
                act.wait_ge(S("qk_cv"), m + 1)
                a_(A[:, 44 + m, :], A[:, 44 + m, :], ACT.Silu).then_inc(S("qk"), 1)
            for i in range(CT):
                act.wait_ge(S("cl_d"), i + 1)
                a_(A[:, 4 + i, :], A[:, 40 + i, :], ACT.Square).then_inc(S("cl_sq"), 1)
            act.wait_ge(S("cl_mm"), 2)
            inv_sqrt(rstd[:], PS[:, 2, :], 1, 1.0 / DC).then_inc(S("cl_ev"), 1)
            for i in range(CT):
                act.wait_ge(S("cl_n"), i + 1)
                a_(A[:, 40 + i, :], A[:, 40 + i, :], ACT.Silu, bias=V("conv_ln_b", i)).then_inc(S("ya_in"), 1)
            act.wait_ge(S("gT_ev"), 1)
            for hd in range(MH):
                act.wait_ge(S("ml_m"), 2 * hd + 2)
                if hd:
                    act.wait_ge(S("ml_n"), hd)
                for s in range(NT):
                    bias = gT[:, s, hd:hd + 1]
                    w = a_(A[:, 52 + s, s * P:(s + 1) * P], A[:, 1, s * P:(s + 1) * P], ACT.Exp, bias=bias)
                    w.then_inc(S("ml_w"), 1)
                    if s < NT - 1:
                        a_(A[:, 52 + s, (s + 1) * P:T], A[:, 0, (s + 1) * P:T], ACT.Exp, bias=bias).then_inc(S("ml_w"), 1)
                act.wait_ge(S("ml_n"), hd + 1)
                a_(A[:, 2, :], PS[:, 7, :], ACT.Abs).then_inc(S("ml_ad"), 1)
            for hd in range(MH):
                act.wait_ge(S("ml_d"), hd + 1)
                a_(A[:, 12 + hd, :], A[:, 8 + hd, :], ACT.Square).then_inc(S("ml_sq"), 1)
            for hd in range(MH):
                act.wait_ge(S("ml_var"), hd + 1)
                inv_sqrt(A[:, 4 + hd, :], PS[:, 4 + hd, :], 1, 1.0 / P).then_inc(S("ml_std"), 1)
            norm(1)
            for k in range(KD):
                act.wait_ge(S("h_pre"), KD + k + 1)
                a_(h[:, k, :], h[:, k, :], ACT.Identity, bias=mod[:, 24 + k:25 + k]).then_inc(S("h"), 1)

            for t in range(NT):
                act.wait_ge(S("ht_mm"), t + 1)
                a_(A[:, 2 * t:2 * t + 2, :], PS[:, 2 + 2 * (t % 2):4 + 2 * (t % 2), :], ACT.Copy).then_inc(S("ht_ev"), 1)
            act.wait_ge(S("rg"), 1)
            a_(r4[0], r4[0], ACT.Exp).then_inc(S("rexp"), 1)
            act.wait_ge(S("rg"), 2)
            a_(rs[8], rs[8], ACT.Exp).then_inc(S("rexp"), 1)
            n = pairs(act)
            with act.Fori(0, n) as i:
                for j in range(2):
                    act.wait_ge(S("m_tr"), 2 * i + j + 1)
                    a_(xgT[j], PS[:, 0:2, :], ACT.Copy).then_inc(S("m_xT"), 1)
                    act.wait_ge(S("m_gu"), 2 * i + j + 1)
                    a_(hid[j], PS[:, 2 + 2 * j, :], ACT.Silu).then_inc(S("m_sg"), 1)
                for j in range(2):
                    act.wait_ge(S("m_dn"), 2 * i + j + 1)
                    rwait(act, S(f"sc{j}"), 16 * i + 16 * NT)
                    a_(yb[j], PS[:, 6:8, :], ACT.Copy).then_inc(S("m_y"), 1)
            norm(2)

            norm(3)
            act.wait_ge(S("ab_ev"), 1)
            a_(dl[0][:], ab[:, :, 0:DH], ACT.Sigmoid).then_inc(S("ab_a"), 1)
            link(a_(dl[1][:], ab[:, :, DH:2 * DH], ACT.Abs))
            link(a_(dl[1][:], dl[1][:], ACT.Exp, scale=-1.0))
            a_(dl[1][:], dl[1][:], ACT.Ln, bias=eps[:, 2:3]).then_inc(S("ab_a"), 1)
            a_(glast[:], R("a_gate")[:, DH:2 * DH], ACT.Exp).then_inc(S("ab_a"), 1)
            for m in range(24):
                act.wait_ge(S("ev_dve"), EMPTIED[G_AIN][1] - 4 + m + 1)
                u = A[:, m if m < 16 else 24 + m, :]
                a_(u, u, ACT.Silu).then_inc(S("a_silu"), 1)
            for g in (6, 7):
                for j in range(4):
                    act.wait_ge(S("mm"), TILE_DONE[G_AIN + g][j])
                    a_(A[:, 16 + 4 * (g - 6) + j, :], PS[:, 4 * ((G_AIN + g) % 2) + j, :], ACT.Silu).then_inc(S("ev_act"), 1)
            act.wait_ge(S("a_silu"), 24)
            for m in range(17):
                if m < 16:
                    if m >= 2:
                        act.wait_ge(S("l_mm"), m - 1)
                    a_(sq[:, m % 2, :], A[:, m, :], ACT.Square).then_inc(S("l_sq"), 1)
                if m >= 1:
                    act.wait_ge(S("l_mm"), m)
                    if m >= 3:
                        act.wait_ge(S("l_n"), m - 2)
                    inv_sqrt(A[:, 48 + (m - 1) % 2, :], PS[:, (m - 1) % 8, :], 0, 1.0).then_inc(S("l_r"), 1)
            for t in range(NT):
                act.wait_ge(S("vk_mm"), 2 * t + 2)
                b = 4 * (t % 2) + 2
                a_(A[:, 32 + 2 * t:34 + 2 * t, :], PS[:, b:b + 2, :], ACT.Copy).then_inc(S("kt"), 1)
            act.wait_ge(S("gc"), 1)
            a_(dl[3][:], dl[2][:], ACT.Exp).then_inc(S("eg"), 1)
            for c in range(NT):
                act.wait_ge(S("d_mm"), 3 * c + 1)
                a_(A[:, 48:50, :], PS[:, 0:2, :], ACT.Exp).then_inc(S("d_eg"), 1)
                act.wait_ge(S("d_arg"), c + 1)
                a_(A[:, 42:44, :], A[:, 42:44, :], ACT.Exp).then_inc(S("d_et"), 1)
                for l in range(1, LEVELS):
                    for s in range(2):
                        act.wait_ge(S(f"d_p{s}"), LEVELS * c + l + 1)
                        a_(A[:, 54 + s, :], PS[:, s, :], ACT.Copy).then_inc(S(f"d_p1{s}"), 1)
                for s in range(2):
                    act.wait_ge(S("d_vn"), 2 * c + s + 1)
                    a_(A[:, 40 + s, :], PS[:, 2 + s, :], ACT.Copy).then_inc(S("d_vs"), 1)
                for s in range(2):
                    act.wait_ge(S("d_om"), 2 * c + s + 1)
                    a_(h[:, 4 * s:4 * s + 4, c * P:(c + 1) * P], PS[:, 4 + s, :].rearrange("p (a b) -> p a b", b=P), ACT.Copy).then_inc(S("d_o"), 1)
            act.wait_ge(S("d_o"), 2 * NT)
            for hd in range(DH + 1):
                if hd < DH:
                    if hd >= 2:
                        act.wait_ge(S("o_mm"), hd - 1)
                    a_(sq[:, hd % 2, :], h[:, hd, :], ACT.Square).then_inc(S("o_sq"), 1)
                if hd >= 1:
                    act.wait_ge(S("o_mm"), hd)
                    inv_sqrt(A[:, 40 + hd - 1, :], PS[:, hd - 1, :], 0, 1.0 / P).then_inc(S("o_r"), 1)

            def ffn(layer, g_up):
                ev0 = EMPTIED[g_up][1] - 4

                def unit(u, par):
                    for j in range(2):
                        act.wait_ge(S("ev_dve"), 4 * u + ev0 + j + 1)
                        t = A[:, 22 + 4 * par + j, :]
                        a_(t, t, ACT.Silu).then_inc(S("f_act"), 1)

                with act.Fori(0, FU // 2) as i:
                    for j in range(2):
                        unit(2 * i + j, j)
                unit(FU - 1, 0)

            norm(4)
            ffn(0, G_UP0)
            norm(5)

            def exps(n):
                b, m = n // 2, n % 2
                act.wait_ge(S("at_m"), 2 * n + 2)
                link(a_(sm[2][:, m, :], sm[2][:, m, :], ACT.Exp))
                for hh in range(8):
                    p = A[:, 20 + 4 * m + hh // 2, (hh % 2) * 256 + (0 if b else P):(hh % 2) * 256 + 256]
                    last = a_(p, p, ACT.Exp, bias=sm[0][:, m, hh:hh + 1], accum_out=sm[1][:, m, hh:hh + 1])
                last.then_inc(S("at_p"), 1)

            exps(0)
            exps(1)
            for n in range(2 * NT):
                b, m = n // 2, n % 2
                act.wait_ge(S("at_t"), n + 1)
                if n >= 2:
                    act.wait_ge(S("at_pv"), n - 1)
                src, dst = PS[:, 4 * m:4 * m + 4, :], A[:, 28 + 4 * m:32 + 4 * m, :]
                if not b:
                    src, dst = (v.rearrange("p a (b c d) -> p (a b) c d", c=2, d=P)[:, :, 1, :] for v in (src, dst))
                a_(dst, src, ACT.Copy).then_inc(S("at_pt"), 1)
                if n + 2 < 2 * NT:
                    exps(n + 2)
            norm(6)
            ffn(1, G_UP1)
            norm(7)

        @block.vector
        def _(dve):
            chain = [0]
            ts, tt, stt, cp = nc.vector.tensor_scalar, nc.vector.tensor_tensor, nc.vector.scalar_tensor_tensor, nc.vector.tensor_copy

            def link(ins):
                chain[0] += 1
                ins.then_inc(S("dve"), 1)
                dve.wait_ge(S("dve"), chain[0])

            for i, e in enumerate((1e-6, 1e-5, 1.0, 0.0)):
                nc.vector.memset(eps[:, i:i + 1], e).then_inc(S("eps"), 1)
            dve.wait_ge(S("x_in"), 16)
            dve.wait_ge(S("silc"), 1)

            def ada_acc(a):
                unit_here(dve, f"ada{a}")
                if a >= 2:
                    dve.wait_ge(S("ada_sum"), a - 1)
                w = ring[:, unit_slot(f"ada{a}")]
                acc = A[:, 52 + a % 2, :]
                link(ts(acc, w[:, 0, :], silc[:, 0:1], None, ALU.mult))
                for k in range(1, KD):
                    ins = stt(acc, w[:, k, :], silc[:, k:k + 1], acc, ALU.mult, ALU.add)
                    if k < KD - 1:
                        link(ins)
                ins.then_inc(S("ada_used"), 1)

            def mod_ev(a, bank):
                dve.wait_ge(S("ada_sum"), a + 1)
                tt(mod[:, 4 * a:4 * a + 4], PS[:, bank, 0:4], V("b_ada", 4 * a, 4), ALU.add).then_inc(S("mod_ev"), 1)

            def gain(layer, gname, sc):
                link(ts(gm[:, layer, :], mod[:, sc:sc + KD], 1.0, None, ALU.add))
                link(tt(gm[:, layer, :], gm[:, layer, :], V(gname, 0, KD), ALU.mult))

            def norm(n, g, dst, done):
                dve.wait_ge(S("std"), n + 1)
                for k in range(KD):
                    stt(dst[:, k, :], x[:, k, :], g[:, k:k + 1], rstd[:], ALU.mult, ALU.mult).then_inc(S(done), 1)

            for a in range(4):
                ada_acc(a)
            for a in range(4):
                mod_ev(a, 1 + a)
            dve.wait_ge(S("mod_ev"), 4)
            gain(0, "g_norm1", 8)
            norm(0, gm[:, 0, :], h, "h_pre")
            dve.wait_ge(S("if_mm"), 1)
            ts(gr[0], PS[0:4, 4, :], bif[0:4], None, ALU.add).then_inc(S("if_ev"), 1)
            ts(gr[1], PS[32:36, 4, :], bif[32:36], None, ALU.add).then_inc(S("if_ev"), 1)
            dve.wait_ge(S("if_ev"), 2)
            link(nc.vector.memset(gr[4], 1.0))
            link(ts(gr[6], gr[1], 0.0, None, ALU.min))
            dve.wait_ge(S("ga"), 3)
            link(tt(gr[2], gr[6], gr[2], ALU.subtract))
            link(nc.vector.tensor_tensor_scan(gr[3], gr[4], gr[2], 0.0, ALU.mult, ALU.add))
            tt(gr[5], gr[0], gr[3], ALU.subtract).then_inc(S("g_rows"), 1)
            dve.wait_ge(S("g_rows"), 1)
            link(nc.vector.tensor_tensor_scan(gr[6], gr[5], gr[5], 0.0, ALU.max, ALU.max))
            link(ts(gr[6], gr[6], -1.0, None, ALU.mult))
            tt(gr[7], gr[6], gr[3], ALU.subtract).then_inc(S("g_rows"), 1)

            for i in range(CT):
                dve.wait_ge(S("ev_act"), 4 + i + 1)
                link(tt(A[:, i, :], A[:, i, :], A[:, 4 + i, :], ALU.mult))

            def conv(dst, src, taps, w, b):
                if b is None:
                    link(ts(dst, src, w(taps - 1), None, ALU.mult))
                else:
                    link(ts(dst, src, w(taps - 1), b, ALU.mult, ALU.add))
                for j in range(taps - 2, -1, -1):
                    s = taps - 1 - j
                    ins = stt(dst[:, s:T], src[:, 0:T - s], w(j), dst[:, s:T], ALU.mult, ALU.add)
                    if j:
                        link(ins)
                return ins

            def conv_u(i):
                conv(A[:, 40 + i, :], A[:, i, :], TAPS, lambda j: V("conv_dw_w", CT * j + i), V("conv_dw_b", i)).then_inc(S("cv"), 1)

            def conv_qk(m):
                dve.wait_ge(S("ev_act"), 8 + m + 1)
                conv(A[:, 44 + m, :], A[:, 8 + m, :], QTAPS, lambda j: V("qk_conv_w", 8 * j + m), V("qk_conv_b", m)).then_inc(S("qk_cv"), 1)

            for i in range(CT):
                ada_acc(4 + i)
                conv_u(i)
                mod_ev(4 + i, 4 * ((3 + i) % 2) + 3)
            ada_acc(8)
            for m in range(4):
                conv_qk(m)
            mod_ev(8, 4 * (7 % 2) + 3)
            ada_acc(9)
            for m in range(4, 8):
                conv_qk(m)
            mod_ev(9, 4 * (8 % 2) + 3)
            ada_acc(10)
            mod_ev(10, 4 * (9 % 2) + 3)
            ada_acc(11)
            dve.wait_ge(S("cl_mm"), 1)
            dve.wait_ge(S("cv"), CT)
            for i in range(CT):
                stt(A[:, 40 + i, :], PS[:, 0, :], -1.0 / DC, A[:, 40 + i, :], ALU.mult, ALU.add).then_inc(S("cl_d"), 1)
            mod_ev(11, 1)
            dve.wait_ge(S("mod_ev"), 12)
            gain(1, "g_norm2", 32)
            dve.wait_ge(S("cl_ev"), 1)
            dve.wait_ge(S("cl_d"), CT)
            for i in range(CT):
                stt(A[:, 40 + i, :], A[:, 40 + i, :], V("conv_ln_g", i), rstd[:], ALU.mult, ALU.mult).then_inc(S("cl_n"), 1)
            dve.wait_ge(S("gT_mm"), 1)
            cp(gT[:], PS[:, 3, 0:16].rearrange("p (a b) -> p a b", b=MH)).then_inc(S("gT_ev"), 1)
            for hd in range(MH):
                dve.wait_ge(S("ml_s"), hd + 1)
                cp(A[:, 0, :], PS[:, 4, :]).then_inc(S("ml_m"), 1)
                tt(A[:, 1, :].rearrange("p (a b) -> p a b", b=P), PS[:, 4, :].rearrange("p (a b) -> p a b", b=P),
                   C("after").rearrange("p (a b) -> p a b", a=1).broadcast_to([P, NT, P]), ALU.add).then_inc(S("ml_m"), 1)
                for s in range(NT):
                    dve.wait_ge(S("ml_w"), 7 * hd + min(2 * s + 2, 7))
                    stt(A[:, 52 + s, s * P:T], PS[:, s, 0:T - s * P], float(P) ** -0.5, A[:, 52 + s, s * P:T], ALU.mult, ALU.mult).then_inc(S("ml_p"), 1)
                dve.wait_ge(S("ml_ad"), hd + 1)
                link(tt(A[:, 2, :], A[:, 2, :], PS[:, 5, :], ALU.max))
                link(nc.vector.reciprocal(A[:, 3, :], A[:, 2, :]))
                tt(A[:, 8 + hd, :], PS[:, 6, :], A[:, 3, :], ALU.mult).then_inc(S("ml_h"), 1)
            dve.wait_ge(S("ml_h"), MH)
            for hd in range(MH):
                dve.wait_ge(S("ml_mu"), hd + 1)
                stt(A[:, 8 + hd, :], PS[:, hd, :], -1.0 / P, A[:, 8 + hd, :], ALU.mult, ALU.add).then_inc(S("ml_d"), 1)
            for hd in range(MH):
                dve.wait_ge(S("ml_std"), hd + 1)
                link(stt(A[:, 8 + hd, :], A[:, 8 + hd, :], V("m_norm_g", hd), A[:, 4 + hd, :], ALU.mult, ALU.mult))
                tt(A[:, 8 + hd, :], A[:, 8 + hd, :], A[:, 20 + hd, :], ALU.mult).then_inc(S("hm"), 1)
            for m in range(2):
                for j in range(4):
                    dve.wait_ge(S("mm"), TILE_DONE[G_CONV + m][j])
                    b = 4 * ((G_CONV + m) % 2) + j
                    tt(A[:, 24 + 4 * m + j, :], A[:, 24 + 4 * m + j, :], PS[:, b, :], ALU.mult).then_inc(S("ev_dve"), 1)
            for m in range(2):
                for j in range(4):
                    dve.wait_ge(S("mm"), TILE_DONE[G_MOUT + m][j])
                    b = 4 * ((G_MOUT + m) % 2) + j
                    tt(A[:, 32 + 4 * m + j, :], A[:, 32 + 4 * m + j, :], PS[:, b, :], ALU.mult).then_inc(S("ev_dve"), 1)
                    dve.wait_ge(S("ev_dve"), 8 + 4 * m + j + 1)
                    tt(A[:, 24 + 4 * m + j, :], A[:, 24 + 4 * m + j, :], A[:, 32 + 4 * m + j, :], ALU.add).then_inc(S("merged"), 1)

            def residual(g, n_of, scale_of=None, bias_of=None):
                for j in range(4):
                    k = 4 * n_of + j
                    dve.wait_ge(S("mm"), TILE_DONE[g][j])
                    src = PS[:, 4 * (g % 2) + j, :]
                    if scale_of is not None:
                        ins = stt(x[:, k, :], src, scale_of(k), x[:, k, :], ALU.mult, ALU.add)
                    elif bias_of is not None:
                        ins = stt(x[:, k, :], src, bias_of(k), x[:, k, :], ALU.add, ALU.add)
                    else:
                        ins = tt(x[:, k, :], src, x[:, k, :], ALU.add)
                    ins.then_inc(S("xt"), 1)

            for m in range(2):
                residual(G_WOUT + m, m, scale_of=lambda k: mod[:, 16 + k:17 + k])
            norm(1, gm[:, 1, :], h, "h_pre")
            X3 = [P, NT, EPG]

            def b3(v, w):
                return v.rearrange("p (a b) -> p a b", b=1).broadcast_to([P, NT, w])

            def bnum(name, w):
                return C(name).rearrange("p (a b) -> p a b", a=1).broadcast_to([P, NT, w])

            def first_of(dst, vals, mx, num, w, t1):
                link(nc.vector.tensor_reduce(mx, vals, AX, ALU.max))
                link(tt(t1, vals, b3(mx, w), ALU.is_lt))
                link(stt(t1, t1, 1000.0, bnum(num, w), ALU.mult, ALU.add))
                link(nc.vector.tensor_reduce(rs[13], t1, AX, ALU.min))
                link(tt(dst, bnum(num, w), b3(rs[13], w), ALU.is_equal))

            dve.wait_ge(S("logits"), 1)
            link(tt(lg, PS[:, 0, 0:256].rearrange("p (a b) -> p a b", b=64)[:, :, 0:NG + E],
                    R("b_router").rearrange("p (a b) -> p a b", a=1).broadcast_to([P, NT, NG + E]), ALU.add))
            first_of(r4[1], lg[:, :, 0:NG], rs[0], "iota4", NG, r4[2])
            tt(r4[0], lg[:, :, 0:NG], b3(rs[0], NG), ALU.subtract).then_inc(S("rg"), 1)
            dve.wait_ge(S("rexp"), 1)
            link(nc.vector.tensor_reduce(rs[1], r4[0], AX, ALU.add))
            link(nc.vector.reciprocal(rs[2], rs[1]))
            for g in range(NG):
                le = lg[:, :, NG + g * EPG:NG + (g + 1) * EPG]
                og = r4[1][:, :, g:g + 1].broadcast_to(X3)
                if g == 0:
                    link(tt(r8[0], le, og, ALU.mult))
                else:
                    link(tt(r8[1], le, og, ALU.mult))
                    link(tt(r8[0], r8[0], r8[1], ALU.add))
            first_of(r8[2], r8[0], rs[3], "iota8", EPG, r8[1])
            link(stt(r8[3], r8[2], NEG, r8[0], ALU.mult, ALU.add))
            first_of(r8[4], r8[3], rs[4], "iota8", EPG, r8[1])
            tt(rs[8], rs[4], rs[3], ALU.subtract).then_inc(S("rg"), 1)
            dve.wait_ge(S("rexp"), 2)
            link(ts(rs[5], rs[8], 1.0, None, ALU.add))
            link(nc.vector.reciprocal(rs[6], rs[5]))
            link(tt(wtok[:, 0, :], rs[6], rs[2], ALU.mult))
            link(tt(wtok[:, 1, :], wtok[:, 0, :], rs[8], ALU.mult))
            for c in range(2):
                for g in range(NG):
                    link(tt(asg[c][:, :, g * EPG:(g + 1) * EPG], r8[2 + 2 * c], r4[1][:, :, g:g + 1].broadcast_to(X3), ALU.mult))
            tt(asg[2], asg[0], asg[1], ALU.add).then_inc(S("asg"), 1)
            dve.wait_ge(S("rank"), 1)
            link(cp(er[0], PS[:, 7, 0:E]))
            link(ts(er[1], er[0], 0.0, None, ALU.is_gt))
            for m in range(1, NT):
                link(ts(er[2], er[0], float(m * P), None, ALU.is_gt))
                link(tt(er[1], er[1], er[2], ALU.add))
            link(nc.vector.memset(er[3], 1.0))
            link(nc.vector.tensor_tensor_scan(er[4], er[3], er[1], 0.0, ALU.mult, ALU.add))
            link(tt(er[5], er[4], er[1], ALU.subtract))
            link(ts(er[5], er[5], float(P), None, ALU.mult))
            link(tt(asg[3], PS[:, 6, 0:NT * E].rearrange("p (a b) -> p a b", b=E), er[5].rearrange("p (a b) -> p a b", a=1).broadcast_to([P, NT, E]), ALU.add))
            for c in range(2):
                link(tt(asg[4], asg[3], asg[c], ALU.mult))
                link(nc.vector.tensor_reduce(rs[9 + c], asg[4], AX, ALU.add))
                cp(posi[:, c, :], rs[9 + c]).then_inc(S("posi"), 1)
            pend = er[4][0:1, :].rearrange("p (a b) -> p a b", a=1).broadcast_to([1, NB, E])
            link(tt(blk[0:1], pend, C("iotab")[0:1, :].rearrange("p (a b) -> p a b", b=1).broadcast_to([1, NB, E]), ALU.is_le))
            link(nc.vector.tensor_reduce(blkf[0:1, 0:NB], blk[0:1], AX, ALU.add))
            link(ts(blkf[0:1, 0:NB], blkf[0:1, 0:NB], float(E - 1), None, ALU.min))
            link(ts(blkf[0:1, NB:NB + 1], er[4][0:1, E - 1:E], 0.5, 0.25, ALU.mult, ALU.add))
            link(cp(blki[0:1, 0:NB], blkf[0:1, 0:NB]))
            cp(blki[0:1, NB:NB + 1], blkf[0:1, NB:NB + 1]).then_inc(S("blocks"), 1)
            nc.vector.memset(rs[12], 0.0).then_inc(S("m_y"), 1)
            n = pairs(dve)
            with dve.Fori(0, n) as i:
                for j in range(2):
                    dve.wait_ge(S("m_sg"), 2 * i + j + 1)
                    tt(hid[j], hid[j], PS[:, 3 + 2 * j, :], ALU.mult).then_inc(S("m_h"), 1)
                for j in range(2):
                    dve.wait_ge(S("m_ht"), 2 * i + j + 1)
                    cp(hidT[j], PS[:, 0, :]).then_inc(S("m_hT"), 1)
            dve.wait_ge(S("y2"), 16 * NT)
            for t in range(NT):
                y2 = A[:, 4 * t:4 * t + 4, :].rearrange("p a b -> p (a b)")
                yy = A[:, 16 + 2 * t:18 + 2 * t, :].rearrange("p a b -> p (a b)")
                link(ts(yy, y2[:, D:2 * D], wtok[:, 1, t:t + 1], None, ALU.mult))
                stt(yy, y2[:, 0:D], wtok[:, 0, t:t + 1], yy, ALU.mult, ALU.add).then_inc(S("y_sum"), 1)
            for k in range(KD):
                dve.wait_ge(S("yT"), k + 1)
                stt(x[:, k, :], PS[:, k, :], mod[:, 40 + k:41 + k], x[:, k, :], ALU.mult, ALU.add).then_inc(S("xt"), 1)
            norm(2, V("g_final", 0, KD), x, "xt")

            norm(3, V("a_norm", 0, KD), h, "h")
            dve.wait_ge(S("ab_mm"), 1)
            pab = PS[:, 4, 0:64].rearrange("p (a b) -> p a b", b=16)
            link(cp(ab[:, :, 0:DH], pab[:, :, 0:DH]))
            tt(ab[:, :, DH:2 * DH], pab[:, :, DH:2 * DH], R("a_gate")[:, 0:DH].rearrange("p (a b) -> p a b", a=1).broadcast_to([P, NT, DH]),
               ALU.add).then_inc(S("ab_ev"), 1)
            dve.wait_ge(S("ab_ev"), 1)
            link(ts(dl[5][:], ab[:, :, DH:2 * DH], 0.0, None, ALU.max))
            dve.wait_ge(S("ab_a"), 3)
            link(tt(dl[1][:], dl[1][:], dl[5][:], ALU.add))
            stt(dl[1][:], dl[1][:], -1.0, glast[:].rearrange("p (a b) -> p a b", a=1).broadcast_to([P, NT, DH]), ALU.mult, ALU.mult).then_inc(S("g"), 1)
            for m in range(24):
                g = G_AIN + m // 4
                dve.wait_ge(S("mm"), TILE_DONE[g][m % 4])
                dst = A[:, m if m < 16 else 24 + m, :]
                src = PS[:, 4 * (g % 2) + m % 4, :]
                conv(dst, src, 4, lambda j: V("a_conv_w", 24 * j + m), None).then_inc(S("ev_dve"), 1)
            for m in range(16):
                dve.wait_ge(S("l_r"), m + 1)
                r = A[:, 48 + m % 2, :]
                if m < 8:
                    stt(A[:, m, :], A[:, m, :], float(P) ** -0.5, r, ALU.mult, ALU.mult).then_inc(S("l_n"), 1)
                else:
                    tt(A[:, m, :], A[:, m, :], r, ALU.mult).then_inc(S("l_n"), 1)

            def per_head(v, n=DH):
                return v.rearrange("p (a b) -> p a b", b=1).broadcast_to([P, n, P])

            def h3(v):
                return v.rearrange("p a (b c) -> p (a b) c", c=P)

            def m4(v):
                return v.rearrange("p (a b) -> p a b", b=P)

            for t in range(NT):
                dve.wait_ge(S("vk_mm"), 2 * t + 1)
                b = 4 * (t % 2)
                v_t = A[:, 24 + 2 * t:26 + 2 * t, :].rearrange("p a (b c) -> p (a b) c", c=P)
                tt(v_t, h3(PS[:, b:b + 2, :]), per_head(dl[0][:, t, :]), ALU.mult).then_inc(S("vt"), 1)
            dve.wait_ge(S("gc_mm"), 1)
            cp(dl[2][:], PS[:, 0, 0:32].rearrange("p (a b) -> p a b", b=DH)).then_inc(S("gc"), 1)
            dve.wait_ge(S("eg"), 1)
            link(stt(dl[4][:], dl[0][:], -1.0, dl[3][:], ALU.mult, ALU.mult))
            identb = ident.rearrange("p (a b) -> p a b", a=1).broadcast_to([P, 4, P])
            for c in range(NT):
                cols = slice(c * P, (c + 1) * P)
                dve.wait_ge(S("d_eg"), c + 1)
                for hd in range(DH):
                    part = slice((hd % 4) * P, (hd % 4 + 1) * P)
                    last = stt(A[:, 42 + hd // 4, part], PS[:, hd // 4, part], dl[2][:, c, hd:hd + 1], C("after"), ALU.subtract, ALU.add)
                last.then_inc(S("d_arg"), 1)
                link(cp(glast[:], h3(A[:, 48:50, :])[:, :, P - 1]))
                dve.wait_ge(S("d_mm"), 3 * c + 3)
                link(tt(A[:, 0:8, cols], A[:, 0:8, cols], h3(A[:, 48:50, :]), ALU.mult))
                dve.wait_ge(S("d_et"), c + 1)
                link(tt(A[:, 44:46, :], PS[:, 4:6, :], A[:, 42:44, :], ALU.mult))
                link(tt(A[:, 46:48, :], PS[:, 2:4, :], A[:, 42:44, :], ALU.mult))
                link(tt(A[:, 46:48, :], A[:, 46:48, :], PS[:, 6:8, :], ALU.mult))
                kd = h3(A[:, 32 + 2 * c:34 + 2 * c, :])
                tt(kd, kd, h3(A[:, 42:44, :])[:, :, P - 1:P].broadcast_to([P, DH, P]), ALU.mult).then_inc(S("d_pre"), 1)

                def nl(l, s):
                    tt(m4(A[:, 48 + s, :]), m4(A[:, 46 + s, :]), levels[:, l:l + 1, :].broadcast_to([P, 4, P]), ALU.mult).then_inc(S(f"d_nl{s}"), 1)

                for s in range(2):
                    nl(0, s)
                for l in range(LEVELS):
                    n = LEVELS * c + l
                    if l == 0:
                        for s in range(2):
                            dve.wait_ge(S(f"d_nl{s}"), n + 1)
                            link(tt(m4(A[:, 50 + s, :]), m4(A[:, 48 + s, :]), identb, ALU.add))
                            dve.wait_ge(S(f"d_p{s}"), n + 1)
                            tt(m4(A[:, 52 + s, :]), m4(PS[:, s, :]), identb, ALU.add).then_inc(S(f"d_X{s}"), 1)
                            nl(1, s)
                        continue
                    if l + 1 < LEVELS:
                        for s in range(2):
                            dve.wait_ge(S(f"d_p{s}"), n + 1)
                            nl(l + 1, s)
                    for s in range(2):
                        dve.wait_ge(S(f"d_dx{s}"), c * (LEVELS - 1) + l)
                        if l < LEVELS - 1:
                            link(tt(A[:, 52 + s, :], A[:, 52 + s, :], PS[:, 2 + s, :], ALU.add))
                        tt(A[:, 50 + s, :], A[:, 50 + s, :], PS[:, 4 + s, :], ALU.add).then_inc(S(f"d_X{s}"), 1)
                if c:
                    for s in range(2):
                        dve.wait_ge(S("d_ks"), 2 * (c - 1) + s + 1)
                        link(tt(m4(A[:, 54 + s, :]), m4(PS[:, s, :]), per_head(dl[4][:, c, 4 * s:4 * s + 4], 4), ALU.mult))
                        tt(A[:, 54 + s, :], A[:, 54 + s, :], A[:, 24 + 2 * c + s, :], ALU.add).then_inc(S("d_R"), 1)
                for s in range(2):
                    dve.wait_ge(S("d_sm"), 2 * c + s + 1)
                    if c:
                        link(tt(m4(A[:, 56 + s, :]), m4(A[:, 56 + s, :]), per_head(glast[:, 4 * s:4 * s + 4], 4), ALU.mult))
                        tt(A[:, 56 + s, :], A[:, 56 + s, :], PS[:, 6 + s, :], ALU.add).then_inc(S("d_S"), 1)
                    else:
                        cp(A[:, 56 + s, :], PS[:, 6 + s, :]).then_inc(S("d_S"), 1)
            for hd in range(DH):
                dve.wait_ge(S("o_r"), hd + 1)
                link(stt(h[:, hd, :], h[:, hd, :], V("a_onorm"), A[:, 40 + hd, :], ALU.mult, ALU.mult))
                tt(h[:, hd, :], h[:, hd, :], A[:, 16 + hd, :], ALU.mult).then_inc(S("o"), 1)
            for m in range(2):
                residual(G_AOUT + m, m)

            def ffn(layer, g_up, g_dn):
                ev0 = EMPTIED[g_up][1] - 4
                mm0 = TILE_DONE[g_up][0]
                LINKS = 8

                def unit(u, par):
                    done = [0]

                    def flink(ins):
                        done[0] += 1
                        ins.then_inc(S("dve_f"), 1)
                        dve.wait_ge(S("dve_f"), LINKS * u + (LINKS * FU * layer + done[0]))

                    for j in range(4):
                        dve.wait_ge(S("mm"), 4 * u + (mm0 + j))
                        t = A[:, 22 + 4 * par + j, :]
                        src = PS[:, 4 * ((g_up + par) % 2) + j, :]
                        tile = (j % 2) + (FT if j >= 2 else 0)

                        def col(name, base):
                            return vec[:, bass.ds(2 * u + (VOFF[name] + base + tile), 1)]

                        flink(ts(t, src, col("f_conv_w", (3 * layer + 2) * 2 * FT), col("f_conv_b", 2 * FT * layer), ALU.mult, ALU.add))
                        flink(stt(t[:, 1:T], src[:, 0:T - 1], col("f_conv_w", (3 * layer + 1) * 2 * FT), t[:, 1:T], ALU.mult, ALU.add))
                        stt(t[:, 2:T], src[:, 0:T - 2], col("f_conv_w", 3 * layer * 2 * FT), t[:, 2:T], ALU.mult, ALU.add).then_inc(S("ev_dve"), 1)
                    assert done[0] == LINKS
                    dve.wait_ge(S("ev_dve"), 4 * u + (ev0 + 4))
                    for j in range(2):
                        dve.wait_ge(S("f_act"), 2 * u + (FT * layer + j + 1))
                        tt(A[:, bass.ds(2 * u + j, 1), :].rearrange("p a b -> p (a b)"), A[:, 22 + 4 * par + j, :], A[:, 24 + 4 * par + j, :],
                           ALU.mult).then_inc(S("f_hid"), 1)

                with dve.Fori(0, FU // 2) as i:
                    for j in range(2):
                        unit(2 * i + j, j)
                unit(FU - 1, 0)
                for m in range(2):
                    residual(g_dn + m, m)

            norm(4, V("f_norm", 0, KD), h, "h")
            ffn(0, G_UP0, G_DN0)

            norm(5, V("kv_norm", 0, KD), h, "h")
            for k in range(KD):
                stt(A[:, 40 + k, :], x[:, k, :], V("b_norm", k), rstd[:], ALU.mult, ALU.mult).then_inc(S("hb"), 1)
            for j in range(4):
                dve.wait_ge(S("mm"), TILE_DONE[G_KV][j])
                src = PS[:, 4 * (G_KV % 2) + j, :]
                if j < 2:
                    ts(A[:, 8 + j, :], src, V("kv_b", j), None, ALU.add).then_inc(S("ev_dve"), 1)
                else:
                    tt(A[:, 8 + j, :].rearrange("p (a b) -> p a b", b=256), src.rearrange("p (a b) -> p a b", b=256),
                       R("kv_b_v").rearrange("p (a b) -> p a b", a=1).broadcast_to([P, 2, 256]), ALU.add).then_inc(S("ev_dve"), 1)
            for m in range(2):
                for j in range(4):
                    dve.wait_ge(S("mm"), TILE_DONE[G_WQ + m][j])
                    ts(A[:, 4 * m + j, :], PS[:, 4 * ((G_WQ + m) % 2) + j, :], V("b_b_q", 4 * m + j), float(HD) ** -0.5, ALU.add, ALU.mult).then_inc(S("ev_dve"), 1)

            def ph(m, b):
                v = A[:, 20 + 4 * m:24 + 4 * m, :].rearrange("p a (b c) -> p (a b) c", c=256)
                return v if b else v[:, :, P:256]

            def maxima(n):
                b, m = n // 2, n % 2
                dve.wait_ge(S("at_s"), n + 1)
                if n >= 2:
                    dve.wait_ge(S("at_t"), n - 1)
                src = PS[:, 4 * m:4 * m + 4, :].rearrange("p a (b c) -> p (a b) c", c=256)
                bias = A[:, 12 + 4 * m:16 + 4 * m, :].rearrange("p a (b c) -> p (a b) c", c=256)
                if not b:
                    src, bias = src[:, :, P:256], bias[:, :, P:256]
                link(tt(ph(m, b), src, bias, ALU.add))
                link(nc.vector.tensor_reduce(sm[3][:, m, :], ph(m, b), AX, ALU.max))
                sink = R("sinks")[:, 8 * m:8 * m + 8]
                link(tt(sm[3][:, m, :], sm[3][:, m, :], sink, ALU.max))
                ts(sm[0][:, m, :], sm[3][:, m, :], -1.0, None, ALU.mult).then_inc(S("at_m"), 1)
                tt(sm[2][:, m, :], sink, sm[3][:, m, :], ALU.subtract).then_inc(S("at_m"), 1)

            dve.wait_ge(S("bias"), 16)
            maxima(0)
            maxima(1)
            for n in range(2 * NT):
                b, m = n // 2, n % 2
                dve.wait_ge(S("at_p"), n + 1)
                link(tt(sm[1][:, m, :], sm[1][:, m, :], sm[2][:, m, :], ALU.add))
                link(nc.vector.reciprocal(sm[1][:, m, :], sm[1][:, m, :]))
                tt(ph(m, b), ph(m, b), sm[1][:, m, :].rearrange("p (a b) -> p a b", b=1).broadcast_to([P, 8, 256 if b else P]), ALU.mult).then_inc(S("at_pn"), 1)
                dve.wait_ge(S("at_pv"), n + 1)
                cp(h[:, 4 * m:4 * m + 4, b * P:(b + 1) * P], m4(PS[:, 4 * m, :])).then_inc(S("at_o"), 1)
                if n + 2 < 2 * NT:
                    maxima(n + 2)
            for m in range(2):
                residual(G_WO + m, m, bias_of=lambda k: V("b_b_o", k))
            norm(6, V("f_norm", KD, KD), h, "h")
            ffn(1, G_UP1, G_DN1)
            norm(7, V("final_norm", 0, KD), h, "h")

        @block.gpsimd
        def _(pool):
            pool.wait_ge(S("slots0"), 16)
            pool.wait_ge(S("small2"), 48)
            pool.wait_ge(S("posi"), 2)
            for t in range(NT):
                for c in range(2):
                    pool.indirect_dma_start(slots, bass.IndirectOffsetOnAxis(ap=posi[:, c, t:t + 1], axis=0),
                                            tok[:, 2 * t + c, :], None).then_inc(S(f"sc{c}"), 16)
            n = pairs(pool)
            for c in range(2):
                pool.wait_ge(S(f"sc{c}"), 16 * NT)
            pool.wait_ge(S("f_tok"), 16 * NT)

            def gather(b, j):
                pool.dma_start(idx[:, j, :], slots[bass.ds(b * P, P), :]).then_inc(S(f"idx{j}"), 16)

            def gather2(j, count):
                rwait(pool, S(f"idx{j}"), count)
                pool.indirect_dma_start(xg[j].rearrange("p a b -> p (a b)"), None, f_tok,
                                        bass.IndirectOffsetOnAxis(ap=idx[:, j, 0:1], axis=0)).then_inc(S(f"xg{j}"), 16)

            for j in range(2):
                gather(j, j)
            for j in range(2):
                gather2(j, 16)
            with pool.Fori(0, n) as i:
                for j in range(2):
                    rwait(pool, S(f"sc{j}"), 16 * i + 16 * NT)
                    rwait(pool, S(f"idx{j}"), 16 * i + 16)
                    nc.gpsimd.tensor_copy(sidx[:, j, :], idx[:, j, :]).then_inc(S("sidx"), 1)
                    rwait(pool, S("sidx"), 2 * i + j + 1)
                    rwait(pool, S(f"xg{j}"), 16 * i + 16)
                    gather(2 * i + 2 + j, j)
                    rwait(pool, S("m_tr"), 2 * i + j + 1)
                    gather2(j, 16 * i + 32)
                for j in range(2):
                    rwait(pool, S("m_y"), 2 * i + j + 2)
                    pool.indirect_dma_start(y_asg, bass.IndirectOffsetOnAxis(ap=sidx[:, j, 1:2], axis=0),
                                            yb[j].rearrange("p a b -> p (a b)"), None, bounds_check=2 * T - 1,
                                            oob_is_err=False).then_inc(S(f"sc{j}"), 16)
            for j in range(2):
                rwait(pool, S(f"xg{j}"), 16 * n + 16)
                rwait(pool, S(f"idx{j}"), 16 * n + 16)


NORM_BANK = [0, 0, 0, 0, 0, 4, 0, 4]


def slab(w, k0, nk, c0, nc_=512):
    return w[k0 * P:(k0 + nk) * P, c0:c0 + nc_].reshape(nk, P, nc_).transpose(1, 0, 2)


def feat(v):
    return np.ascontiguousarray(v.reshape(-1, P).T)


def pack(I):
    g = {k: np.asarray(v) for k, v in I.items()}
    w_in, ada = g["w_in"][0], g["w_ada"][0]
    wall = np.zeros((NU, P, 8, 512), np.float32)

    def put(name, *slabs):
        o = 0
        for s in slabs:
            wall[UIDX[name], :, o:o + s.shape[1]] = s
            o += s.shape[1]

    for a in range(12):
        put(f"ada{a}", slab(ada, 0, 8, 512 * a))
    for i in range(10):
        put(f"in{i}", slab(w_in, 0, 8, 512 * i if i < 6 else 512 * i + 2 * MH))
    for n in ("conv_out", "m_out"):
        w = g["w_" + n][0]
        put(n, slab(w, 0, 4, 0), slab(w, 0, 4, 512))
    for m in range(2):
        put(f"w_out{m}", slab(g["w_out"][0], 0, 8, 512 * m))
        put(f"a_out{m}", slab(g["a_w_out_2"][0], 0, 8, 512 * m))
        put(f"w_o{m}", slab(g["b_w_o_2"][0], 0, 8, 512 * m))
        wq = g["b_w_q_2"][0].reshape(D, 2, 2, 4, HD)[:, m].transpose(0, 2, 1, 3).reshape(D, 512)
        put(f"w_q{m}", slab(wq, 0, 8, 0))
    for i in range(8):
        put(f"a_in{i}", slab(g["a_w_in_2"][0], 0, 8, 512 * i))
    put("kv", slab(g["kv_w_2"], 0, 8, 0))
    for l in range(2):
        up, dn = g["f_w_up_2"][l], g["f_w_down_2"][l]
        for i in range(FU):
            u = np.concatenate([slab(up, 0, 8, 256 * i, 256), slab(up, 0, 8, FF + 256 * i, 256)], 2)
            put(f"up{l}_{i}", u)
        for m in range(2):
            for i in range(3):
                put(f"down{l}_{3 * m + i}", slab(dn, 8 * i, 8 if i < 2 else FT - 16, 512 * m))
    we = np.empty((E, 3, P, 8, 512), np.float32)
    we[:, 0] = g["w_e_gate"][0].reshape(E, 8, P, 512).transpose(0, 2, 1, 3)
    we[:, 1] = g["w_e_up"][0].reshape(E, 8, P, 512).transpose(0, 2, 1, 3)
    we[:, 2] = g["w_e_down"][0].reshape(E, 4, P, 2, 512).transpose(0, 2, 3, 1, 4).reshape(E, P, 8, 512)
    wif = np.zeros((P, KD, 64), np.float32)
    wi = w_in[:, 3072:3072 + 2 * MH].reshape(KD, P, 2 * MH).transpose(1, 0, 2)
    wif[:, :, 0:4], wif[:, :, 32:36] = wi[:, :, 0:4], wi[:, :, 4:8]
    wr = np.concatenate([g["w_rg"][0], g["w_re"][0]], 1).reshape(KD, P, NG + E).transpose(1, 0, 2)
    wab = g["a_w_in_2"][0][:, 4096:].reshape(KD, P, 2 * DH).transpose(1, 0, 2)
    bq = g["b_b_q_2"][0].reshape(2, 2, 4, HD).transpose(0, 2, 1, 3)
    src = dict(c=g["c"], b_ada=g["b_ada"], g_norm1=g["g_norm1"], conv_dw_w=g["conv_dw_w"], conv_dw_b=g["conv_dw_b"],
               conv_ln_g=g["conv_ln_g"], conv_ln_b=g["conv_ln_b"], qk_conv_w=g["qk_conv_w"], qk_conv_b=g["qk_conv_b"],
               m_norm_g=g["m_norm_g"], g_norm2=g["g_norm2"], g_final=g["g_final"], a_norm=g["a_norm_2"],
               a_conv_w=g["a_conv_w_2"], a_onorm=g["a_onorm_2"], kv_norm=g["kv_norm_2"], kv_b=g["kv_b_2"][:256],
               b_norm=g["b_norm_2"], b_b_q=bq, b_b_o=g["b_b_o_2"], f_norm=g["f_norm_2"], f_conv_w=g["f_conv_w_2"],
               f_conv_b=g["f_conv_b_2"], final_norm=g["final_norm_2"])
    vecs = np.concatenate([feat(np.ascontiguousarray(src[n])) for n, _ in VECS], 1)
    assert vecs.shape == (P, NVEC)
    rows = np.concatenate([g["b_rg"][0], g["b_re"][0], g["a_dt_bias_2"][0], g["a_A_log_2"][0], g["kv_b_2"][256:], g["b_sinks_2"][0]])
    p, f = np.arange(P)[:, None], np.arange(P)[None, :]
    lev = []
    for l in range(LEVELS):
        lev.append(-(((f >> l) == (p >> l) + 1) & ((f >> l) % 2 == 1)).astype(np.float32))
    zero = np.zeros((P, 1), np.float32)
    cst = np.concatenate([np.eye(P), np.ones((P, P)), np.where(f < p, NEG, 0.0), (p < f) * 1.0, (p <= f) * 1.0,
                          zero + np.arange(NG), zero + np.arange(EPG), zero + np.arange(NB)], 1).astype(np.float32)
    t = np.arange(P)[:, None, None] + P * np.arange(NT)[None, :, None] + 0 * np.arange(2)[None, None, :]
    tokens = np.stack([t, 2 * t + np.arange(2)], -1).reshape(P, -1)
    none = np.tile(np.array([0, 2 * T], np.int64), (P, NB + 2))
    ints = np.concatenate([tokens, none], 1).astype(np.int32)
    dist = p + P - np.arange(2 * P)[None, :]
    slopes = 2.0 ** (-8.0 * np.arange(1, AH + 1, dtype=np.float32) / AH)
    ok = (dist >= 0) & (dist < P)
    att = np.where(ok[:, None, :], -slopes[None, :, None] * dist[:, None, :], NEG).astype(np.float32)
    xt = np.ascontiguousarray(g["x"][0].T.reshape(KD, P, T).transpose(1, 0, 2))
    return dict(xt_in=xt, wall=wall, wexp=we, w_if=wif, w_router=np.ascontiguousarray(wr), w_ab=np.ascontiguousarray(wab),
                vecs=vecs, rows=rows, b_if=np.ascontiguousarray(g["b_if"].reshape(8, 1)), cst_in=cst, ints=ints, att_bias=att,
                levels_in=np.concatenate(lev, 1))


def kernel(**inputs):
    import concourse.bacc as bacc
    from concourse.bass_utils import run_bass_kernel_spmd

    arrays = {name: np.ascontiguousarray(v) for name, v in pack(inputs).items()}
    nc = bacc.Bacc("TRN2", target_bir_lowering=False, num_devices=1)
    handles = {name: nc.dram_tensor(name, list(v.shape), mybir.dt.from_np(v.dtype), kind="ExternalInput").ap() for name, v in arrays.items()}
    out_t = nc.dram_tensor("out_t", [P, KD, T], F32, kind="ExternalOutput").ap()
    build(nc, out_t=out_t, **handles)
    result = run_bass_kernel_spmd(nc, [arrays], core_ids=[0])
    return np.ascontiguousarray(result.results[0]["out_t"].transpose(1, 0, 2).reshape(D, T).T[None])
```

```python
from contextlib import ExitStack

import numpy as np

import concourse.bass as bass
from concourse import mybir

ALU = mybir.AluOpType
ACT = mybir.ActivationFunctionType
AX = mybir.AxisListType.X
F32 = mybir.dt.float32
F32R = mybir.dt.float32r
I32 = mybir.dt.int32

P = 128
D = 1024
T = 512
KD = D // P
NT = T // P
NEG = -1.0e30

DC = 512
CT = DC // P
TAPS = 31
QTAPS = 4
MH = 4
E = 32
NG = 4
EPG = 8
NB = 2 * T // P + E
DH = 8
LEVELS = 7
AH = 16
HD = 64
KVH = 4
FF = 2816
FT = FF // P
FU = 11

VECS = [("c", 8), ("b_ada", 48), ("g_norm1", 8), ("conv_dw_w", TAPS * 4), ("conv_dw_b", 4), ("conv_ln_g", 4),
        ("conv_ln_b", 4), ("qk_conv_w", 32), ("qk_conv_b", 8), ("m_norm_g", 4), ("g_norm2", 8), ("g_final", 8),
        ("a_norm", 8), ("a_conv_w", 96), ("a_onorm", 1), ("kv_norm", 8), ("kv_b", 2), ("b_norm", 8), ("b_b_q", 8),
        ("b_b_o", 8), ("f_norm", 16), ("f_conv_w", 2 * 3 * 44), ("f_conv_b", 2 * 44), ("final_norm", 8)]
VOFF, NVEC = {}, 0
for _n, _w in VECS:
    VOFF[_n] = NVEC
    NVEC += _w
ROWS = [("b_router", NG + E), ("a_gate", 2 * DH), ("kv_b_v", 256), ("sinks", AH)]
ROFF, NROW = {}, 0
for _n, _w in ROWS:
    ROFF[_n] = NROW
    NROW += _w
CONSTS = [("ident", P), ("ones", P), ("after", P), ("tri_strict", P), ("tri_incl", P),
          ("iota4", NG), ("iota8", EPG), ("iotab", NB)]
COFF, NCST = {}, 0
for _n, _w in CONSTS:
    COFF[_n] = NCST
    NCST += _w

UNITS1 = [f"in{i}" for i in range(10)] + ["conv_out", "m_out", "w_out0", "w_out1"]
UNITS2 = ([f"a_in{i}" for i in range(8)] + ["a_out0", "a_out1"] + [f"up0_{i}" for i in range(FU)]
          + [f"down0_{i}" for i in range(6)] + ["kv", "w_q0", "w_q1", "w_o0", "w_o1"]
          + [f"up1_{i}" for i in range(FU)] + [f"down1_{i}" for i in range(6)])
UNITS = UNITS1 + UNITS2
NU1, NU = len(UNITS1), len(UNITS)
UIDX = {n: i for i, n in enumerate(UNITS)}

GROUPS = ([([f"in{i}"], "A") for i in range(10)] + [(["conv_out"], "D")] * 2 + [(["m_out"], "D")] * 2
          + [(["w_out0"], "X"), (["w_out1"], "X")]
          + [([f"a_in{i}"], "D" if i < 6 else "A") for i in range(8)] + [(["a_out0"], "X"), (["a_out1"], "X")]
          + [([f"up0_{i}"], "D") for i in range(FU)] + [([f"down0_{3 * m + i}" for i in range(3)], "X") for m in range(2)]
          + [(["kv"], "D"), (["w_q0"], "D"), (["w_q1"], "D"), (["w_o0"], "X"), (["w_o1"], "X")]
          + [([f"up1_{i}"], "D") for i in range(FU)] + [([f"down1_{3 * m + i}" for i in range(3)], "X") for m in range(2)])
G_CONV, G_MOUT, G_WOUT, G_AIN, G_AOUT, G_UP0, G_DN0, G_KV, G_WQ, G_WO, G_UP1, G_DN1 = 10, 12, 14, 16, 24, 26, 37, 39, 40, 42, 44, 55
TILE_DONE, UNIT_USED, EMPTIED = [], {}, []
_mm, _ev = 0, {"A": 0, "D": 0, "X": 0}
for _us, _e in GROUPS:
    if _us[0] == "a_out0":
        _ev["X"] += 2 * KD
    for _u in _us[:-1]:
        _mm += 4
        UNIT_USED[_u] = _mm
    TILE_DONE.append([_mm + j + 1 for j in range(4)])
    _mm += 4
    UNIT_USED[_us[-1]] = _mm
    _ev[_e] += 4
    EMPTIED.append((_e, _ev[_e]))



def tile_done(u, j):
    if UNITS[u] == "kv" and j == 2:
        j = 3
    return UNIT_USED[UNITS[NU1 - 1]] + 4 * (u - NU1) + j + 1


def split_count(u, j):
    return 4 * (u - NU1) + j + 1


def build(nc, xt_in, wada, wall, wexp, w_if, w_router, w_ab, vecs, rows, b_if, cst_in, ints, att_bias, levels_in, out_t):
    f_tok = nc.dram_tensor("h2_tokens", [T, D], F32, kind="Internal").ap()
    y_asg = nc.dram_tensor("y_assignments", [2 * T, D], F32, kind="Internal").ap()
    slots = nc.dram_tensor("slot_table", [(NB + 2) * P, 2], I32, kind="Internal").ap()

    ctx = ExitStack()
    with ctx:
        def sb(name, shape, dt=F32):
            return ctx.enter_context(nc.sbuf_tensor(name, shape, dt))

        sems = {}

        def S(name):
            if name not in sems:
                sems[name] = ctx.enter_context(nc.semaphore(name))
            return sems[name]

        PS = ctx.enter_context(nc.psum_tensor("PS", [P, 8, 512], F32))
        with ExitStack() as views:
            def view(name, *dims):
                return views.enter_context(nc.sbuf_tensor(name, [P, *dims], F32R))

            h_r = view("h_r", KD, T)
            ring_r = view("ring_r", 2, 8, 512)
            hid_r = view("hid_r", FT, 512)
            hb_hi_r = view("hb_hi_r", 8, 512)
            w_hi_r = view("w_hi_r", 8, 512)
            h_hi_r = view("h_hi_r", 8, 512)
            top_r = view("top_r", 13, 512)
        h = sb("h", [P, KD, T])
        ring = sb("ring", [P, 2, 8, 512])
        A = sb("A", [P, 59, 512])
        x = sb("x", [P, KD, T])
        sq = sb("sq", [P, 2, T])
        rstd = sb("rstd", [P, T])
        vec = sb("vec", [P, NVEC])
        row = sb("row", [P, NROW])
        cst = sb("cst", [P, NCST])
        eps = sb("eps", [P, 4])
        mod = sb("mod", [P, 48])
        gm = sb("gm", [P, 2, KD])
        silc = sb("silc", [P, KD])

        def V(name, i=0, n=1):
            return vec[:, VOFF[name] + i:VOFF[name] + i + n]

        def C(name):
            w = dict(CONSTS)[name]
            return cst[:, COFF[name]:COFF[name] + w]

        def R(name):
            w = dict(ROWS)[name]
            return row[:, ROFF[name]:ROFF[name] + w]

        ident, ones = C("ident"), C("ones")

        wif = sb("wif", [P, KD, 64])
        bif = sb("bif", [64, 1])
        gr = [A[0:4, u, :] for u in (44, 45, 46, 47, 48, 56, 57, 58)]
        gT = sb("gT", [P, NT, MH])
        wrt = sb("wrt", [P, KD, NG + E])
        tok = sb("tok", [P, 8, 2], I32)
        idx = sb("idx", [P, 2, 2], I32)
        sidx = sb("sidx", [P, 2, 2], I32)
        wtok = sb("wtok", [P, 2, NT])
        blki = sb("blki", [1, NB + 2], I32)

        used_r = [0]

        def carve(*dims):
            n = int(np.prod(dims))
            v = A[:, 48:59, :].rearrange("p a b -> p (a b)")[:, used_r[0]:used_r[0] + n]
            used_r[0] += n
            if len(dims) == 2:
                return v.rearrange("p (a b) -> p a b", b=dims[1])
            if len(dims) == 3:
                return v.rearrange("p (a b c) -> p a b c", b=dims[1], c=dims[2])
            return v

        lg = carve(NT, NG + E)
        rs = [carve(NT) for _ in range(14)]
        r4 = [carve(NT, NG) for _ in range(3)]
        r8 = [carve(NT, EPG) for _ in range(5)]
        asg = [carve(NT, E) for _ in range(5)]
        er = [carve(E) for _ in range(6)]
        blk = carve(NB, E)
        blkf = carve(NB + 2)
        assert used_r[0] <= 11 * 512
        posi = sb("posi", [P, 2, NT], I32)
        wab = sb("wab", [P, KD, 2 * DH])
        levels = sb("levels", [P, LEVELS, P])
        ab = sb("ab", [P, NT, 2 * DH])
        dl = [sb(f"dl{i}", [P, NT, DH]) for i in range(6)]
        glast = sb("glast", [P, DH])
        sm = [sb(f"sm{i}", [P, 2, 8]) for i in range(4)]

        moe_w = [[ring[:, 0], ring[:, 1], A[:, 0:8]], [A[:, 8:16], A[:, 16:24], A[:, 24:32]]]
        xg = [A[:, 32 + 2 * j:34 + 2 * j, :] for j in range(2)]
        xgT = [A[:, 36 + 2 * j:38 + 2 * j, :] for j in range(2)]
        hid = [A[:, 40 + j, :] for j in range(2)]
        hidT = [A[:, 42 + j, :] for j in range(2)]
        yb = [A[:, 44 + 2 * j:46 + 2 * j, :] for j in range(2)]
        PAIRS_MIN = 2 * T // T * (T // P) // 2
        PAIRS_MAX = NB // 2

        def rwait(eng, sem, value):
            eng.wait_ge(sem, value)
            eng.sem_inc(S("waits"), 1)

        def pairs(eng):
            eng.wait_ge(S("blocks"), 1)
            return eng.value_load(blki[0:1, NB:NB + 1], min_val=PAIRS_MIN, max_val=PAIRS_MAX)

        block = ctx.enter_context(nc.Block())

        def freed(eng, g):
            if g >= 0:
                e, n = EMPTIED[g]
                eng.wait_ge(S({"A": "ev_act", "D": "ev_dve", "X": "xt"}[e]), n)

        def hidden_hi(t):
            if t < 13:
                return top_r[:, t, :]
            return h_r[:, t - 13, :] if t < 21 else h_hi_r[:, 0, :]

        def ada_sums(a):
            return A[:, 52 + a if a < 4 else 12 + a, :]

        def unit_slot(name):
            return UIDX[name] % 2

        def unit_here(eng, name):
            u = UIDX[name]
            eng.wait_ge(S(f"unit{u % 2}"), 16 * (u // 2 + 1))

        @block.sync
        def _(sp):
            sp.dma_start(vec[:], vecs).then_inc(S("small"), 16)
            sp.dma_start(cst[:], cst_in).then_inc(S("small"), 16)
            sp.dma_start(bif[0:4], b_if[0:4]).then_inc(S("small"), 16)
            sp.dma_start(bif[32:36], b_if[4:8]).then_inc(S("small"), 16)
            sp.dma_start(row[:], rows.partition_broadcast(P)).then_inc(S("small"), 16)
            sp.dma_start(x[:], xt_in).then_inc(S("x_in"), 16)
            sp.dma_start(wif[:], w_if).then_inc(S("small2"), 16)
            sp.dma_start(wrt[:], w_router).then_inc(S("small2"), 16)
            sp.dma_start(tok[:], ints[:, 0:16].rearrange("p (a b) -> p a b", b=2)).then_inc(S("small2"), 16)
            sp.dma_start(slots.rearrange("(p a) b -> p (a b)", p=P), ints[:, 16:16 + 2 * (NB + 2)]).then_inc(S("slots0"), 16)
            def load_ada(a):
                if a >= 2:
                    sp.wait_ge(S("ada_used"), a - 1)
                sp.dma_start(A[:, 24 + 8 * (a % 2):32 + 8 * (a % 2), :], wada[a]).then_inc(S(f"ada{a % 2}"), 16)

            for a in range(3):
                load_ada(a)
            sp.dma_start(ring[:, 0], wall[0]).then_inc(S("unit0"), 16)
            load_ada(3)
            sp.dma_start(ring[:, 1], wall[1]).then_inc(S("unit1"), 16)
            for a in range(4, 12):
                load_ada(a)
            for u in range(2, NU1):
                sp.wait_ge(S("mm"), UNIT_USED[UNITS[u - 2]])
                sp.dma_start(ring[:, u % 2], wall[u]).then_inc(S(f"unit{u % 2}"), 16)

            for t in range(NT):
                sp.wait_ge(S("ht_ev"), t + 1)
                sp.dma_start(f_tok[t * P:(t + 1) * P, :], A[:, 2 * t:2 * t + 2, :].rearrange("p a b -> p (a b)")).then_inc(S("f_tok"), 16)
            n = pairs(sp)
            sp.wait_ge(S("f_tok"), 16 * NT)

            def expert(b, j, part):
                e = sp.value_load(blki[0:1, bass.ds(b, 1)], min_val=0, max_val=E - 1)
                return wexp[bass.ds(e, 1), part].rearrange("a p k n -> p (a k) n")

            order = [(0, 0), (0, 1), (1, 0), (1, 1), (0, 2), (1, 2)]
            for j, part in order:
                if j == 1 and part < 2:
                    sp.wait_ge(S(f"w0{part}"), 16)
                sp.dma_start(moe_w[j][part], expert(j, j, part)).then_inc(S(f"w{j}{part}"), 16)
            with sp.Fori(1, n) as i:
                for j, part in order:
                    rwait(sp, S("m_dn" if part == 2 else "m_gu"), 2 * i + j - 1)
                    sp.dma_start(moe_w[j][part], expert(2 * i + j, j, part)).then_inc(S(f"w{j}{part}"), 16)
            for j in range(2):
                rwait(sp, S(f"sc{j}"), 16 * n + 16 * NT)
            rwait(sp, S("m_dn"), 2 * n)
            for t in range(NT):
                sp.dma_start(A[:, 4 * t:4 * t + 4, :], y_asg.rearrange("(t p c) d -> t p (c d)", p=P, c=2)[t]).then_inc(S("y2"), 16)
            for u in range(NU1, NU1 + 2):
                sp.dma_start(ring[:, u % 2], wall[u]).then_inc(S(f"unit{u % 2}"), 16)

            sp.dma_start(wab[:], w_ab).then_inc(S("small3"), 16)
            sp.dma_start(levels[:], levels_in.rearrange("p (l f) -> p l f", f=P)).then_inc(S("small3"), 16)

            def load(u):
                sp.wait_ge(S("mm"), UNIT_USED[UNITS[u - 2]])
                sp.dma_start(ring[:, u % 2], wall[u]).then_inc(S(f"unit{u % 2}"), 16)

            def load_up(layer):
                u0 = UIDX[f"up{layer}_0"]
                load(u0)
                load(u0 + 1)
                with sp.Fori(0, (FU - 3) // 2) as i:
                    for j in range(2):
                        sp.wait_ge(S("mm"), 8 * i + UNIT_USED[UNITS[u0 + j]])
                        sp.dma_start(ring[:, (u0 + j) % 2], wall[bass.ds(2 * i + u0 + 2 + j, 1)].rearrange("a p k n -> p (a k) n")).then_inc(S(f"unit{(u0 + j) % 2}"), 16)
                load(u0 + FU - 1)

            for u in range(NU1 + 2, UIDX["up0_0"]):
                load(u)
            load_up(0)
            for u in range(UIDX["down0_0"], UIDX["w_q1"] + 1):
                load(u)
            sp.wait_ge(S("xt"), 40)
            sp.dma_start(A[:, 12:20, :], att_bias.rearrange("p a b -> p (a b)").rearrange("p (a b) -> p a b", b=512)).then_inc(S("bias"), 16)
            for u in range(UIDX["w_q1"] + 1, UIDX["up1_0"]):
                load(u)
            load_up(1)
            for u in range(UIDX["down1_0"], NU):
                load(u)
            sp.wait_ge(S("h"), 56)
            sp.dma_start(out_t, h[:]).then_inc(S("out"), 16)
            sp.wait_ge(S("out"), 16)

        @block.tensor
        def _(pe):
            mm = nc.tensor.matmul

            def group(g, k_tiles, rhs, lhs=None, k0=0):
                name = GROUPS[g][0][0]
                unit_here(pe, name)
                freed(pe, g - 2)
                if g in (1, 2):
                    for a in range(4 * g, 4 * g + 4):
                        ada(a, 4 * (g % 2) + 3)
                w = ring[:, unit_slot(name)]
                for j in range(4):
                    if g in (1, 2) and j == 3:
                        pe.wait_ge(S("mod_ev"), g + 1)
                    for k in range(k_tiles):
                        last = mm(PS[:, 4 * (g % 2) + j, :], w[:, k0 + k, j * P:(j + 1) * P] if lhs is None else lhs(j, k, w),
                                  rhs(k) if lhs is None else rhs(k, w), start=k == 0, stop=k == k_tiles - 1)
                    last.then_inc(S("mm"), 1)

            def wait_h(n):
                pe.wait_ge(S("h"), KD * (n + 1))

            def norm(n, bank):
                for k in range(KD):
                    pe.wait_ge(S("sq"), KD * n + k + 1)
                    mm(PS[:, bank, :], ones, sq[:, k % 2, :], start=k == 0, stop=k == KD - 1).then_inc(S("sq_used"), 1)

            pe.wait_ge(S("small"), 80)
            norm(0, 0)

            def ada(a, bank):
                pe.wait_ge(S("ada_used"), a + 1)
                for j in range(4):
                    last = mm(PS[:, bank, 4 * a + j:4 * a + j + 1], ada_sums(a)[:, j * P:(j + 1) * P], ones[:, 0:1], start=True, stop=True)
                last.then_inc(S("ada_sum"), 1)

            for a in range(4):
                ada(a, 1)
            wait_h(0)
            pe.wait_ge(S("small2"), 48)
            for k in range(KD):
                last = mm(PS[0:64, 4, :], wif[:, k, :], h[:, k, :], start=k == 0, stop=k == KD - 1)
            last.then_inc(S("if_mm"), 1)
            for g in range(10):
                if g == 1:
                    pe.wait_ge(S("if_ev"), 2)
                if g == 4:
                    group(g, KD, lambda k, w: w[:, k, :], lambda j, k, w: h[:, k, j * P:(j + 1) * P])
                else:
                    group(g, KD, lambda k: h[:, k, :])

            freed(pe, 8)
            pe.wait_ge(S("cv"), CT)
            for i in range(CT):
                last = mm(PS[:, 0, :], ones, A[:, 40 + i, :], start=i == 0, stop=i == CT - 1)
            last.then_inc(S("cl_mm"), 1)
            for i in range(CT):
                pe.wait_ge(S("cl_sq"), i + 1)
                last = mm(PS[:, 2, :], ones, A[:, 4 + i, :], start=i == 0, stop=i == CT - 1)
            last.then_inc(S("cl_mm"), 1)
            pe.wait_ge(S("g_rows"), 1)
            for t in range(NT):
                last = nc.tensor.transpose(PS[:, 3, 4 * t:4 * t + 4], gr[5][:, t * P:(t + 1) * P], ident[0:4, 0:4])
            last.then_inc(S("gT_mm"), 1)

            pe.wait_ge(S("qk"), 8)
            freed(pe, 9)
            pe.wait_ge(S("mod_ev"), 3)
            pe.wait_ge(S("gT_ev"), 1)
            pe.wait_ge(S("cl_ev"), 1)
            pe.wait_ge(S("em"), 1)
            for hd in range(MH):
                if hd:
                    pe.wait_ge(S("ml_h"), hd)
                for s in range(NT):
                    mm(PS[:, s, 0:T - s * P], A[:, 48 + hd, s * P:(s + 1) * P], A[:, 44 + hd, s * P:T], start=True, stop=True)
                sel = ident[0:4, hd:hd + 1].broadcast_to([4, P])
                mm(PS[:, 4, :], sel, gr[6], start=True, stop=True)
                mm(PS[:, 5, :], sel, gr[7], start=True, stop=True).then_inc(S("ml_s"), 1)
                for s in range(NT):
                    pe.wait_ge(S("ml_p"), NT * hd + s + 1)
                    mm(PS[:, 6, s * P:T], A[:, 16 + s, hd * P:(hd + 1) * P], A[:, 52 + s, s * P:T], start=s == 0,
                       stop=s == NT - 1)
                    last = mm(PS[:, 7, s * P:T], ones, A[:, 52 + s, s * P:T], start=s == 0, stop=s == NT - 1)
                last.then_inc(S("ml_n"), 1)
            pe.wait_ge(S("ml_h"), MH)
            for hd in range(MH):
                mm(PS[:, hd, :], ones, A[:, 8 + hd, :], start=True, stop=True).then_inc(S("ml_mu"), 1)
            for hd in range(MH):
                pe.wait_ge(S("ml_sq"), hd + 1)
                mm(PS[:, 4 + hd, :], ones, A[:, 12 + hd, :], start=True, stop=True).then_inc(S("ml_var"), 1)
            pe.wait_ge(S("ya_in"), CT)
            pe.wait_ge(S("ml_std"), MH)
            for m in range(2):
                group(G_CONV + m, CT, lambda k: A[:, 40 + k, :], k0=0 if m == 0 else 4)
            pe.wait_ge(S("hm"), MH)
            for m in range(2):
                group(G_MOUT + m, CT, lambda k: A[:, 8 + k, :], k0=0 if m == 0 else 4)
            for m in range(2):
                pe.wait_ge(S("merged"), KD)
                group(G_WOUT + m, KD, lambda k: A[:, 24 + k, :])
            norm(1, 4 * (G_WOUT % 2))
            wait_h(1)
            freed(pe, 15)
            for t in range(NT):
                for k in range(KD):
                    last = mm(PS[:, 0, 64 * t:64 * t + NG + E], h[:, k, t * P:(t + 1) * P], wrt[:, k, :], start=k == 0, stop=k == KD - 1)
            last.then_inc(S("logits"), 1)
            for t in range(NT):
                if t >= 2:
                    pe.wait_ge(S("ht_ev"), t - 1)
                for k in range(KD):
                    last = nc.tensor.transpose(PS[:, 2 + 2 * (t % 2) + k // 4, (k % 4) * P:(k % 4 + 1) * P], h[:, k, t * P:(t + 1) * P], ident)
                last.then_inc(S("ht_mm"), 1)
            pe.wait_ge(S("asg"), 1)
            for t in range(NT):
                for u in range(t + 1):
                    mm(PS[:, 6, t * E:(t + 1) * E], C("tri_strict") if u == t else ones, asg[2][:, u, :], start=u == 0, stop=u == t)
            for u in range(NT):
                last = mm(PS[:, 7, 0:E], ones, asg[2][:, u, :], start=u == 0, stop=u == NT - 1)
            last.then_inc(S("rank"), 1)
            n = pairs(pe)
            pe.wait_ge(S("ht_ev"), NT)
            with pe.Fori(0, n) as i:
                for j in range(2):
                    pe.wait_ge(S(f"xg{j}"), 16 * i + 16)
                    for k in range(KD):
                        last = nc.tensor.transpose(PS[:, k // 4, (k % 4) * P:(k % 4 + 1) * P], xg[j][:, k // 4, (k % 4) * P:(k % 4 + 1) * P], ident)
                    last.then_inc(S("m_tr"), 1)
                    pe.wait_ge(S("m_xT"), 2 * i + j + 1)
                    for part in range(2):
                        pe.wait_ge(S(f"w{j}{part}"), 16 * i + 16)
                        for k in range(KD):
                            last = mm(PS[:, 2 + 2 * j + part, :], xgT[j][:, k // 4, (k % 4) * P:(k % 4 + 1) * P], moe_w[j][part][:, k, :],
                                      start=k == 0, stop=k == KD - 1)
                    last.then_inc(S("m_gu"), 1)
                for j in range(2):
                    pe.wait_ge(S("m_h"), 2 * i + j + 1)
                    for k in range(4):
                        last = nc.tensor.transpose(PS[:, 0, k * P:(k + 1) * P], hid[j][:, k * P:(k + 1) * P], ident)
                    last.then_inc(S("m_ht"), 1)
                    pe.wait_ge(S("m_hT"), 2 * i + j + 1)
                    pe.wait_ge(S(f"w{j}2"), 16 * i + 16)
                    pe.wait_ge(S("m_y"), 2 * i + j + 1)
                    for m in range(2):
                        for k in range(4):
                            last = mm(PS[:, 6 + m, :], hidT[j][:, k * P:(k + 1) * P], moe_w[j][2][:, 4 * m + k, :], start=k == 0, stop=k == 3)
                    last.then_inc(S("m_dn"), 1)
            for t in range(NT):
                pe.wait_ge(S("y_sum"), t + 1)
            for k in range(KD):
                for t in range(NT):
                    last = nc.tensor.transpose(PS[:, k, t * P:(t + 1) * P], A[:, 16 + 2 * t + k // 4, (k % 4) * P:(k % 4 + 1) * P], ident)
                last.then_inc(S("yT"), 1)
            norm(2, 0)

            def product(out, w, x_, first, last_):
                mm(out, w[0], x_[0], start=first, stop=False)
                mm(out, w[0], x_[1], start=False, stop=False)
                return mm(out, w[1], x_[0], start=False, stop=last_)

            def w_split(slot, k, cols):
                return w_hi_r[:, k, cols], ring_r[:, slot, k, cols]

            def h_split(k):
                return h_hi_r[:, k, :], h_r[:, k, :]

            def hb_split(k):
                return hb_hi_r[:, k, :], top_r[:, k, :]

            def wait_split(n):
                pe.wait_ge(S("h_lo"), KD * n)

            def sgroup(g, rhs):
                name = GROUPS[g][0][0]
                freed(pe, g - 2)
                for j in range(4):
                    pe.wait_ge(S("w_lo"), split_count(UIDX[name], j))
                    for k in range(KD):
                        last = product(PS[:, 4 * (g % 2) + j, :], w_split(unit_slot(name), k, slice(j * P, (j + 1) * P)), rhs(k), k == 0, k == KD - 1)
                    last.then_inc(S("mm"), 1)

            norm(3, 0)
            wait_split(1)
            pe.wait_ge(S("small3"), 32)
            for t in range(NT):
                for k in range(KD):
                    for part in range(2):
                        last = mm(PS[:, 4, 16 * t:16 * t + 16], h_split(k)[part][:, t * P:(t + 1) * P].bitcast(F32), wab[:, k, :],
                                  start=k == 0 and part == 0, stop=k == KD - 1 and part == 1)
            last.then_inc(S("ab_mm"), 1)
            for g in range(8):
                if g == 1:
                    pe.wait_ge(S("ab_ev"), 1)
                sgroup(G_AIN + g, h_split)
            freed(pe, G_AIN + 6)
            freed(pe, G_AIN + 7)
            for m in range(16):
                pe.wait_ge(S("l_sq"), m + 1)
                if m >= 8:
                    pe.wait_ge(S("l_ln"), m - 7)
                mm(PS[:, m % 8, :], ones, sq[:, m % 2, :], start=True, stop=True).then_inc(S("l_mm"), 1)
            pe.wait_ge(S("l_r"), 16)
            for t in range(NT):
                for which in range(2):
                    if which == 0:
                        pe.wait_ge(S("a_silu"), 24)
                        if t >= 2:
                            pe.wait_ge(S("vt"), t - 1)
                    else:
                        pe.wait_ge(S("l_n"), 16)
                        if t >= 2:
                            pe.wait_ge(S("kt"), t - 1)
                    b = 4 * (t % 2) + 2 * which
                    for hd in range(DH):
                        last = nc.tensor.transpose(PS[:, b + hd // 4, (hd % 4) * P:(hd % 4 + 1) * P], A[:, (8 if which else 46) + hd, t * P:(t + 1) * P], ident)
                    last.then_inc(S("vk_mm"), 1)
            pe.wait_ge(S("g"), 1)
            pe.wait_ge(S("vt"), NT)
            for c in range(NT):
                last = mm(PS[:, 0, 8 * c:8 * c + 8], C("tri_incl"), dl[1][:, c, :], start=True, stop=True)
            last.then_inc(S("gc_mm"), 1)
            pe.wait_ge(S("kt"), NT)
            pe.wait_ge(S("gc"), 1)

            def heads(bank, lhs, rhs, sets=(0, 1)):
                for hd in range(4 * sets[0], 4 * sets[-1] + 4):
                    last = mm(PS[:, bank + hd // 4, (hd % 4) * P:(hd % 4 + 1) * P], lhs(hd), rhs(hd), start=True, stop=True)
                return last

            def hv(u):
                return lambda hd: A[:, u + hd // 4, (hd % 4) * P:(hd % 4 + 1) * P]

            def identity(hd):
                return ident

            for c in range(NT):
                cols = slice(c * P, (c + 1) * P)

                def qT(hd):
                    return A[:, hd, cols]

                def kT(hd):
                    return A[:, 8 + hd, cols]

                if c:
                    pe.wait_ge(S("d_S"), 2 * c)
                    pe.wait_ge(S("d_o"), 2 * c)
                heads(0, lambda hd: dl[1][:, c, hd:hd + 1].broadcast_to([P, P]), lambda hd: C("tri_incl")).then_inc(S("d_mm"), 1)
                heads(6, lambda hd: dl[0][:, c, hd:hd + 1].broadcast_to([P, P]), identity)
                heads(2, kT, kT).then_inc(S("d_mm"), 1)
                heads(4, kT, qT).then_inc(S("d_mm"), 1)
                pe.wait_ge(S("d_pre"), c + 1)
                for l in range(LEVELS):
                    n = LEVELS * c + l
                    for s in range(2):
                        pe.wait_ge(S(f"d_nl{s}"), n + 1)
                        if l:
                            pe.wait_ge(S(f"d_X{s}"), n)
                        heads(0, hv(48), identity if l == 0 else hv(52), (s,)).then_inc(S(f"d_p{s}"), 1)
                    if l:
                        for s in range(2):
                            pe.wait_ge(S(f"d_p1{s}"), c * (LEVELS - 1) + l)
                            if l < LEVELS - 1:
                                heads(2, hv(50), hv(54), (s,))
                            heads(4, hv(54), hv(50), (s,)).then_inc(S(f"d_dx{s}"), 1)
                if c:
                    for s in range(2):
                        heads(0, kT, hv(56), (s,)).then_inc(S("d_ks"), 1)
                for s in range(2):
                    pe.wait_ge(S(f"d_X{s}"), LEVELS * (c + 1))
                    if c:
                        pe.wait_ge(S("d_R"), 2 * (c - 1) + s + 1)
                    heads(2, hv(50), hv(54) if c else hv(24), (s,)).then_inc(S("d_vn"), 1)
                for s in range(2):
                    pe.wait_ge(S("d_vs"), 2 * c + s + 1)
                    for hd in range(4 * s, 4 * s + 4):
                        o = PS[:, 4 + s, (hd % 4) * P:(hd % 4 + 1) * P]
                        if c:
                            mm(o, hv(56)(hd), qT(hd), start=True, stop=False)
                        last = mm(o, hv(40)(hd), hv(44)(hd), start=not c, stop=True)
                    last.then_inc(S("d_om"), 1)
                    heads(6, hv(32 + 2 * c), hv(40), (s,)).then_inc(S("d_sm"), 1)
            pe.wait_ge(S("d_o"), 2 * NT)
            pe.wait_ge(S("d_S"), 2 * NT)
            for hd in range(DH):
                pe.wait_ge(S("o_sq"), hd + 1)
                mm(PS[:, hd, :], ones, sq[:, hd % 2, :], start=True, stop=True).then_inc(S("o_mm"), 1)
            wait_split(2)
            for m in range(2):
                sgroup(G_AOUT + m, h_split)

            def ffn(layer, g_up, g_dn):
                u0 = UIDX[f"up{layer}_0"]

                for j in range(2):
                    sgroup(g_up + j, h_split)
                with pe.Fori(0, (FU - 3) // 2) as i:
                    for j in range(2):
                        pe.wait_ge(S("ev_dve"), 8 * i + EMPTIED[g_up + j][1])
                        for t in range(4):
                            pe.wait_ge(S("w_lo"), 8 * i + split_count(u0 + 2 + j, t))
                            for k in range(KD):
                                last = product(PS[:, 4 * ((g_up + j) % 2) + t, :], w_split((u0 + j) % 2, k, slice(t * P, (t + 1) * P)), h_split(k), k == 0, k == KD - 1)
                            last.then_inc(S("mm"), 1)
                sgroup(g_up + FU - 1, h_split)
                for m in range(2):
                    g = g_dn + m
                    freed(pe, g - 2)
                    for ui in range(3):
                        u = UIDX[f"down{layer}_{3 * m + ui}"]
                        nk = 8 if ui < 2 else FT - 16
                        for j in range(4):
                            pe.wait_ge(S("w_lo"), split_count(u, j))
                            for k in range(nk):
                                if m == 0 and j == 0:
                                    pe.wait_ge(S("f_lo"), FT * layer + 8 * ui + k + 1)
                                last = product(PS[:, 4 * (g % 2) + j, :], w_split(u % 2, k, slice(j * P, (j + 1) * P)), (hidden_hi(8 * ui + k), hid_r[:, 8 * ui + k, :]),
                                               ui == 0 and k == 0, ui == 2 and k == nk - 1)
                            last.then_inc(S("mm"), 1)

            norm(4, NORM_BANK[4])
            wait_split(3)
            ffn(0, G_UP0, G_DN0)

            norm(5, NORM_BANK[5])
            wait_split(4)
            g = G_KV
            freed(pe, g - 2)
            for j in range(2):
                pe.wait_ge(S("w_lo"), split_count(UIDX["kv"], j))
                for k in range(KD):
                    last = product(PS[:, 4 * (g % 2) + j, :], w_split(unit_slot("kv"), k, slice(j * P, (j + 1) * P)), h_split(k), k == 0, k == KD - 1)
                last.then_inc(S("mm"), 1)
            pe.wait_ge(S("w_lo"), split_count(UIDX["kv"], 3))
            for j in range(2):
                for t in range(2 * j, 2 * j + 2):
                    for k in range(KD):
                        last = product(PS[:, 4 * (g % 2) + 2 + j, 256 * (t % 2):256 * (t % 2) + 256], [v[:, t * P:(t + 1) * P] for v in h_split(k)],
                                       w_split(unit_slot("kv"), k, slice(256, 512)), k == 0, k == KD - 1)
                last.then_inc(S("mm"), 1)
            wait_split(5)
            for m in range(2):
                sgroup(G_WQ + m, hb_split)

            def scores(n):
                b, m = n // 2, n % 2
                if n >= 2:
                    pe.wait_ge(S("at_o"), n - 1)
                k0 = max(b - 1, 0) * P
                for hh in range(8):
                    base = 64 * (hh // 4)
                    last = mm(PS[:, 4 * m + hh // 2, (hh % 2) * 256 + (0 if b else P):(hh % 2) * 256 + 256],
                              A[base:base + HD, 4 * m + hh % 4, b * P:(b + 1) * P], A[base:base + HD, 8 + m, k0:(b + 1) * P], start=True, stop=True)
                last.then_inc(S("at_s"), 1)

            freed(pe, G_WQ)
            freed(pe, G_WQ + 1)
            scores(0)
            scores(1)
            for n in range(2 * NT):
                b, m = n // 2, n % 2
                pe.wait_ge(S("at_pn"), n + 1)
                for hh in range(8):
                    for kk in range(0 if b else 1, 2):
                        i = 2 * hh + kk
                        last = nc.tensor.transpose(PS[:, 4 * m + i // 4, (i % 4) * P:(i % 4 + 1) * P], A[:, 20 + 4 * m + i // 4, (i % 4) * P:(i % 4 + 1) * P], ident)
                last.then_inc(S("at_t"), 1)
                pe.wait_ge(S("at_pt"), n + 1)
                for hh in range(8):
                    kv = 2 * m + hh // 4
                    for kk in range(0 if b else 1, 2):
                        i, t = 2 * hh + kk, b - 1 + kk
                        last = mm(PS[64 * (hh % 2):64 * (hh % 2) + HD, 4 * m, (hh // 2) * P:(hh // 2 + 1) * P],
                                  A[:, 10 + t // 2, 256 * (t % 2) + kv * HD:256 * (t % 2) + (kv + 1) * HD],
                                  A[:, 28 + 4 * m + i // 4, (i % 4) * P:(i % 4 + 1) * P], start=kk == 0 or not b, stop=kk == 1)
                last.then_inc(S("at_pv"), 1)
                if n + 2 < 2 * NT:
                    scores(n + 2)
            wait_split(6)
            for m in range(2):
                sgroup(G_WO + m, h_split)
            norm(6, NORM_BANK[6])
            wait_split(7)
            ffn(1, G_UP1, G_DN1)
            norm(7, NORM_BANK[7])

        @block.scalar
        def _(act):
            a_ = nc.scalar.activation
            chain = [0]

            def link(ins):
                chain[0] += 1
                ins.then_inc(S("act"), 1)
                act.wait_ge(S("act"), chain[0])

            def inv_sqrt(dst, src, e, scale):
                link(a_(dst, src, ACT.Ln, bias=eps[:, e:e + 1], scale=scale))
                return a_(dst, dst, ACT.Exp, scale=-0.5)

            def norm(n):
                for k in range(KD):
                    if n == 0:
                        act.wait_ge(S("x_in"), 16)
                    else:
                        act.wait_ge(S("xt"), KD * (n - 1) + k + 1)
                    if KD * n + k >= 2:
                        act.wait_ge(S("sq_used"), KD * n + k - 1)
                    a_(sq[:, k % 2, :], x[:, k, :], ACT.Square).then_inc(S("sq"), 1)
                act.wait_ge(S("sq_used"), KD * (n + 1))
                bank = NORM_BANK[n]
                inv_sqrt(rstd[:], PS[:, bank, :], 0, 1.0 / D).then_inc(S("std"), 1)

            act.wait_ge(S("small"), 80)
            a_(silc[:], V("c", 0, KD), ACT.Silu).then_inc(S("silc"), 1)
            act.wait_ge(S("eps"), 4)
            norm(0)
            for k in range(KD):
                act.wait_ge(S("h_pre"), k + 1)
                a_(h[:, k, :], h[:, k, :], ACT.Identity, bias=mod[:, k:k + 1]).then_inc(S("h"), 1)
            act.wait_ge(S("if_ev"), 2)
            a_(gr[2], gr[1], ACT.Abs).then_inc(S("ga"), 1)
            act.wait_ge(S("ga"), 1)
            a_(gr[2], gr[2], ACT.Exp, scale=-1.0).then_inc(S("ga"), 1)
            act.wait_ge(S("ga"), 2)
            a_(gr[2], gr[2], ACT.Ln, bias=eps[0:4, 2:3]).then_inc(S("ga"), 1)

            for g in range(10):
                for j in range(4):
                    act.wait_ge(S("mm"), TILE_DONE[g][j])
                    a_(A[:, 4 * g + j, :], PS[:, 4 * (g % 2) + j, :], ACT.Copy if g in (0, 2, 3, 4) else ACT.Sigmoid).then_inc(S("ev_act"), 1)
                if g == 0:
                    act.wait_ge(S("g_rows"), 2)
                    a_(gr[7], gr[7], ACT.Exp).then_inc(S("em"), 1)
            for m in range(8):
                act.wait_ge(S("qk_cv"), m + 1)
                a_(A[:, 44 + m, :], A[:, 44 + m, :], ACT.Silu).then_inc(S("qk"), 1)
            for i in range(CT):
                act.wait_ge(S("cl_d"), i + 1)
                a_(A[:, 4 + i, :], A[:, 40 + i, :], ACT.Square).then_inc(S("cl_sq"), 1)
            act.wait_ge(S("cl_mm"), 2)
            inv_sqrt(rstd[:], PS[:, 2, :], 1, 1.0 / DC).then_inc(S("cl_ev"), 1)
            for i in range(CT):
                act.wait_ge(S("cl_n"), i + 1)
                a_(A[:, 40 + i, :], A[:, 40 + i, :], ACT.Silu, bias=V("conv_ln_b", i)).then_inc(S("ya_in"), 1)
            act.wait_ge(S("gT_ev"), 1)
            for hd in range(MH):
                act.wait_ge(S("ml_m"), 2 * hd + 2)
                if hd:
                    act.wait_ge(S("ml_n"), hd)
                for s in range(NT):
                    bias = gT[:, s, hd:hd + 1]
                    w = a_(A[:, 52 + s, s * P:(s + 1) * P], A[:, 1, s * P:(s + 1) * P], ACT.Exp, bias=bias)
                    w.then_inc(S("ml_w"), 1)
                    if s < NT - 1:
                        a_(A[:, 52 + s, (s + 1) * P:T], A[:, 0, (s + 1) * P:T], ACT.Exp, bias=bias).then_inc(S("ml_w"), 1)
                act.wait_ge(S("ml_n"), hd + 1)
                a_(A[:, 2, :], PS[:, 7, :], ACT.Abs).then_inc(S("ml_ad"), 1)
            for hd in range(MH):
                act.wait_ge(S("ml_d"), hd + 1)
                a_(A[:, 12 + hd, :], A[:, 8 + hd, :], ACT.Square).then_inc(S("ml_sq"), 1)
            for hd in range(MH):
                act.wait_ge(S("ml_var"), hd + 1)
                a_(A[:, 4 + hd, :], PS[:, 4 + hd, :], ACT.Ln, bias=eps[:, 1:2], scale=1.0 / P).then_inc(S("ml_ln"), 1)
            act.wait_ge(S("ml_ln"), MH)
            for hd in range(MH):
                a_(A[:, 4 + hd, :], A[:, 4 + hd, :], ACT.Exp, scale=-0.5).then_inc(S("ml_std"), 1)
            norm(1)
            for k in range(KD):
                act.wait_ge(S("h_pre"), KD + k + 1)
                a_(h[:, k, :], h[:, k, :], ACT.Identity, bias=mod[:, 24 + k:25 + k]).then_inc(S("h"), 1)

            for t in range(NT):
                act.wait_ge(S("ht_mm"), t + 1)
                a_(A[:, 2 * t:2 * t + 2, :], PS[:, 2 + 2 * (t % 2):4 + 2 * (t % 2), :], ACT.Copy).then_inc(S("ht_ev"), 1)
            act.wait_ge(S("rg"), 1)
            a_(r4[0], r4[0], ACT.Exp).then_inc(S("rexp"), 1)
            act.wait_ge(S("rg"), 2)
            a_(rs[8], rs[8], ACT.Exp).then_inc(S("rexp"), 1)
            n = pairs(act)
            with act.Fori(0, n) as i:
                for j in range(2):
                    act.wait_ge(S("m_tr"), 2 * i + j + 1)
                    a_(xgT[j], PS[:, 0:2, :], ACT.Copy).then_inc(S("m_xT"), 1)
                    act.wait_ge(S("m_gu"), 2 * i + j + 1)
                    a_(hid[j], PS[:, 2 + 2 * j, :], ACT.Silu).then_inc(S("m_sg"), 1)
                for j in range(2):
                    act.wait_ge(S("m_dn"), 2 * i + j + 1)
                    rwait(act, S(f"sc{j}"), 16 * i + 16 * NT)
                    a_(yb[j], PS[:, 6:8, :], ACT.Copy).then_inc(S("m_y"), 1)
            norm(2)

            def w_hi(u, j, load_count=None, free_count=None, slot=None):
                slot = u % 2 if slot is None else slot
                act.wait_ge(S(f"unit{slot}"), 16 * (u // 2 + 1) if load_count is None else load_count)
                if free_count is not None or u > NU1:
                    act.wait_ge(S("mm"), tile_done(u - 1, j) if free_count is None else free_count)
                a_(w_hi_r[:, :, j * P:(j + 1) * P], ring[:, slot, :, j * P:(j + 1) * P], ACT.Copy).then_inc(S("w_hi"), 1)

            def h_hi(ready, count, src=None, dst=None):
                for k in range(KD):
                    act.wait_ge(S(ready), count - KD + k + 1)
                    a_((h_hi_r if dst is None else dst)[:, k, :], h[:, k, :] if src is None else A[:, src + k, :], ACT.Copy).then_inc(S("h_hi"), 1)

            norm(3)
            for j in range(4):
                w_hi(NU1, j)
            h_hi("h", KD * 3)
            act.wait_ge(S("ab_ev"), 1)
            a_(dl[0][:], ab[:, :, 0:DH], ACT.Sigmoid).then_inc(S("ab_a"), 1)
            link(a_(dl[1][:], ab[:, :, DH:2 * DH], ACT.Abs))
            link(a_(dl[1][:], dl[1][:], ACT.Exp, scale=-1.0))
            a_(dl[1][:], dl[1][:], ACT.Ln, bias=eps[:, 2:3]).then_inc(S("ab_a"), 1)
            a_(glast[:], R("a_gate")[:, DH:2 * DH], ACT.Exp).then_inc(S("ab_a"), 1)
            for m in range(24):
                w_hi(NU1 + 1 + m // 4, m % 4)
                act.wait_ge(S("ev_dve"), EMPTIED[G_AIN][1] - 4 + m + 1)
                u = A[:, m if m < 16 else 30 + m, :]
                a_(u, u, ACT.Silu).then_inc(S("a_silu"), 1)
            for g in (6, 7):
                for j in range(4):
                    if g == 6:
                        w_hi(NU1 + 7, j)
                    act.wait_ge(S("mm"), TILE_DONE[G_AIN + g][j])
                    a_(A[:, 16 + 4 * (g - 6) + j, :], PS[:, 4 * ((G_AIN + g) % 2) + j, :], ACT.Silu).then_inc(S("ev_act"), 1)
            act.wait_ge(S("a_silu"), 24)
            for half in range(2):
                for m in range(8 * half, 8 * half + 8):
                    if m >= 2:
                        act.wait_ge(S("l_mm"), m - 1)
                    a_(sq[:, m % 2, :], A[:, m, :], ACT.Square).then_inc(S("l_sq"), 1)
                for m in range(8 * half, 8 * half + 8):
                    act.wait_ge(S("l_mm"), m + 1)
                    a_(A[:, 30 + m, :], PS[:, m % 8, :], ACT.Ln, bias=eps[:, 0:1]).then_inc(S("l_ln"), 1)
            act.wait_ge(S("l_ln"), 16)
            for m in range(16):
                a_(A[:, 30 + m, :], A[:, 30 + m, :], ACT.Exp, scale=-0.5).then_inc(S("l_r"), 1)
            for t in range(NT):
                act.wait_ge(S("vk_mm"), 2 * t + 2)
                b = 4 * (t % 2) + 2
                a_(A[:, 32 + 2 * t:34 + 2 * t, :], PS[:, b:b + 2, :], ACT.Copy).then_inc(S("kt"), 1)
            act.wait_ge(S("gc"), 1)
            a_(dl[3][:], dl[2][:], ACT.Exp).then_inc(S("eg"), 1)
            for c in range(NT):
                act.wait_ge(S("d_mm"), 3 * c + 1)
                a_(A[:, 48:50, :], PS[:, 0:2, :], ACT.Exp).then_inc(S("d_eg"), 1)
                act.wait_ge(S("d_arg"), c + 1)
                a_(A[:, 42:44, :], A[:, 42:44, :], ACT.Exp).then_inc(S("d_et"), 1)
                for l in range(1, LEVELS):
                    for s in range(2):
                        act.wait_ge(S(f"d_p{s}"), LEVELS * c + l + 1)
                        a_(A[:, 54 + s, :], PS[:, s, :], ACT.Copy).then_inc(S(f"d_p1{s}"), 1)
                for s in range(2):
                    act.wait_ge(S("d_vn"), 2 * c + s + 1)
                    a_(A[:, 40 + s, :], PS[:, 2 + s, :], ACT.Copy).then_inc(S("d_vs"), 1)
                for s in range(2):
                    act.wait_ge(S("d_om"), 2 * c + s + 1)
                    a_(h[:, 4 * s:4 * s + 4, c * P:(c + 1) * P], PS[:, 4 + s, :].rearrange("p (a b) -> p a b", b=P), ACT.Copy).then_inc(S("d_o"), 1)
            act.wait_ge(S("d_o"), 2 * NT)
            act.wait_ge(S("d_S"), 2 * NT)
            u = UIDX["a_out0"]
            for j in range(4):
                w_hi(u, j)
            for hd in range(DH):
                if hd >= 2:
                    act.wait_ge(S("o_mm"), hd - 1)
                a_(sq[:, hd % 2, :], h[:, hd, :], ACT.Square).then_inc(S("o_sq"), 1)
            for hd in range(DH):
                act.wait_ge(S("o_mm"), hd + 1)
                a_(A[:, 46 + hd, :], PS[:, hd, :], ACT.Ln, bias=eps[:, 0:1], scale=1.0 / P).then_inc(S("o_ln"), 1)
            act.wait_ge(S("o_ln"), DH)
            for hd in range(DH):
                a_(A[:, 46 + hd, :], A[:, 46 + hd, :], ACT.Exp, scale=-0.5).then_inc(S("o_r"), 1)
            h_hi("o", DH)
            for m in range(2):
                for j in range(4):
                    w_hi(u + m + 1, j)

            def ffn(layer, g_up):
                ev0 = EMPTIED[g_up][1] - 4
                u0 = UIDX[f"up{layer}_0"]

                def unit(u, par, i):
                    for j in range(4):
                        w_hi(u0 + par + 1, j, 16 * i + 16 * ((u0 + par + 1) // 2 + 1), 8 * i + tile_done(u0 + par, j))
                        if j < 2:
                            act.wait_ge(S("ev_dve"), 4 * u + ev0 + j + 1)
                            t = A[:, 22 + 4 * par + j, :]
                            a_(t, t, ACT.Silu).then_inc(S("f_act"), 1)

                def hidden(tiles):
                    for t in tiles:
                        act.wait_ge(S("f_hid"), FT * layer + t + 1)
                        a_(hidden_hi(t), A[:, t, :], ACT.Copy).then_inc(S("f_hi"), 1)

                with act.Fori(0, FU // 2) as i:
                    for j in range(2):
                        unit(2 * i + j, j, i)
                hidden(range(13))
                unit(FU - 1, 0, FU // 2)
                act.wait_ge(S("mm"), UNIT_USED[f"up{layer}_{FU - 1}"])
                hidden(range(13, FT))
                for u in range(6):
                    for j in range(4):
                        if UIDX[f"down{layer}_{u}"] + 1 < NU:
                            w_hi(UIDX[f"down{layer}_{u}"] + 1, j)

            norm(4)
            h_hi("h", KD * 4)
            ffn(0, G_UP0)
            norm(5)
            h_hi("h", KD * 5)
            h_hi("hb", KD, 46, hb_hi_r)
            for u in (UIDX["w_q0"], UIDX["w_q1"]):
                for j in range(4):
                    w_hi(u, j)

            def exps(n):
                b, m = n // 2, n % 2
                act.wait_ge(S("at_m"), 2 * n + 2)
                link(a_(sm[2][:, m, :], sm[2][:, m, :], ACT.Exp))
                for hh in range(8):
                    p = A[:, 20 + 4 * m + hh // 2, (hh % 2) * 256 + (0 if b else P):(hh % 2) * 256 + 256]
                    last = a_(p, p, ACT.Exp, bias=sm[0][:, m, hh:hh + 1], accum_out=sm[1][:, m, hh:hh + 1])
                last.then_inc(S("at_p"), 1)

            exps(0)
            exps(1)
            for n in range(2 * NT):
                b, m = n // 2, n % 2
                act.wait_ge(S("at_t"), n + 1)
                if n >= 2:
                    act.wait_ge(S("at_pv"), n - 1)
                src, dst = PS[:, 4 * m:4 * m + 4, :], A[:, 28 + 4 * m:32 + 4 * m, :]
                if not b:
                    src, dst = (v.rearrange("p a (b c d) -> p (a b) c d", c=2, d=P)[:, :, 1, :] for v in (src, dst))
                a_(dst, src, ACT.Copy).then_inc(S("at_pt"), 1)
                if n + 2 < 2 * NT:
                    exps(n + 2)
            act.wait_ge(S("at_pv"), 2 * NT)
            for j in range(4):
                w_hi(UIDX["w_o0"], j)
            act.wait_ge(S("at_o"), 2 * NT)
            h_hi("at_o", 2 * NT)
            for m in range(2):
                for j in range(4):
                    w_hi(UIDX["w_o1"] + m, j)
            norm(6)
            h_hi("h", KD * 6)
            ffn(1, G_UP1)
            norm(7)

        @block.vector
        def _(dve):
            chain = [0]
            ts, tt, stt, cp = nc.vector.tensor_scalar, nc.vector.tensor_tensor, nc.vector.scalar_tensor_tensor, nc.vector.tensor_copy

            def link(ins):
                chain[0] += 1
                ins.then_inc(S("dve"), 1)
                dve.wait_ge(S("dve"), chain[0])

            for i, e in enumerate((1e-6, 1e-5, 1.0, 0.0)):
                nc.vector.memset(eps[:, i:i + 1], e).then_inc(S("eps"), 1)
            dve.wait_ge(S("x_in"), 16)
            dve.wait_ge(S("silc"), 1)

            def ada_acc(a):
                dve.wait_ge(S(f"ada{a % 2}"), 16 * (a // 2 + 1))
                w = A[:, 24 + 8 * (a % 2):32 + 8 * (a % 2), :]
                acc = ada_sums(a)
                link(ts(acc, w[:, 0, :], silc[:, 0:1], None, ALU.mult))
                for k in range(1, KD):
                    ins = stt(acc, w[:, k, :], silc[:, k:k + 1], acc, ALU.mult, ALU.add)
                    if k < KD - 1:
                        link(ins)
                ins.then_inc(S("ada_used"), 1)

            def mod_ev(n, bank):
                dve.wait_ge(S("ada_sum"), 4 * n + 4)
                tt(mod[:, 16 * n:16 * n + 16], PS[:, bank, 16 * n:16 * n + 16], V("b_ada", 16 * n, 16), ALU.add).then_inc(S("mod_ev"), 1)

            def gain(layer, gname, sc):
                link(ts(gm[:, layer, :], mod[:, sc:sc + KD], 1.0, None, ALU.add))
                link(tt(gm[:, layer, :], gm[:, layer, :], V(gname, 0, KD), ALU.mult))

            def norm(n, g, dst, done):
                dve.wait_ge(S("std"), n + 1)
                for k in range(KD):
                    stt(dst[:, k, :], x[:, k, :], g[:, k:k + 1], rstd[:], ALU.mult, ALU.mult).then_inc(S(done), 1)

            for a in range(4):
                ada_acc(a)
            mod_ev(0, 1)
            dve.wait_ge(S("mod_ev"), 1)
            gain(0, "g_norm1", 8)
            norm(0, gm[:, 0, :], h, "h_pre")
            dve.wait_ge(S("if_mm"), 1)
            ts(gr[0], PS[0:4, 4, :], bif[0:4], None, ALU.add).then_inc(S("if_ev"), 1)
            ts(gr[1], PS[32:36, 4, :], bif[32:36], None, ALU.add).then_inc(S("if_ev"), 1)
            dve.wait_ge(S("if_ev"), 2)
            link(nc.vector.memset(gr[4], 1.0))
            link(ts(gr[6], gr[1], 0.0, None, ALU.min))
            dve.wait_ge(S("ga"), 3)
            link(tt(gr[2], gr[6], gr[2], ALU.subtract))
            link(nc.vector.tensor_tensor_scan(gr[3], gr[4], gr[2], 0.0, ALU.mult, ALU.add))
            tt(gr[5], gr[0], gr[3], ALU.subtract).then_inc(S("g_rows"), 1)
            dve.wait_ge(S("g_rows"), 1)
            link(nc.vector.tensor_tensor_scan(gr[6], gr[5], gr[5], 0.0, ALU.max, ALU.max))
            link(ts(gr[6], gr[6], -1.0, None, ALU.mult))
            tt(gr[7], gr[6], gr[3], ALU.subtract).then_inc(S("g_rows"), 1)

            for n in (1, 2):
                for a in range(4 * n, 4 * n + 4):
                    ada_acc(a)
                mod_ev(n, 4 * (n % 2) + 3)
            for i in range(CT):
                dve.wait_ge(S("ev_act"), 4 + i + 1)
                link(tt(A[:, i, :], A[:, i, :], A[:, 4 + i, :], ALU.mult))

            def conv(dst, src, taps, w, b):
                if b is None:
                    link(ts(dst, src, w(taps - 1), None, ALU.mult))
                else:
                    link(ts(dst, src, w(taps - 1), b, ALU.mult, ALU.add))
                for j in range(taps - 2, -1, -1):
                    s = taps - 1 - j
                    ins = stt(dst[:, s:T], src[:, 0:T - s], w(j), dst[:, s:T], ALU.mult, ALU.add)
                    if j:
                        link(ins)
                return ins

            def conv_u(i):
                conv(A[:, 40 + i, :], A[:, i, :], TAPS, lambda j: V("conv_dw_w", CT * j + i), V("conv_dw_b", i)).then_inc(S("cv"), 1)

            def conv_qk(m):
                dve.wait_ge(S("ev_act"), 8 + m + 1)
                conv(A[:, 44 + m, :], A[:, 8 + m, :], QTAPS, lambda j: V("qk_conv_w", 8 * j + m), V("qk_conv_b", m)).then_inc(S("qk_cv"), 1)

            for i in range(CT):
                conv_u(i)
            for m in range(8):
                conv_qk(m)
            dve.wait_ge(S("cl_mm"), 1)
            dve.wait_ge(S("cv"), CT)
            for i in range(CT):
                stt(A[:, 40 + i, :], PS[:, 0, :], -1.0 / DC, A[:, 40 + i, :], ALU.mult, ALU.add).then_inc(S("cl_d"), 1)
            dve.wait_ge(S("mod_ev"), 3)
            gain(1, "g_norm2", 32)
            dve.wait_ge(S("cl_ev"), 1)
            dve.wait_ge(S("cl_d"), CT)
            for i in range(CT):
                stt(A[:, 40 + i, :], A[:, 40 + i, :], V("conv_ln_g", i), rstd[:], ALU.mult, ALU.mult).then_inc(S("cl_n"), 1)
            dve.wait_ge(S("gT_mm"), 1)
            cp(gT[:], PS[:, 3, 0:16].rearrange("p (a b) -> p a b", b=MH)).then_inc(S("gT_ev"), 1)
            for hd in range(MH):
                dve.wait_ge(S("ml_s"), hd + 1)
                cp(A[:, 0, :], PS[:, 4, :]).then_inc(S("ml_m"), 1)
                tt(A[:, 1, :].rearrange("p (a b) -> p a b", b=P), PS[:, 4, :].rearrange("p (a b) -> p a b", b=P),
                   C("after").rearrange("p (a b) -> p a b", a=1).broadcast_to([P, NT, P]), ALU.add).then_inc(S("ml_m"), 1)
                for s in range(NT):
                    dve.wait_ge(S("ml_w"), 7 * hd + min(2 * s + 2, 7))
                    stt(A[:, 52 + s, s * P:T], PS[:, s, 0:T - s * P], float(P) ** -0.5, A[:, 52 + s, s * P:T], ALU.mult, ALU.mult).then_inc(S("ml_p"), 1)
                dve.wait_ge(S("ml_ad"), hd + 1)
                link(tt(A[:, 2, :], A[:, 2, :], PS[:, 5, :], ALU.max))
                link(nc.vector.reciprocal(A[:, 3, :], A[:, 2, :]))
                tt(A[:, 8 + hd, :], PS[:, 6, :], A[:, 3, :], ALU.mult).then_inc(S("ml_h"), 1)
            dve.wait_ge(S("ml_h"), MH)
            for hd in range(MH):
                dve.wait_ge(S("ml_mu"), hd + 1)
                stt(A[:, 8 + hd, :], PS[:, hd, :], -1.0 / P, A[:, 8 + hd, :], ALU.mult, ALU.add).then_inc(S("ml_d"), 1)
            for hd in range(MH):
                dve.wait_ge(S("ml_std"), hd + 1)
                link(stt(A[:, 8 + hd, :], A[:, 8 + hd, :], V("m_norm_g", hd), A[:, 4 + hd, :], ALU.mult, ALU.mult))
                tt(A[:, 8 + hd, :], A[:, 8 + hd, :], A[:, 20 + hd, :], ALU.mult).then_inc(S("hm"), 1)
            for m in range(2):
                for j in range(4):
                    dve.wait_ge(S("mm"), TILE_DONE[G_CONV + m][j])
                    b = 4 * ((G_CONV + m) % 2) + j
                    tt(A[:, 24 + 4 * m + j, :], A[:, 24 + 4 * m + j, :], PS[:, b, :], ALU.mult).then_inc(S("ev_dve"), 1)
            for m in range(2):
                for j in range(4):
                    dve.wait_ge(S("mm"), TILE_DONE[G_MOUT + m][j])
                    b = 4 * ((G_MOUT + m) % 2) + j
                    tt(A[:, 32 + 4 * m + j, :], A[:, 32 + 4 * m + j, :], PS[:, b, :], ALU.mult).then_inc(S("ev_dve"), 1)
                    dve.wait_ge(S("ev_dve"), 8 + 4 * m + j + 1)
                    tt(A[:, 24 + 4 * m + j, :], A[:, 24 + 4 * m + j, :], A[:, 32 + 4 * m + j, :], ALU.add).then_inc(S("merged"), 1)

            def residual(g, n_of, scale_of=None, bias_of=None, next_unit=NU):
                for j in range(4):
                    if next_unit < NU:
                        w_lo(next_unit, j)
                    k = 4 * n_of + j
                    dve.wait_ge(S("mm"), TILE_DONE[g][j])
                    src = PS[:, 4 * (g % 2) + j, :]
                    if scale_of is not None:
                        ins = stt(x[:, k, :], src, scale_of(k), x[:, k, :], ALU.mult, ALU.add)
                    elif bias_of is not None:
                        ins = stt(x[:, k, :], src, bias_of(k), x[:, k, :], ALU.add, ALU.add)
                    else:
                        ins = tt(x[:, k, :], src, x[:, k, :], ALU.add)
                    ins.then_inc(S("xt"), 1)

            for m in range(2):
                residual(G_WOUT + m, m, scale_of=lambda k: mod[:, 16 + k:17 + k])
            norm(1, gm[:, 1, :], h, "h_pre")
            X3 = [P, NT, EPG]

            def b3(v, w):
                return v.rearrange("p (a b) -> p a b", b=1).broadcast_to([P, NT, w])

            def bnum(name, w):
                return C(name).rearrange("p (a b) -> p a b", a=1).broadcast_to([P, NT, w])

            def first_of(dst, vals, mx, num, w, t1):
                link(nc.vector.tensor_reduce(mx, vals, AX, ALU.max))
                link(tt(t1, vals, b3(mx, w), ALU.is_lt))
                link(stt(t1, t1, 1000.0, bnum(num, w), ALU.mult, ALU.add))
                link(nc.vector.tensor_reduce(rs[13], t1, AX, ALU.min))
                link(tt(dst, bnum(num, w), b3(rs[13], w), ALU.is_equal))

            dve.wait_ge(S("logits"), 1)
            link(tt(lg, PS[:, 0, 0:256].rearrange("p (a b) -> p a b", b=64)[:, :, 0:NG + E],
                    R("b_router").rearrange("p (a b) -> p a b", a=1).broadcast_to([P, NT, NG + E]), ALU.add))
            first_of(r4[1], lg[:, :, 0:NG], rs[0], "iota4", NG, r4[2])
            tt(r4[0], lg[:, :, 0:NG], b3(rs[0], NG), ALU.subtract).then_inc(S("rg"), 1)
            dve.wait_ge(S("rexp"), 1)
            link(nc.vector.tensor_reduce(rs[1], r4[0], AX, ALU.add))
            link(nc.vector.reciprocal(rs[2], rs[1]))
            for g in range(NG):
                le = lg[:, :, NG + g * EPG:NG + (g + 1) * EPG]
                og = r4[1][:, :, g:g + 1].broadcast_to(X3)
                if g == 0:
                    link(tt(r8[0], le, og, ALU.mult))
                else:
                    link(tt(r8[1], le, og, ALU.mult))
                    link(tt(r8[0], r8[0], r8[1], ALU.add))
            first_of(r8[2], r8[0], rs[3], "iota8", EPG, r8[1])
            link(stt(r8[3], r8[2], NEG, r8[0], ALU.mult, ALU.add))
            first_of(r8[4], r8[3], rs[4], "iota8", EPG, r8[1])
            tt(rs[8], rs[4], rs[3], ALU.subtract).then_inc(S("rg"), 1)
            dve.wait_ge(S("rexp"), 2)
            link(ts(rs[5], rs[8], 1.0, None, ALU.add))
            link(nc.vector.reciprocal(rs[6], rs[5]))
            link(tt(wtok[:, 0, :], rs[6], rs[2], ALU.mult))
            link(tt(wtok[:, 1, :], wtok[:, 0, :], rs[8], ALU.mult))
            for c in range(2):
                for g in range(NG):
                    link(tt(asg[c][:, :, g * EPG:(g + 1) * EPG], r8[2 + 2 * c], r4[1][:, :, g:g + 1].broadcast_to(X3), ALU.mult))
            tt(asg[2], asg[0], asg[1], ALU.add).then_inc(S("asg"), 1)
            dve.wait_ge(S("rank"), 1)
            link(cp(er[0], PS[:, 7, 0:E]))
            link(ts(er[1], er[0], 0.0, None, ALU.is_gt))
            for m in range(1, NT):
                link(ts(er[2], er[0], float(m * P), None, ALU.is_gt))
                link(tt(er[1], er[1], er[2], ALU.add))
            link(nc.vector.memset(er[3], 1.0))
            link(nc.vector.tensor_tensor_scan(er[4], er[3], er[1], 0.0, ALU.mult, ALU.add))
            link(tt(er[5], er[4], er[1], ALU.subtract))
            link(ts(er[5], er[5], float(P), None, ALU.mult))
            link(tt(asg[3], PS[:, 6, 0:NT * E].rearrange("p (a b) -> p a b", b=E), er[5].rearrange("p (a b) -> p a b", a=1).broadcast_to([P, NT, E]), ALU.add))
            for c in range(2):
                link(tt(asg[4], asg[3], asg[c], ALU.mult))
                link(nc.vector.tensor_reduce(rs[9 + c], asg[4], AX, ALU.add))
                cp(posi[:, c, :], rs[9 + c]).then_inc(S("posi"), 1)
            pend = er[4][0:1, :].rearrange("p (a b) -> p a b", a=1).broadcast_to([1, NB, E])
            link(tt(blk[0:1], pend, C("iotab")[0:1, :].rearrange("p (a b) -> p a b", b=1).broadcast_to([1, NB, E]), ALU.is_le))
            link(nc.vector.tensor_reduce(blkf[0:1, 0:NB], blk[0:1], AX, ALU.add))
            link(ts(blkf[0:1, 0:NB], blkf[0:1, 0:NB], float(E - 1), None, ALU.min))
            link(ts(blkf[0:1, NB:NB + 1], er[4][0:1, E - 1:E], 0.5, 0.25, ALU.mult, ALU.add))
            link(cp(blki[0:1, 0:NB], blkf[0:1, 0:NB]))
            cp(blki[0:1, NB:NB + 1], blkf[0:1, NB:NB + 1]).then_inc(S("blocks"), 1)
            nc.vector.memset(rs[12], 0.0).then_inc(S("m_y"), 1)
            n = pairs(dve)
            with dve.Fori(0, n) as i:
                for j in range(2):
                    dve.wait_ge(S("m_sg"), 2 * i + j + 1)
                    tt(hid[j], hid[j], PS[:, 3 + 2 * j, :], ALU.mult).then_inc(S("m_h"), 1)
                for j in range(2):
                    dve.wait_ge(S("m_ht"), 2 * i + j + 1)
                    cp(hidT[j], PS[:, 0, :]).then_inc(S("m_hT"), 1)
            dve.wait_ge(S("y2"), 16 * NT)
            for t in range(NT):
                y2 = A[:, 4 * t:4 * t + 4, :].rearrange("p a b -> p (a b)")
                yy = A[:, 16 + 2 * t:18 + 2 * t, :].rearrange("p a b -> p (a b)")
                link(ts(yy, y2[:, D:2 * D], wtok[:, 1, t:t + 1], None, ALU.mult))
                stt(yy, y2[:, 0:D], wtok[:, 0, t:t + 1], yy, ALU.mult, ALU.add).then_inc(S("y_sum"), 1)
            for k in range(KD):
                dve.wait_ge(S("yT"), k + 1)
                stt(x[:, k, :], PS[:, k, :], mod[:, 40 + k:41 + k], x[:, k, :], ALU.mult, ALU.add).then_inc(S("xt"), 1)
            norm(2, V("g_final", 0, KD), x, "xt")

            def w_lo(u, j, count=None, slot=None):
                slot = u % 2 if slot is None else slot
                dve.wait_ge(S("w_hi"), split_count(u, j) if count is None else count)
                cols = slice(j * P, (j + 1) * P)
                tt(ring_r[:, slot, :, cols], ring[:, slot, :, cols], w_hi_r[:, :, cols].bitcast(F32), ALU.subtract).then_inc(S("w_lo"), 1)

            h_sets = [0]

            def h_lo(src=None):
                for k in range(KD):
                    dve.wait_ge(S("h_hi"), KD * h_sets[0] + k + 1)
                    v, r, top = (h[:, k, :], h_r[:, k, :], h_hi_r[:, k, :]) if src is None else (A[:, src + k, :], top_r[:, k, :], hb_hi_r[:, k, :])
                    tt(r, v, top.bitcast(F32), ALU.subtract).then_inc(S("h_lo"), 1)
                h_sets[0] += 1

            norm(3, V("a_norm", 0, KD), h, "h")
            for j in range(4):
                w_lo(NU1, j)
            h_lo()
            dve.wait_ge(S("ab_mm"), 1)
            pab = PS[:, 4, 0:64].rearrange("p (a b) -> p a b", b=16)
            link(cp(ab[:, :, 0:DH], pab[:, :, 0:DH]))
            tt(ab[:, :, DH:2 * DH], pab[:, :, DH:2 * DH], R("a_gate")[:, 0:DH].rearrange("p (a b) -> p a b", a=1).broadcast_to([P, NT, DH]),
               ALU.add).then_inc(S("ab_ev"), 1)
            dve.wait_ge(S("ab_ev"), 1)
            link(ts(dl[5][:], ab[:, :, DH:2 * DH], 0.0, None, ALU.max))
            dve.wait_ge(S("ab_a"), 3)
            link(tt(dl[1][:], dl[1][:], dl[5][:], ALU.add))
            stt(dl[1][:], dl[1][:], -1.0, glast[:].rearrange("p (a b) -> p a b", a=1).broadcast_to([P, NT, DH]), ALU.mult, ALU.mult).then_inc(S("g"), 1)
            for m in range(24):
                g = G_AIN + m // 4
                w_lo(NU1 + 1 + m // 4, m % 4)
                dve.wait_ge(S("mm"), TILE_DONE[g][m % 4])
                dst = A[:, m if m < 16 else 30 + m, :]
                src = PS[:, 4 * (g % 2) + m % 4, :]
                conv(dst, src, 4, lambda j: V("a_conv_w", 24 * j + m), None).then_inc(S("ev_dve"), 1)
            for j in range(4):
                w_lo(NU1 + 7, j)
            for m in range(16):
                dve.wait_ge(S("l_r"), m + 1)
                r = A[:, 30 + m, :]
                if m < 8:
                    stt(A[:, m, :], A[:, m, :], float(P) ** -0.5, r, ALU.mult, ALU.mult).then_inc(S("l_n"), 1)
                else:
                    tt(A[:, m, :], A[:, m, :], r, ALU.mult).then_inc(S("l_n"), 1)

            def per_head(v, n=DH):
                return v.rearrange("p (a b) -> p a b", b=1).broadcast_to([P, n, P])

            def h3(v):
                return v.rearrange("p a (b c) -> p (a b) c", c=P)

            def m4(v):
                return v.rearrange("p (a b) -> p a b", b=P)

            for t in range(NT):
                dve.wait_ge(S("vk_mm"), 2 * t + 1)
                b = 4 * (t % 2)
                v_t = A[:, 24 + 2 * t:26 + 2 * t, :].rearrange("p a (b c) -> p (a b) c", c=P)
                tt(v_t, h3(PS[:, b:b + 2, :]), per_head(dl[0][:, t, :]), ALU.mult).then_inc(S("vt"), 1)
            dve.wait_ge(S("gc_mm"), 1)
            cp(dl[2][:], PS[:, 0, 0:32].rearrange("p (a b) -> p a b", b=DH)).then_inc(S("gc"), 1)
            dve.wait_ge(S("eg"), 1)
            link(stt(dl[4][:], dl[0][:], -1.0, dl[3][:], ALU.mult, ALU.mult))
            identb = ident.rearrange("p (a b) -> p a b", a=1).broadcast_to([P, 4, P])
            for c in range(NT):
                cols = slice(c * P, (c + 1) * P)
                dve.wait_ge(S("d_eg"), c + 1)
                for hd in range(DH):
                    part = slice((hd % 4) * P, (hd % 4 + 1) * P)
                    last = stt(A[:, 42 + hd // 4, part], PS[:, hd // 4, part], dl[2][:, c, hd:hd + 1], C("after"), ALU.subtract, ALU.add)
                last.then_inc(S("d_arg"), 1)
                link(cp(glast[:], h3(A[:, 48:50, :])[:, :, P - 1]))
                dve.wait_ge(S("d_mm"), 3 * c + 3)
                link(tt(A[:, 0:8, cols], A[:, 0:8, cols], h3(A[:, 48:50, :]), ALU.mult))
                dve.wait_ge(S("d_et"), c + 1)
                link(tt(A[:, 44:46, :], PS[:, 4:6, :], A[:, 42:44, :], ALU.mult))
                link(tt(A[:, 46:48, :], PS[:, 2:4, :], A[:, 42:44, :], ALU.mult))
                link(tt(A[:, 46:48, :], A[:, 46:48, :], PS[:, 6:8, :], ALU.mult))
                kd = h3(A[:, 32 + 2 * c:34 + 2 * c, :])
                tt(kd, kd, h3(A[:, 42:44, :])[:, :, P - 1:P].broadcast_to([P, DH, P]), ALU.mult).then_inc(S("d_pre"), 1)

                def nl(l, s):
                    tt(m4(A[:, 48 + s, :]), m4(A[:, 46 + s, :]), levels[:, l:l + 1, :].broadcast_to([P, 4, P]), ALU.mult).then_inc(S(f"d_nl{s}"), 1)

                for s in range(2):
                    nl(0, s)
                for l in range(LEVELS):
                    n = LEVELS * c + l
                    if l == 0:
                        for s in range(2):
                            dve.wait_ge(S(f"d_nl{s}"), n + 1)
                            link(tt(m4(A[:, 50 + s, :]), m4(A[:, 48 + s, :]), identb, ALU.add))
                            dve.wait_ge(S(f"d_p{s}"), n + 1)
                            tt(m4(A[:, 52 + s, :]), m4(PS[:, s, :]), identb, ALU.add).then_inc(S(f"d_X{s}"), 1)
                            nl(1, s)
                        continue
                    if l + 1 < LEVELS:
                        for s in range(2):
                            dve.wait_ge(S(f"d_p{s}"), n + 1)
                            nl(l + 1, s)
                    for s in range(2):
                        dve.wait_ge(S(f"d_dx{s}"), c * (LEVELS - 1) + l)
                        if l < LEVELS - 1:
                            link(tt(A[:, 52 + s, :], A[:, 52 + s, :], PS[:, 2 + s, :], ALU.add))
                        tt(A[:, 50 + s, :], A[:, 50 + s, :], PS[:, 4 + s, :], ALU.add).then_inc(S(f"d_X{s}"), 1)
                if c:
                    for s in range(2):
                        dve.wait_ge(S("d_ks"), 2 * (c - 1) + s + 1)
                        link(tt(m4(A[:, 54 + s, :]), m4(PS[:, s, :]), per_head(dl[4][:, c, 4 * s:4 * s + 4], 4), ALU.mult))
                        tt(A[:, 54 + s, :], A[:, 54 + s, :], A[:, 24 + 2 * c + s, :], ALU.add).then_inc(S("d_R"), 1)
                for s in range(2):
                    dve.wait_ge(S("d_sm"), 2 * c + s + 1)
                    if c:
                        link(tt(m4(A[:, 56 + s, :]), m4(A[:, 56 + s, :]), per_head(glast[:, 4 * s:4 * s + 4], 4), ALU.mult))
                        tt(A[:, 56 + s, :], A[:, 56 + s, :], PS[:, 6 + s, :], ALU.add).then_inc(S("d_S"), 1)
                    else:
                        cp(A[:, 56 + s, :], PS[:, 6 + s, :]).then_inc(S("d_S"), 1)
            for j in range(4):
                w_lo(UIDX["a_out0"], j)
            for hd in range(DH):
                dve.wait_ge(S("o_r"), hd + 1)
                link(stt(h[:, hd, :], h[:, hd, :], V("a_onorm"), A[:, 46 + hd, :], ALU.mult, ALU.mult))
                tt(h[:, hd, :], h[:, hd, :], A[:, 16 + hd, :], ALU.mult).then_inc(S("o"), 1)
            h_lo()
            for m in range(2):
                residual(G_AOUT + m, m, next_unit=UIDX["a_out0"] + m + 1)

            def ffn(layer, g_up, g_dn):
                ev0 = EMPTIED[g_up][1] - 4
                mm0 = TILE_DONE[g_up][0]
                LINKS = 8
                u0 = UIDX[f"up{layer}_0"]

                def unit(u, par, i):
                    done = [0]

                    def flink(ins):
                        done[0] += 1
                        ins.then_inc(S("dve_f"), 1)
                        dve.wait_ge(S("dve_f"), LINKS * u + (LINKS * FU * layer + done[0]))

                    for j in range(4):
                        w_lo(u0 + par + 1, j, 8 * i + split_count(u0 + par + 1, j))
                        dve.wait_ge(S("mm"), 4 * u + (mm0 + j))
                        t = A[:, 22 + 4 * par + j, :]
                        src = PS[:, 4 * ((g_up + par) % 2) + j, :]
                        tile = (j % 2) + (FT if j >= 2 else 0)

                        def col(name, base):
                            return vec[:, bass.ds(2 * u + (VOFF[name] + base + tile), 1)]

                        flink(ts(t, src, col("f_conv_w", (3 * layer + 2) * 2 * FT), col("f_conv_b", 2 * FT * layer), ALU.mult, ALU.add))
                        flink(stt(t[:, 1:T], src[:, 0:T - 1], col("f_conv_w", (3 * layer + 1) * 2 * FT), t[:, 1:T], ALU.mult, ALU.add))
                        stt(t[:, 2:T], src[:, 0:T - 2], col("f_conv_w", 3 * layer * 2 * FT), t[:, 2:T], ALU.mult, ALU.add).then_inc(S("ev_dve"), 1)
                    assert done[0] == LINKS
                    dve.wait_ge(S("ev_dve"), 4 * u + (ev0 + 4))
                    for j in range(2):
                        dve.wait_ge(S("f_act"), 2 * u + (FT * layer + j + 1))
                        tt(A[:, bass.ds(2 * u + j, 1), :].rearrange("p a b -> p (a b)"), A[:, 22 + 4 * par + j, :], A[:, 24 + 4 * par + j, :],
                           ALU.mult).then_inc(S("f_hid"), 1)

                def hidden(tiles):
                    for t in tiles:
                        dve.wait_ge(S("f_hi"), FT * layer + t + 1)
                        tt(hid_r[:, t, :], A[:, t, :], hidden_hi(t).bitcast(F32), ALU.subtract).then_inc(S("f_lo"), 1)

                with dve.Fori(0, FU // 2) as i:
                    for j in range(2):
                        unit(2 * i + j, j, i)
                hidden(range(13))
                unit(FU - 1, 0, FU // 2)
                hidden(range(13, FT))
                for m in range(2):
                    u = UIDX[f"down{layer}_{3 * m}"]
                    for j in range(8):
                        w_lo(u + 1 + j // 4, j % 4)
                    residual(g_dn + m, m, next_unit=u + 3)


            norm(4, V("f_norm", 0, KD), h, "h")
            h_lo()
            ffn(0, G_UP0, G_DN0)

            norm(5, V("kv_norm", 0, KD), h, "h")
            h_lo()
            for k in range(KD):
                stt(A[:, 46 + k, :], x[:, k, :], V("b_norm", k), rstd[:], ALU.mult, ALU.mult).then_inc(S("hb"), 1)
            h_lo(46)
            for j in range(4):
                if j < 2:
                    w_lo(UIDX["w_q0"], j)
                dve.wait_ge(S("mm"), TILE_DONE[G_KV][j])
                src = PS[:, 4 * (G_KV % 2) + j, :]
                if j < 2:
                    ts(A[:, 8 + j, :], src, V("kv_b", j), None, ALU.add).then_inc(S("ev_dve"), 1)
                else:
                    tt(A[:, 8 + j, :].rearrange("p (a b) -> p a b", b=256), src.rearrange("p (a b) -> p a b", b=256),
                       R("kv_b_v").rearrange("p (a b) -> p a b", a=1).broadcast_to([P, 2, 256]), ALU.add).then_inc(S("ev_dve"), 1)
            for j in (2, 3):
                w_lo(UIDX["w_q0"], j)
            for m in range(2):
                for j in range(4):
                    if m == 0:
                        w_lo(UIDX["w_q1"], j)
                    dve.wait_ge(S("mm"), TILE_DONE[G_WQ + m][j])
                    ts(A[:, 4 * m + j, :], PS[:, 4 * ((G_WQ + m) % 2) + j, :], V("b_b_q", 4 * m + j), float(HD) ** -0.5, ALU.add, ALU.mult).then_inc(S("ev_dve"), 1)

            def ph(m, b):
                v = A[:, 20 + 4 * m:24 + 4 * m, :].rearrange("p a (b c) -> p (a b) c", c=256)
                return v if b else v[:, :, P:256]

            def maxima(n):
                b, m = n // 2, n % 2
                dve.wait_ge(S("at_s"), n + 1)
                if n >= 2:
                    dve.wait_ge(S("at_t"), n - 1)
                src = PS[:, 4 * m:4 * m + 4, :].rearrange("p a (b c) -> p (a b) c", c=256)
                bias = A[:, 12 + 4 * m:16 + 4 * m, :].rearrange("p a (b c) -> p (a b) c", c=256)
                if not b:
                    src, bias = src[:, :, P:256], bias[:, :, P:256]
                link(tt(ph(m, b), src, bias, ALU.add))
                link(nc.vector.tensor_reduce(sm[3][:, m, :], ph(m, b), AX, ALU.max))
                sink = R("sinks")[:, 8 * m:8 * m + 8]
                link(tt(sm[3][:, m, :], sm[3][:, m, :], sink, ALU.max))
                ts(sm[0][:, m, :], sm[3][:, m, :], -1.0, None, ALU.mult).then_inc(S("at_m"), 1)
                tt(sm[2][:, m, :], sink, sm[3][:, m, :], ALU.subtract).then_inc(S("at_m"), 1)

            dve.wait_ge(S("bias"), 16)
            maxima(0)
            maxima(1)
            for n in range(2 * NT):
                b, m = n // 2, n % 2
                dve.wait_ge(S("at_p"), n + 1)
                link(tt(sm[1][:, m, :], sm[1][:, m, :], sm[2][:, m, :], ALU.add))
                link(nc.vector.reciprocal(sm[1][:, m, :], sm[1][:, m, :]))
                tt(ph(m, b), ph(m, b), sm[1][:, m, :].rearrange("p (a b) -> p a b", b=1).broadcast_to([P, 8, 256 if b else P]), ALU.mult).then_inc(S("at_pn"), 1)
                dve.wait_ge(S("at_pv"), n + 1)
                cp(h[:, 4 * m:4 * m + 4, b * P:(b + 1) * P], m4(PS[:, 4 * m, :])).then_inc(S("at_o"), 1)
                if n + 2 < 2 * NT:
                    maxima(n + 2)
            for j in range(4):
                w_lo(UIDX["w_o0"], j)
            h_lo()
            for m in range(2):
                residual(G_WO + m, m, bias_of=lambda k: V("b_b_o", k), next_unit=UIDX["w_o1"] + m)
            norm(6, V("f_norm", KD, KD), h, "h")
            h_lo()
            ffn(1, G_UP1, G_DN1)
            norm(7, V("final_norm", 0, KD), h, "h")

        @block.gpsimd
        def _(pool):
            pool.wait_ge(S("slots0"), 16)
            pool.wait_ge(S("small2"), 48)
            pool.wait_ge(S("posi"), 2)
            for t in range(NT):
                for c in range(2):
                    pool.indirect_dma_start(slots, bass.IndirectOffsetOnAxis(ap=posi[:, c, t:t + 1], axis=0),
                                            tok[:, 2 * t + c, :], None).then_inc(S(f"sc{c}"), 16)
            n = pairs(pool)
            for c in range(2):
                pool.wait_ge(S(f"sc{c}"), 16 * NT)
            pool.wait_ge(S("f_tok"), 16 * NT)

            def gather(b, j):
                pool.dma_start(idx[:, j, :], slots[bass.ds(b * P, P), :]).then_inc(S(f"idx{j}"), 16)

            def gather2(j, count):
                rwait(pool, S(f"idx{j}"), count)
                pool.indirect_dma_start(xg[j].rearrange("p a b -> p (a b)"), None, f_tok,
                                        bass.IndirectOffsetOnAxis(ap=idx[:, j, 0:1], axis=0)).then_inc(S(f"xg{j}"), 16)

            for j in range(2):
                gather(j, j)
            for j in range(2):
                gather2(j, 16)
            with pool.Fori(0, n) as i:
                for j in range(2):
                    rwait(pool, S(f"sc{j}"), 16 * i + 16 * NT)
                    rwait(pool, S(f"idx{j}"), 16 * i + 16)
                    nc.gpsimd.tensor_copy(sidx[:, j, :], idx[:, j, :]).then_inc(S("sidx"), 1)
                    rwait(pool, S("sidx"), 2 * i + j + 1)
                    rwait(pool, S(f"xg{j}"), 16 * i + 16)
                    gather(2 * i + 2 + j, j)
                    rwait(pool, S("m_tr"), 2 * i + j + 1)
                    gather2(j, 16 * i + 32)
                for j in range(2):
                    rwait(pool, S("m_y"), 2 * i + j + 2)
                    pool.indirect_dma_start(y_asg, bass.IndirectOffsetOnAxis(ap=sidx[:, j, 1:2], axis=0),
                                            yb[j].rearrange("p a b -> p (a b)"), None, bounds_check=2 * T - 1,
                                            oob_is_err=False).then_inc(S(f"sc{j}"), 16)
            for j in range(2):
                rwait(pool, S(f"xg{j}"), 16 * n + 16)
                rwait(pool, S(f"idx{j}"), 16 * n + 16)


NORM_BANK = [0, 0, 0, 0, 0, 4, 0, 4]


def slab(w, k0, nk, c0, nc_=512):
    return w[k0 * P:(k0 + nk) * P, c0:c0 + nc_].reshape(nk, P, nc_).transpose(1, 0, 2)


def feat(v):
    return np.ascontiguousarray(v.reshape(-1, P).T)


def pack(I):
    g = {k: np.asarray(v) for k, v in I.items()}
    w_in, ada = g["w_in"][0], g["w_ada"][0]
    wall = np.zeros((NU, P, 8, 512), np.float32)

    def put(name, *slabs):
        o = 0
        for s in slabs:
            wall[UIDX[name], :, o:o + s.shape[1]] = s
            o += s.shape[1]

    wada = np.stack([slab(ada, 0, 8, 512 * a) for a in range(12)])
    for i in range(10):
        put(f"in{i}", slab(w_in, 0, 8, 512 * i if i < 6 else 512 * i + 2 * MH))
    for n in ("conv_out", "m_out"):
        w = g["w_" + n][0]
        put(n, slab(w, 0, 4, 0), slab(w, 0, 4, 512))
    for m in range(2):
        put(f"w_out{m}", slab(g["w_out"][0], 0, 8, 512 * m))
        put(f"a_out{m}", slab(g["a_w_out_2"][0], 0, 8, 512 * m))
        put(f"w_o{m}", slab(g["b_w_o_2"][0], 0, 8, 512 * m))
        wq = g["b_w_q_2"][0].reshape(D, 2, 2, 4, HD)[:, m].transpose(0, 2, 1, 3).reshape(D, 512)
        put(f"w_q{m}", slab(wq, 0, 8, 0))
    for i in range(8):
        put(f"a_in{i}", slab(g["a_w_in_2"][0], 0, 8, 512 * i))
    put("kv", slab(g["kv_w_2"], 0, 8, 0))
    for l in range(2):
        up, dn = g["f_w_up_2"][l], g["f_w_down_2"][l]
        for i in range(FU):
            u = np.concatenate([slab(up, 0, 8, 256 * i, 256), slab(up, 0, 8, FF + 256 * i, 256)], 2)
            put(f"up{l}_{i}", u)
        for m in range(2):
            for i in range(3):
                put(f"down{l}_{3 * m + i}", slab(dn, 8 * i, 8 if i < 2 else FT - 16, 512 * m))
    we = np.empty((E, 3, P, 8, 512), np.float32)
    we[:, 0] = g["w_e_gate"][0].reshape(E, 8, P, 512).transpose(0, 2, 1, 3)
    we[:, 1] = g["w_e_up"][0].reshape(E, 8, P, 512).transpose(0, 2, 1, 3)
    we[:, 2] = g["w_e_down"][0].reshape(E, 4, P, 2, 512).transpose(0, 2, 3, 1, 4).reshape(E, P, 8, 512)
    wif = np.zeros((P, KD, 64), np.float32)
    wi = w_in[:, 3072:3072 + 2 * MH].reshape(KD, P, 2 * MH).transpose(1, 0, 2)
    wif[:, :, 0:4], wif[:, :, 32:36] = wi[:, :, 0:4], wi[:, :, 4:8]
    wr = np.concatenate([g["w_rg"][0], g["w_re"][0]], 1).reshape(KD, P, NG + E).transpose(1, 0, 2)
    wab = g["a_w_in_2"][0][:, 4096:].reshape(KD, P, 2 * DH).transpose(1, 0, 2)
    bq = g["b_b_q_2"][0].reshape(2, 2, 4, HD).transpose(0, 2, 1, 3)
    src = dict(c=g["c"], b_ada=g["b_ada"], g_norm1=g["g_norm1"], conv_dw_w=g["conv_dw_w"], conv_dw_b=g["conv_dw_b"],
               conv_ln_g=g["conv_ln_g"], conv_ln_b=g["conv_ln_b"], qk_conv_w=g["qk_conv_w"], qk_conv_b=g["qk_conv_b"],
               m_norm_g=g["m_norm_g"], g_norm2=g["g_norm2"], g_final=g["g_final"], a_norm=g["a_norm_2"],
               a_conv_w=g["a_conv_w_2"], a_onorm=g["a_onorm_2"], kv_norm=g["kv_norm_2"], kv_b=g["kv_b_2"][:256],
               b_norm=g["b_norm_2"], b_b_q=bq, b_b_o=g["b_b_o_2"], f_norm=g["f_norm_2"], f_conv_w=g["f_conv_w_2"],
               f_conv_b=g["f_conv_b_2"], final_norm=g["final_norm_2"])
    vecs = np.concatenate([feat(np.ascontiguousarray(src[n])) for n, _ in VECS], 1)
    assert vecs.shape == (P, NVEC)
    rows = np.concatenate([g["b_rg"][0], g["b_re"][0], g["a_dt_bias_2"][0], g["a_A_log_2"][0], g["kv_b_2"][256:], g["b_sinks_2"][0]])
    p, f = np.arange(P)[:, None], np.arange(P)[None, :]
    lev = []
    for l in range(LEVELS):
        lev.append(-(((f >> l) == (p >> l) + 1) & ((f >> l) % 2 == 1)).astype(np.float32))
    zero = np.zeros((P, 1), np.float32)
    cst = np.concatenate([np.eye(P), np.ones((P, P)), np.where(f < p, NEG, 0.0), (p < f) * 1.0, (p <= f) * 1.0,
                          zero + np.arange(NG), zero + np.arange(EPG), zero + np.arange(NB)], 1).astype(np.float32)
    t = np.arange(P)[:, None, None] + P * np.arange(NT)[None, :, None] + 0 * np.arange(2)[None, None, :]
    tokens = np.stack([t, 2 * t + np.arange(2)], -1).reshape(P, -1)
    none = np.tile(np.array([0, 2 * T], np.int64), (P, NB + 2))
    ints = np.concatenate([tokens, none], 1).astype(np.int32)
    dist = p + P - np.arange(2 * P)[None, :]
    slopes = 2.0 ** (-8.0 * np.arange(1, AH + 1, dtype=np.float32) / AH)
    ok = (dist >= 0) & (dist < P)
    att = np.where(ok[:, None, :], -slopes[None, :, None] * dist[:, None, :], NEG).astype(np.float32)
    xt = np.ascontiguousarray(g["x"][0].T.reshape(KD, P, T).transpose(1, 0, 2))
    return dict(xt_in=xt, wada=wada, wall=wall, wexp=we, w_if=wif, w_router=np.ascontiguousarray(wr), w_ab=np.ascontiguousarray(wab),
                vecs=vecs, rows=rows, b_if=np.ascontiguousarray(g["b_if"].reshape(8, 1)), cst_in=cst, ints=ints, att_bias=att,
                levels_in=np.concatenate(lev, 1))


def kernel(**inputs):
    import concourse.bacc as bacc
    from concourse.bass_utils import run_bass_kernel_spmd

    arrays = {name: np.ascontiguousarray(v) for name, v in pack(inputs).items()}
    nc = bacc.Bacc("TRN2", target_bir_lowering=False, num_devices=1)
    handles = {name: nc.dram_tensor(name, list(v.shape), mybir.dt.from_np(v.dtype), kind="ExternalInput").ap() for name, v in arrays.items()}
    out_t = nc.dram_tensor("out_t", [P, KD, T], F32, kind="ExternalOutput").ap()
    build(nc, out_t=out_t, **handles)
    result = run_bass_kernel_spmd(nc, [arrays], core_ids=[0])
    return np.ascontiguousarray(result.results[0]["out_t"].transpose(1, 0, 2).reshape(D, T).T[None])
```

```python
from contextlib import ExitStack

import numpy as np

import concourse.bass as bass
from concourse import mybir

ALU = mybir.AluOpType
ACT = mybir.ActivationFunctionType
AX = mybir.AxisListType.X
F32 = mybir.dt.float32
F32R = mybir.dt.float32r
I32 = mybir.dt.int32

P = 128
D = 1024
T = 512
KD = D // P
NT = T // P
NEG = -1.0e30

DC = 512
CT = DC // P
TAPS = 31
QTAPS = 4
MH = 4
E = 32
NG = 4
EPG = 8
NB = 2 * T // P + E
DH = 8
LEVELS = 7
AH = 16
HD = 64
KVH = 4
FF = 2816
FT = FF // P
FU = 11

VECS = [("c", 8), ("b_ada", 48), ("g_norm1", 8), ("conv_dw_w", TAPS * 4), ("conv_dw_b", 4), ("conv_ln_g", 4),
        ("conv_ln_b", 4), ("qk_conv_w", 32), ("qk_conv_b", 8), ("m_norm_g", 4), ("g_norm2", 8), ("g_final", 8),
        ("a_norm", 8), ("a_conv_w", 96), ("a_onorm", 1), ("kv_norm", 8), ("kv_b", 2), ("b_norm", 8), ("b_b_q", 8),
        ("b_b_o", 8), ("f_norm", 16), ("f_conv_w", 2 * 3 * 44), ("f_conv_b", 2 * 44), ("final_norm", 8)]
VOFF, NVEC = {}, 0
for _n, _w in VECS:
    VOFF[_n] = NVEC
    NVEC += _w
ROWS = [("b_router", NG + E), ("a_gate", 2 * DH), ("kv_b_v", 256), ("sinks", AH)]
ROFF, NROW = {}, 0
for _n, _w in ROWS:
    ROFF[_n] = NROW
    NROW += _w
CONSTS = [("ident", P), ("ones", P), ("after", P), ("tri_strict", P), ("tri_incl", P),
          ("iota4", NG), ("iota8", EPG), ("iotab", NB)]
COFF, NCST = {}, 0
for _n, _w in CONSTS:
    COFF[_n] = NCST
    NCST += _w

UNITS1 = [f"in{i}" for i in range(10)] + ["conv_out", "m_out", "w_out0", "w_out1"]
UNITS2 = ([f"a_in{i}" for i in range(8)] + ["a_out0", "a_out1"] + [f"up0_{i}" for i in range(FU)]
          + [f"down0_{i}" for i in range(6)] + ["kv", "w_q0", "w_q1", "w_o0", "w_o1"]
          + [f"up1_{i}" for i in range(FU)] + [f"down1_{i}" for i in range(6)])
UNITS = UNITS1 + UNITS2
NU1, NU = len(UNITS1), len(UNITS)
UIDX = {n: i for i, n in enumerate(UNITS)}

GROUPS = ([([f"in{i}"], "A") for i in range(10)] + [(["conv_out"], "D")] * 2 + [(["m_out"], "D")] * 2
          + [(["w_out0"], "X"), (["w_out1"], "X")]
          + [([f"a_in{i}"], "D" if i < 6 else "A") for i in range(8)] + [(["a_out0"], "X"), (["a_out1"], "X")]
          + [([f"up0_{i}"], "D") for i in range(FU)] + [([f"down0_{3 * m + i}" for i in range(3)], "X") for m in range(2)]
          + [(["kv"], "D"), (["w_q0"], "D"), (["w_q1"], "D"), (["w_o0"], "X"), (["w_o1"], "X")]
          + [([f"up1_{i}"], "D") for i in range(FU)] + [([f"down1_{3 * m + i}" for i in range(3)], "X") for m in range(2)])
G_CONV, G_MOUT, G_WOUT, G_AIN, G_AOUT, G_UP0, G_DN0, G_KV, G_WQ, G_WO, G_UP1, G_DN1 = 10, 12, 14, 16, 24, 26, 37, 39, 40, 42, 44, 55
TILE_DONE, UNIT_USED, EMPTIED = [], {}, []
_mm, _ev = 0, {"A": 0, "D": 0, "X": 0}
for _us, _e in GROUPS:
    if _us[0] == "conv_out" and _ev["A"] == 40:
        _ev["A"] += 1
    if _us[0] == "a_out0":
        _ev["X"] += 2 * KD
    for _u in _us[:-1]:
        _mm += 4
        UNIT_USED[_u] = _mm
    TILE_DONE.append([_mm + j + 1 for j in range(4)])
    _mm += 4
    UNIT_USED[_us[-1]] = _mm
    _ev[_e] += 4
    EMPTIED.append((_e, _ev[_e]))



PIECES1 = 40


def tile_done(u, j):
    if UNITS[u] == "kv" and j == 2:
        j = 3
    return UNIT_USED[UNITS[NU1 - 1]] + 4 * (u - NU1) + j + 1


def split_count(u, j):
    return PIECES1 + 4 * (u - NU1) + j + 1


def build(nc, xt_in, wada, wall, wexp, w_if, w_router, w_ab, vecs, rows, b_if, cst_in, ints, att_bias, levels_in, out_t):
    f_tok = nc.dram_tensor("h2_tokens", [T, D], F32, kind="Internal").ap()
    y_asg = nc.dram_tensor("y_assignments", [2 * T, D], F32, kind="Internal").ap()
    slots = nc.dram_tensor("slot_table", [(NB + 2) * P, 2], I32, kind="Internal").ap()

    ctx = ExitStack()
    with ctx:
        def sb(name, shape, dt=F32):
            return ctx.enter_context(nc.sbuf_tensor(name, shape, dt))

        sems = {}

        def S(name):
            if name not in sems:
                sems[name] = ctx.enter_context(nc.semaphore(name))
            return sems[name]

        PS = ctx.enter_context(nc.psum_tensor("PS", [P, 8, 512], F32))
        with ExitStack() as views:
            def view(name, *dims):
                return views.enter_context(nc.sbuf_tensor(name, [P, *dims], F32R))

            h_r = view("h_r", KD, T)
            ring_r = view("ring_r", 2, 8, 512)
            hid_r = view("hid_r", FT, 512)
            hb_hi_r = view("hb_hi_r", 8, 512)
            w_hi_r = view("w_hi_r", 8, 512)
            h_hi_r = view("h_hi_r", 8, 512)
            top_r = view("top_r", 13, 512)
            x_r = view("x_r", KD, T)
        h = sb("h", [P, KD, T])
        ring = sb("ring", [P, 2, 8, 512])
        A = sb("A", [P, 59, 512])
        x = sb("x", [P, KD, T])
        sq = sb("sq", [P, 2, T])
        rstd = sb("rstd", [P, T])
        vec = sb("vec", [P, NVEC])
        row = sb("row", [P, NROW])
        cst = sb("cst", [P, NCST])
        eps = sb("eps", [P, 4])
        mod = sb("mod", [P, 48])
        gm = sb("gm", [P, 2, KD])
        silc = sb("silc", [P, KD])

        def V(name, i=0, n=1):
            return vec[:, VOFF[name] + i:VOFF[name] + i + n]

        def C(name):
            w = dict(CONSTS)[name]
            return cst[:, COFF[name]:COFF[name] + w]

        def R(name):
            w = dict(ROWS)[name]
            return row[:, ROFF[name]:ROFF[name] + w]

        ident, ones = C("ident"), C("ones")

        wif = sb("wif", [P, KD, 64])
        bif = sb("bif", [64, 1])
        gr = [A[0:4, u, :] for u in (44, 45, 46, 47, 48, 56, 57, 58)]
        gT = sb("gT", [P, NT, MH])
        wrt = sb("wrt", [P, KD, NG + E])
        tok = sb("tok", [P, 8, 2], I32)
        idx = sb("idx", [P, 2, 2], I32)
        sidx = sb("sidx", [P, 2, 2], I32)
        wtok = sb("wtok", [P, 2, NT])
        blki = sb("blki", [1, NB + 2], I32)

        used_r = [0]

        def carve(*dims):
            n = int(np.prod(dims))
            v = A[:, 48:59, :].rearrange("p a b -> p (a b)")[:, used_r[0]:used_r[0] + n]
            used_r[0] += n
            if len(dims) == 2:
                return v.rearrange("p (a b) -> p a b", b=dims[1])
            if len(dims) == 3:
                return v.rearrange("p (a b c) -> p a b c", b=dims[1], c=dims[2])
            return v

        lg = carve(NT, NG + E)
        rs = [carve(NT) for _ in range(14)]
        r4 = [carve(NT, NG) for _ in range(3)]
        r8 = [carve(NT, EPG) for _ in range(5)]
        asg = [carve(NT, E) for _ in range(5)]
        er = [carve(E) for _ in range(6)]
        blk = carve(NB, E)
        blkf = carve(NB + 2)
        assert used_r[0] <= 11 * 512
        posi = sb("posi", [P, 2, NT], I32)
        wab = sb("wab", [P, KD, 2 * DH])
        levels = sb("levels", [P, LEVELS, P])
        ab = sb("ab", [P, NT, 2 * DH])
        dl = [sb(f"dl{i}", [P, NT, DH]) for i in range(6)]
        glast = sb("glast", [P, DH])
        ab_rows = A[0:2 * DH, 57, :]
        wab_hi, wab_lo = [top_r[:, 12, 256 * i:256 * i + KD * 2 * DH].rearrange("p (a b) -> p a b", b=2 * DH) for i in range(2)]
        sm = [sb(f"sm{i}", [P, 2, 8]) for i in range(4)]

        moe_w = [[ring[:, 0], ring[:, 1], A[:, 0:8]], [A[:, 8:16], A[:, 16:24], A[:, 24:32]]]
        xg = [A[:, 32 + 2 * j:34 + 2 * j, :] for j in range(2)]
        hid = [A[:, 40 + j, :] for j in range(2)]
        yb = [A[:, 44 + 2 * j:46 + 2 * j, :] for j in range(2)]
        PAIRS_MIN = 2 * T // T * (T // P) // 2
        PAIRS_MAX = NB // 2

        def a_r(u, n=1):
            for first, size, v in ((0, FT, hid_r), (22, 8, hb_hi_r), (30, 8, w_hi_r), (38, 8, h_hi_r), (46, 13, top_r)):
                if first <= u and u + n <= first + size:
                    return v[:, u - first:u - first + n, :]

        xT_hi, xT_lo = [[a_r(u + 2 * j, 2) for j in range(2)] for u in (48, 36)]
        hT_hi, hT_lo = [[a_r(u + j)[:, 0, :] for j in range(2)] for u in (52, 42)]

        PIECES, DEPTH = 24, 4

        def piece(p):
            return (p // 8, p % 8 // 4, 2 * (p % 4)) if p < 16 else ((p - 16) // 4, 2, 2 * (p % 4))

        def m_weights(p):
            j, part, k = piece(p)
            w = 8 * (3 * j + part - 2)
            lo = ring_r[:, part, k:k + 2, :] if w < 0 else a_r(w + k, 2)
            return moe_w[j][part][:, k:k + 2, :], lo, h_r[:, 2 * (p % DEPTH):2 * (p % DEPTH) + 2, :]

        def m_turn(i, n):
            return 4 * i + (n + 1)

        def m_used(i, p, back=0):
            return PIECES * i + (DEPTH + p + 1 - PIECES * back)

        def rwait(eng, sem, value):
            eng.wait_ge(sem, value)
            eng.sem_inc(S("waits"), 1)

        def pairs(eng):
            eng.wait_ge(S("blocks"), 1)
            return eng.value_load(blki[0:1, NB:NB + 1], min_val=PAIRS_MIN, max_val=PAIRS_MAX)

        block = ctx.enter_context(nc.Block())

        def freed(eng, g):
            if g >= 0:
                e, n = EMPTIED[g]
                eng.wait_ge(S({"A": "ev_act", "D": "ev_dve", "X": "xt"}[e]), n)

        def hidden_hi(t):
            if t < 13:
                return top_r[:, t, :]
            return h_r[:, t - 13, :] if t < 21 else h_hi_r[:, 0, :]

        def in_hi(p):
            return top_r[:, 6 + 2 * (p % 2):8 + 2 * (p % 2), :].rearrange("p a (b c) -> p (a b) c", c=P)

        wif_hi, wif_lo = [h_hi_r[:, 2 + i, :].rearrange("p (a b) -> p a b", b=64) for i in range(2)]

        def ada_place(a):
            u = (24, 32, 0, 8)[a] if a < 4 else 24 + 8 * (a % 2)
            return A[:, u:u + 8, :]

        def ada_sem(a):
            return f"ada{a if a < 4 else a % 2}"

        def ada_sums(a):
            return A[:, 52 + a if a < 4 else 12 + a, :]

        def unit_slot(name):
            return UIDX[name] % 2

        def unit_here(eng, name):
            u = UIDX[name]
            eng.wait_ge(S(f"unit{u % 2}"), 16 * (u // 2 + 1))

        @block.sync
        def _(sp):
            sp.dma_start(vec[:], vecs).then_inc(S("small"), 16)
            sp.dma_start(cst[:], cst_in).then_inc(S("small"), 16)
            sp.dma_start(bif[0:4], b_if[0:4]).then_inc(S("small"), 16)
            sp.dma_start(bif[32:36], b_if[4:8]).then_inc(S("small"), 16)
            sp.dma_start(row[:], rows.partition_broadcast(P)).then_inc(S("small"), 16)

            def load_ada(a):
                if a >= 4:
                    sp.wait_ge(S("ada_used"), a - 1 if a >= 6 else a - 3)
                sp.dma_start(ada_place(a), wada[a]).then_inc(S(ada_sem(a)), 16)

            load_ada(0)
            sp.dma_start(x[:], xt_in).then_inc(S("x_in"), 16)
            for a in range(1, 4):
                load_ada(a)
            sp.dma_start(wif[:], w_if).then_inc(S("small2"), 16)
            sp.dma_start(wrt[:], w_router).then_inc(S("small2"), 16)
            sp.dma_start(tok[:], ints[:, 0:16].rearrange("p (a b) -> p a b", b=2)).then_inc(S("small2"), 16)
            sp.dma_start(slots.rearrange("(p a) b -> p (a b)", p=P), ints[:, 16:16 + 2 * (NB + 2)]).then_inc(S("slots0"), 16)
            for u in range(2):
                sp.dma_start(ring[:, u], wall[u]).then_inc(S(f"unit{u}"), 16)
            for a in range(4, 8):
                load_ada(a)
            for u in range(2, NU1):
                if u == 3:
                    for a in range(8, 12):
                        load_ada(a)
                sp.wait_ge(S("mm"), UNIT_USED[UNITS[u - 2]])
                sp.dma_start(ring[:, u % 2], wall[u]).then_inc(S(f"unit{u % 2}"), 16)

            sp.wait_ge(S("mm"), UNIT_USED["in9"])
            sp.dma_start(x[:], xt_in).then_inc(S("x_in"), 16)

            for t in range(NT):
                sp.wait_ge(S("ht_ev"), t + 1)
                sp.dma_start(f_tok[t * P:(t + 1) * P, :], A[:, 2 * t:2 * t + 2, :].rearrange("p a b -> p (a b)")).then_inc(S("f_tok"), 16)
            n = pairs(sp)
            sp.wait_ge(S("f_tok"), 16 * NT)

            def expert(b, j, part):
                e = sp.value_load(blki[0:1, bass.ds(b, 1)], min_val=0, max_val=E - 1)
                return wexp[bass.ds(e, 1), part].rearrange("a p k n -> p (a k) n")

            order = [(0, 0), (0, 1), (1, 0), (1, 1), (0, 2), (1, 2)]
            for j, part in [(0, 0), (0, 1), (0, 2), (1, 0), (1, 1), (1, 2)]:
                if (j, part) == (1, 0):
                    sp.wait_ge(S("xg0"), 16)
                sp.dma_start(moe_w[j][part], expert(j, j, part)).then_inc(S(f"w{j}{part}"), 16)
            with sp.Fori(1, n) as i:
                for j, part in order:
                    rwait(sp, S("m_pc"), m_used(i, 19 + 4 * j if part == 2 else 8 * j + 4 * part + 3, back=1))
                    sp.dma_start(moe_w[j][part], expert(2 * i + j, j, part)).then_inc(S(f"w{j}{part}"), 16)
            for j in range(2):
                rwait(sp, S(f"sc{j}"), 16 * n + 16 * NT)
            rwait(sp, S("m_pc"), m_used(n, PIECES - 1, back=1))
            for t in range(NT):
                sp.dma_start(A[:, 4 * t:4 * t + 4, :], y_asg.rearrange("(t p c) d -> t p (c d)", p=P, c=2)[t]).then_inc(S("y2"), 16)
            for u in range(NU1, NU1 + 2):
                sp.dma_start(ring[:, u % 2], wall[u]).then_inc(S(f"unit{u % 2}"), 16)

            sp.dma_start(wab[:], w_ab).then_inc(S("small3"), 16)
            sp.dma_start(levels[:], levels_in.rearrange("p (l f) -> p l f", f=P)).then_inc(S("small3"), 16)

            def load(u):
                sp.wait_ge(S("mm"), UNIT_USED[UNITS[u - 2]])
                sp.dma_start(ring[:, u % 2], wall[u]).then_inc(S(f"unit{u % 2}"), 16)

            def load_up(layer):
                u0 = UIDX[f"up{layer}_0"]
                load(u0)
                load(u0 + 1)
                with sp.Fori(0, (FU - 3) // 2) as i:
                    for j in range(2):
                        sp.wait_ge(S("mm"), 8 * i + UNIT_USED[UNITS[u0 + j]])
                        sp.dma_start(ring[:, (u0 + j) % 2], wall[bass.ds(2 * i + u0 + 2 + j, 1)].rearrange("a p k n -> p (a k) n")).then_inc(S(f"unit{(u0 + j) % 2}"), 16)
                load(u0 + FU - 1)

            for u in range(NU1 + 2, UIDX["up0_0"]):
                load(u)
            load_up(0)
            for u in range(UIDX["down0_0"], UIDX["w_q1"] + 1):
                load(u)
            sp.wait_ge(S("xt"), 40)
            sp.dma_start(A[:, 12:20, :], att_bias.rearrange("p a b -> p (a b)").rearrange("p (a b) -> p a b", b=512)).then_inc(S("bias"), 16)
            for u in range(UIDX["w_q1"] + 1, UIDX["up1_0"]):
                load(u)
            load_up(1)
            for u in range(UIDX["down1_0"], NU):
                load(u)
            sp.wait_ge(S("h"), 56)
            sp.dma_start(out_t, h[:]).then_inc(S("out"), 16)
            sp.wait_ge(S("out"), 16)

        @block.tensor
        def _(pe):
            mm = nc.tensor.matmul

            def group(g, k_tiles, rhs, k0=0):
                name = GROUPS[g][0][0]
                unit_here(pe, name)
                freed(pe, g - 2)
                w = ring[:, unit_slot(name)]
                for j in range(4):
                    for k in range(k_tiles):
                        last = mm(PS[:, 4 * (g % 2) + j, :], w[:, k0 + k, j * P:(j + 1) * P], rhs(k), start=k == 0, stop=k == k_tiles - 1)
                    last.then_inc(S("mm"), 1)

            def wait_h(n):
                pe.wait_ge(S("h"), KD * (n + 1))

            def norm(n, bank):
                for k in range(KD):
                    pe.wait_ge(S("sq"), KD * n + k + 1)
                    mm(PS[:, bank, :], ones, sq[:, k % 2, :], start=k == 0, stop=k == KD - 1).then_inc(S("sq_used"), 1)

            pe.wait_ge(S("small"), 80)
            norm(0, 0)

            def ada(a, bank):
                pe.wait_ge(S("ada_used"), a + 1)
                for j in range(4):
                    last = mm(PS[:, bank, 4 * a + j:4 * a + j + 1], ada_sums(a)[:, j * P:(j + 1) * P], ones[:, 0:1], start=True, stop=True)
                last.then_inc(S("ada_sum"), 1)

            for a in range(4):
                ada(a, 1)
            def product(out, w, x_, first, last_):
                mm(out, w[0], x_[0], start=first, stop=False)
                mm(out, w[0], x_[1], start=False, stop=False)
                return mm(out, w[1], x_[0], start=False, stop=last_)

            def wait_split(n):
                pe.wait_ge(S("h_lo"), KD * (n + 1))

            wait_split(0)
            for k in range(KD):
                last = product(PS[0:64, 4, :], (wif_hi[:, k, :], wif_lo[:, k, :]), (x_r[:, k, :], h_r[:, k, :]), k == 0, k == KD - 1)
            last.then_inc(S("if_mm"), 1)
            for g in range(10):
                if g == 1:
                    pe.wait_ge(S("if_ev"), 2)
                freed(pe, g - 2)
                if g in (2, 3):
                    for a in range(4 * g - 4, 4 * g):
                        ada(a, 4 * (g % 2) + 3)
                for j in range(4):
                    p = 4 * g + j
                    if g in (2, 3) and j == 3:
                        pe.wait_ge(S("mod_ev"), g)
                    pe.wait_ge(S("w_lo"), p + 1)
                    for k in range(KD):
                        last = product(PS[:, 4 * (g % 2) + j, :], (in_hi(p)[:, k, :], ring_r[:, g % 2, k, j * P:(j + 1) * P]),
                                       (x_r[:, k, :], h_r[:, k, :]), k == 0, k == KD - 1)
                    last.then_inc(S("mm"), 1)
            freed(pe, 9)
            for t in range(NT):
                for hd in range(MH):
                    last = nc.tensor.transpose(PS[:, 4 + t, hd * P:(hd + 1) * P], A[:, 16 + hd, t * P:(t + 1) * P], ident)
            last.then_inc(S("gT_mm"), 1)

            freed(pe, 8)
            pe.wait_ge(S("cv"), CT)
            for i in range(CT):
                last = mm(PS[:, 0, :], ones, A[:, 40 + i, :], start=i == 0, stop=i == CT - 1)
            last.then_inc(S("cl_mm"), 1)
            for i in range(CT):
                pe.wait_ge(S("cl_sq"), i + 1)
                last = mm(PS[:, 2, :], ones, A[:, 4 + i, :], start=i == 0, stop=i == CT - 1)
            last.then_inc(S("cl_mm"), 1)
            pe.wait_ge(S("g_rows"), 1)
            for t in range(NT):
                last = nc.tensor.transpose(PS[:, 3, 4 * t:4 * t + 4], gr[5][:, t * P:(t + 1) * P], ident[0:4, 0:4])
            last.then_inc(S("gT_mm"), 1)

            pe.wait_ge(S("qk"), 8)
            pe.wait_ge(S("ev_act"), 41)
            pe.wait_ge(S("mod_ev"), 3)
            pe.wait_ge(S("gT_ev"), 1)
            pe.wait_ge(S("cl_ev"), 1)
            pe.wait_ge(S("em"), 1)
            for hd in range(MH):
                if hd:
                    pe.wait_ge(S("ml_h"), hd)
                for s in range(NT):
                    mm(PS[:, s, 0:T - s * P], A[:, 48 + hd, s * P:(s + 1) * P], A[:, 44 + hd, s * P:T], start=True, stop=True)
                sel = ident[0:4, hd:hd + 1].broadcast_to([4, P])
                mm(PS[:, 4, :], sel, gr[6], start=True, stop=True)
                mm(PS[:, 5, :], sel, gr[7], start=True, stop=True).then_inc(S("ml_s"), 1)
                for s in range(NT):
                    pe.wait_ge(S("ml_p"), NT * hd + s + 1)
                    mm(PS[:, 6, s * P:T], A[:, 16 + s, hd * P:(hd + 1) * P], A[:, 52 + s, s * P:T], start=s == 0,
                       stop=s == NT - 1)
                    last = mm(PS[:, 7, s * P:T], ones, A[:, 52 + s, s * P:T], start=s == 0, stop=s == NT - 1)
                last.then_inc(S("ml_n"), 1)
            pe.wait_ge(S("ml_h"), MH)
            for hd in range(MH):
                mm(PS[:, hd, :], ones, A[:, 8 + hd, :], start=True, stop=True).then_inc(S("ml_mu"), 1)
            for hd in range(MH):
                pe.wait_ge(S("ml_sq"), hd + 1)
                mm(PS[:, 4 + hd, :], ones, A[:, 12 + hd, :], start=True, stop=True).then_inc(S("ml_var"), 1)
            pe.wait_ge(S("ya_in"), CT)
            pe.wait_ge(S("ml_std"), MH)
            for m in range(2):
                group(G_CONV + m, CT, lambda k: A[:, 40 + k, :], k0=0 if m == 0 else 4)
            pe.wait_ge(S("hm"), MH)
            for m in range(2):
                group(G_MOUT + m, CT, lambda k: A[:, 8 + k, :], k0=0 if m == 0 else 4)
            for m in range(2):
                pe.wait_ge(S("merged"), KD)
                group(G_WOUT + m, KD, lambda k: A[:, 24 + k, :])
            norm(1, 4 * (G_WOUT % 2))
            wait_h(1)
            freed(pe, 15)
            for t in range(NT):
                for k in range(KD):
                    last = mm(PS[:, 0, 64 * t:64 * t + NG + E], h[:, k, t * P:(t + 1) * P], wrt[:, k, :], start=k == 0, stop=k == KD - 1)
            last.then_inc(S("logits"), 1)
            for t in range(NT):
                if t >= 2:
                    pe.wait_ge(S("ht_ev"), t - 1)
                for k in range(KD):
                    last = nc.tensor.transpose(PS[:, 2 + 2 * (t % 2) + k // 4, (k % 4) * P:(k % 4 + 1) * P], h[:, k, t * P:(t + 1) * P], ident)
                last.then_inc(S("ht_mm"), 1)
            pe.wait_ge(S("asg"), 1)
            for t in range(NT):
                for u in range(t + 1):
                    mm(PS[:, 6, t * E:(t + 1) * E], C("tri_strict") if u == t else ones, asg[2][:, u, :], start=u == 0, stop=u == t)
            for u in range(NT):
                last = mm(PS[:, 7, 0:E], ones, asg[2][:, u, :], start=u == 0, stop=u == NT - 1)
            last.then_inc(S("rank"), 1)
            n = pairs(pe)
            pe.wait_ge(S("ht_ev"), NT)

            def rows_T(j, count):
                pe.wait_ge(S(f"xg{j}"), count)
                for k in range(KD):
                    last = nc.tensor.transpose(PS[:, k // 4, (k % 4) * P:(k % 4 + 1) * P], xg[j][:, k // 4, (k % 4) * P:(k % 4 + 1) * P], ident)
                last.then_inc(S("m_tr"), 1)

            def hidden_T(j, i):
                pe.wait_ge(S("m_h"), 2 * i + j + 1)
                for k in range(4):
                    last = nc.tensor.transpose(PS[:, 0, k * P:(k + 1) * P], hid[j][:, k * P:(k + 1) * P], ident)
                last.then_inc(S("m_tr"), 1)

            rows_T(0, 16)
            with pe.Fori(0, n) as i:
                for p in range(PIECES):
                    j, part, k0 = piece(p)
                    if p in (0, 8):
                        pe.wait_ge(S("m_xl"), m_turn(i, j))
                    if p == 8:
                        pe.wait_ge(S("m_y1"), i + 1)
                    if p in (16, 20):
                        pe.wait_ge(S("m_xl"), m_turn(i, 2 + j))
                    if p == 16:
                        pe.wait_ge(S("m_y0"), i + 1)
                    pe.wait_ge(S("m_lo"), PIECES * i + p + 1)
                    _, lo, hi = m_weights(p)
                    for q in range(2):
                        k = k0 + q
                        if part < 2:
                            out, cols = PS[:, 2 + 2 * j + part, :], slice((k % 4) * P, (k % 4 + 1) * P)
                            x_hi, x_lo = xT_hi[j][:, k // 4, cols], xT_lo[j][:, k // 4, cols]
                            first, final = k == 0, k == KD - 1
                        else:
                            out, cols = PS[:, (6 if j == 0 else 4) + k // 4, :], slice((k % 4) * P, (k % 4 + 1) * P)
                            x_hi, x_lo = hT_hi[j][:, cols], hT_lo[j][:, cols]
                            first, final = k % 4 == 0, k % 4 == 3
                        mm(out, x_hi, hi[:, q, :], start=first, stop=False)
                        mm(out, x_lo, hi[:, q, :], start=False, stop=False)
                        last = mm(out, x_hi, lo[:, q, :], start=False, stop=final)
                    last.then_inc(S("m_pc"), 1)
                    if p == 3:
                        rows_T(1, 16 * i + 16)
                    if p == 12:
                        hidden_T(0, i)
                    if p == 17:
                        hidden_T(1, i)
                    if p == 21:
                        rows_T(0, 16 * i + 32)
            for t in range(NT):
                pe.wait_ge(S("y_sum"), t + 1)
            for k in range(KD):
                for t in range(NT):
                    last = nc.tensor.transpose(PS[:, k, t * P:(t + 1) * P], A[:, 16 + 2 * t + k // 4, (k % 4) * P:(k % 4 + 1) * P], ident)
                last.then_inc(S("yT"), 1)
            norm(2, 0)

            def w_split(slot, k, cols):
                return w_hi_r[:, k, cols], ring_r[:, slot, k, cols]

            def h_split(k):
                return h_hi_r[:, k, :], h_r[:, k, :]

            def hb_split(k):
                return hb_hi_r[:, k, :], top_r[:, k, :]

            def sgroup(g, rhs):
                name = GROUPS[g][0][0]
                freed(pe, g - 2)
                for j in range(4):
                    pe.wait_ge(S("w_lo"), split_count(UIDX[name], j))
                    if g == G_AIN + 1 and j == 3:
                        pe.wait_ge(S("ab_ev"), 2)
                    for k in range(KD):
                        last = product(PS[:, 4 * (g % 2) + j, :], w_split(unit_slot(name), k, slice(j * P, (j + 1) * P)), rhs(k), k == 0, k == KD - 1)
                    last.then_inc(S("mm"), 1)

            norm(3, 0)
            wait_split(1)
            for k in range(KD):
                last = product(PS[0:2 * DH, 4, :], (wab_hi[:, k, :], wab_lo[:, k, :]), h_split(k), k == 0, k == KD - 1)
            last.then_inc(S("ab_mm"), 1)
            sgroup(G_AIN, h_split)
            pe.wait_ge(S("ab_ev"), 1)
            for t in range(NT):
                last = nc.tensor.transpose(PS[:, 7, 16 * t:16 * t + 16], ab_rows[:, t * P:(t + 1) * P], ident[0:2 * DH, 0:2 * DH])
            last.then_inc(S("ab_mm"), 1)
            for g in range(1, 8):
                sgroup(G_AIN + g, h_split)
            freed(pe, G_AIN + 6)
            freed(pe, G_AIN + 7)
            for m in range(16):
                pe.wait_ge(S("l_sq"), m + 1)
                if m >= 8:
                    pe.wait_ge(S("l_ln"), m - 7)
                mm(PS[:, m % 8, :], ones, sq[:, m % 2, :], start=True, stop=True).then_inc(S("l_mm"), 1)
            pe.wait_ge(S("l_r"), 16)
            for t in range(NT):
                for which in range(2):
                    if which == 0:
                        pe.wait_ge(S("a_silu"), 24)
                        if t >= 2:
                            pe.wait_ge(S("vt"), t - 1)
                    else:
                        pe.wait_ge(S("l_n"), 16)
                        if t >= 2:
                            pe.wait_ge(S("kt"), t - 1)
                    b = 4 * (t % 2) + 2 * which
                    for hd in range(DH):
                        last = nc.tensor.transpose(PS[:, b + hd // 4, (hd % 4) * P:(hd % 4 + 1) * P], A[:, (8 if which else 46) + hd, t * P:(t + 1) * P], ident)
                    last.then_inc(S("vk_mm"), 1)
            pe.wait_ge(S("g"), 1)
            pe.wait_ge(S("vt"), NT)
            for c in range(NT):
                last = mm(PS[:, 0, 8 * c:8 * c + 8], C("tri_incl"), dl[1][:, c, :], start=True, stop=True)
            last.then_inc(S("gc_mm"), 1)
            pe.wait_ge(S("kt"), NT)
            pe.wait_ge(S("gc"), 1)

            def heads(bank, lhs, rhs, sets=(0, 1)):
                for hd in range(4 * sets[0], 4 * sets[-1] + 4):
                    last = mm(PS[:, bank + hd // 4, (hd % 4) * P:(hd % 4 + 1) * P], lhs(hd), rhs(hd), start=True, stop=True)
                return last

            def hv(u):
                return lambda hd: A[:, u + hd // 4, (hd % 4) * P:(hd % 4 + 1) * P]

            def identity(hd):
                return ident

            for c in range(NT):
                cols = slice(c * P, (c + 1) * P)

                def qT(hd):
                    return A[:, hd, cols]

                def kT(hd):
                    return A[:, 8 + hd, cols]

                if c:
                    pe.wait_ge(S("d_S"), 2 * c)
                    pe.wait_ge(S("d_o"), 2 * c)
                heads(0, lambda hd: dl[1][:, c, hd:hd + 1].broadcast_to([P, P]), lambda hd: C("tri_incl")).then_inc(S("d_mm"), 1)
                heads(6, lambda hd: dl[0][:, c, hd:hd + 1].broadcast_to([P, P]), identity)
                heads(2, kT, kT).then_inc(S("d_mm"), 1)
                heads(4, kT, qT).then_inc(S("d_mm"), 1)
                pe.wait_ge(S("d_pre"), c + 1)
                for l in range(LEVELS):
                    n = LEVELS * c + l
                    for s in range(2):
                        pe.wait_ge(S(f"d_nl{s}"), n + 1)
                        if l:
                            pe.wait_ge(S(f"d_X{s}"), n)
                        heads(0, hv(48), identity if l == 0 else hv(52), (s,)).then_inc(S(f"d_p{s}"), 1)
                    if l:
                        for s in range(2):
                            pe.wait_ge(S(f"d_p1{s}"), c * (LEVELS - 1) + l)
                            if l < LEVELS - 1:
                                heads(2, hv(50), hv(54), (s,))
                            heads(4, hv(54), hv(50), (s,)).then_inc(S(f"d_dx{s}"), 1)
                if c:
                    for s in range(2):
                        heads(0, kT, hv(56), (s,)).then_inc(S("d_ks"), 1)
                for s in range(2):
                    pe.wait_ge(S(f"d_X{s}"), LEVELS * (c + 1))
                    if c:
                        pe.wait_ge(S("d_R"), 2 * (c - 1) + s + 1)
                    heads(2, hv(50), hv(54) if c else hv(24), (s,)).then_inc(S("d_vn"), 1)
                for s in range(2):
                    pe.wait_ge(S("d_vs"), 2 * c + s + 1)
                    for hd in range(4 * s, 4 * s + 4):
                        o = PS[:, 4 + s, (hd % 4) * P:(hd % 4 + 1) * P]
                        if c:
                            mm(o, hv(56)(hd), qT(hd), start=True, stop=False)
                        last = mm(o, hv(40)(hd), hv(44)(hd), start=not c, stop=True)
                    last.then_inc(S("d_om"), 1)
                    heads(6, hv(32 + 2 * c), hv(40), (s,)).then_inc(S("d_sm"), 1)
            pe.wait_ge(S("d_o"), 2 * NT)
            pe.wait_ge(S("d_S"), 2 * NT)
            for hd in range(DH):
                pe.wait_ge(S("o_sq"), hd + 1)
                mm(PS[:, hd, :], ones, sq[:, hd % 2, :], start=True, stop=True).then_inc(S("o_mm"), 1)
            wait_split(2)
            for m in range(2):
                sgroup(G_AOUT + m, h_split)

            def ffn(layer, g_up, g_dn):
                u0 = UIDX[f"up{layer}_0"]

                for j in range(2):
                    sgroup(g_up + j, h_split)
                with pe.Fori(0, (FU - 3) // 2) as i:
                    for j in range(2):
                        pe.wait_ge(S("ev_dve"), 8 * i + EMPTIED[g_up + j][1])
                        for t in range(4):
                            pe.wait_ge(S("w_lo"), 8 * i + split_count(u0 + 2 + j, t))
                            for k in range(KD):
                                last = product(PS[:, 4 * ((g_up + j) % 2) + t, :], w_split((u0 + j) % 2, k, slice(t * P, (t + 1) * P)), h_split(k), k == 0, k == KD - 1)
                            last.then_inc(S("mm"), 1)
                sgroup(g_up + FU - 1, h_split)
                for m in range(2):
                    g = g_dn + m
                    freed(pe, g - 2)
                    for ui in range(3):
                        u = UIDX[f"down{layer}_{3 * m + ui}"]
                        nk = 8 if ui < 2 else FT - 16
                        for j in range(4):
                            pe.wait_ge(S("w_lo"), split_count(u, j))
                            for k in range(nk):
                                if m == 0 and j == 0:
                                    pe.wait_ge(S("f_lo"), FT * layer + 8 * ui + k + 1)
                                last = product(PS[:, 4 * (g % 2) + j, :], w_split(u % 2, k, slice(j * P, (j + 1) * P)), (hidden_hi(8 * ui + k), hid_r[:, 8 * ui + k, :]),
                                               ui == 0 and k == 0, ui == 2 and k == nk - 1)
                            last.then_inc(S("mm"), 1)

            norm(4, NORM_BANK[4])
            wait_split(3)
            ffn(0, G_UP0, G_DN0)

            norm(5, NORM_BANK[5])
            wait_split(4)
            g = G_KV
            freed(pe, g - 2)
            for j in range(2):
                pe.wait_ge(S("w_lo"), split_count(UIDX["kv"], j))
                for k in range(KD):
                    last = product(PS[:, 4 * (g % 2) + j, :], w_split(unit_slot("kv"), k, slice(j * P, (j + 1) * P)), h_split(k), k == 0, k == KD - 1)
                last.then_inc(S("mm"), 1)
            pe.wait_ge(S("w_lo"), split_count(UIDX["kv"], 3))
            for j in range(2):
                for t in range(2 * j, 2 * j + 2):
                    for k in range(KD):
                        last = product(PS[:, 4 * (g % 2) + 2 + j, 256 * (t % 2):256 * (t % 2) + 256], [v[:, t * P:(t + 1) * P] for v in h_split(k)],
                                       w_split(unit_slot("kv"), k, slice(256, 512)), k == 0, k == KD - 1)
                last.then_inc(S("mm"), 1)
            wait_split(5)
            for m in range(2):
                sgroup(G_WQ + m, hb_split)

            def scores(n):
                b, m = n // 2, n % 2
                if n >= 2:
                    pe.wait_ge(S("at_o"), n - 1)
                k0 = max(b - 1, 0) * P
                for hh in range(8):
                    base = 64 * (hh // 4)
                    last = mm(PS[:, 4 * m + hh // 2, (hh % 2) * 256 + (0 if b else P):(hh % 2) * 256 + 256],
                              A[base:base + HD, 4 * m + hh % 4, b * P:(b + 1) * P], A[base:base + HD, 8 + m, k0:(b + 1) * P], start=True, stop=True)
                last.then_inc(S("at_s"), 1)

            freed(pe, G_WQ)
            freed(pe, G_WQ + 1)
            scores(0)
            scores(1)
            for n in range(2 * NT):
                b, m = n // 2, n % 2
                pe.wait_ge(S("at_pn"), n + 1)
                for hh in range(8):
                    for kk in range(0 if b else 1, 2):
                        i = 2 * hh + kk
                        last = nc.tensor.transpose(PS[:, 4 * m + i // 4, (i % 4) * P:(i % 4 + 1) * P], A[:, 20 + 4 * m + i // 4, (i % 4) * P:(i % 4 + 1) * P], ident)
                last.then_inc(S("at_t"), 1)
                pe.wait_ge(S("at_pt"), n + 1)
                for hh in range(8):
                    kv = 2 * m + hh // 4
                    for kk in range(0 if b else 1, 2):
                        i, t = 2 * hh + kk, b - 1 + kk
                        last = mm(PS[64 * (hh % 2):64 * (hh % 2) + HD, 4 * m, (hh // 2) * P:(hh // 2 + 1) * P],
                                  A[:, 10 + t // 2, 256 * (t % 2) + kv * HD:256 * (t % 2) + (kv + 1) * HD],
                                  A[:, 28 + 4 * m + i // 4, (i % 4) * P:(i % 4 + 1) * P], start=kk == 0 or not b, stop=kk == 1)
                last.then_inc(S("at_pv"), 1)
                if n + 2 < 2 * NT:
                    scores(n + 2)
            wait_split(6)
            for m in range(2):
                sgroup(G_WO + m, h_split)
            norm(6, NORM_BANK[6])
            wait_split(7)
            ffn(1, G_UP1, G_DN1)
            norm(7, NORM_BANK[7])

        @block.scalar
        def _(act):
            a_ = nc.scalar.activation
            chain = [0]

            def link(ins):
                chain[0] += 1
                ins.then_inc(S("act"), 1)
                act.wait_ge(S("act"), chain[0])

            def inv_sqrt(dst, src, e, scale):
                link(a_(dst, src, ACT.Ln, bias=eps[:, e:e + 1], scale=scale))
                return a_(dst, dst, ACT.Exp, scale=-0.5)

            def norm(n):
                for k in range(KD):
                    if n == 0:
                        act.wait_ge(S("x_in"), 16)
                    else:
                        act.wait_ge(S("xt"), KD * (n - 1) + k + 1)
                    if KD * n + k >= 2:
                        act.wait_ge(S("sq_used"), KD * n + k - 1)
                    a_(sq[:, k % 2, :], x[:, k, :], ACT.Square).then_inc(S("sq"), 1)
                act.wait_ge(S("sq_used"), KD * (n + 1))
                bank = NORM_BANK[n]
                inv_sqrt(rstd[:], PS[:, bank, :], 0, 1.0 / D).then_inc(S("std"), 1)

            act.wait_ge(S("small"), 80)
            a_(silc[:], V("c", 0, KD), ACT.Silu).then_inc(S("silc"), 1)
            act.wait_ge(S("eps"), 4)
            norm(0)
            for k in range(KD):
                act.wait_ge(S("h_pre"), k + 1)
                a_(h[:, k, :], h[:, k, :], ACT.Identity, bias=mod[:, k:k + 1]).then_inc(S("h"), 1)
            for k in range(KD):
                act.wait_ge(S("h"), k + 1)
                a_(x_r[:, k, :], h[:, k, :], ACT.Copy).then_inc(S("h_hi"), 1)

            def w_hi_in(p):
                if p < PIECES1:
                    g, j = p // 4, p % 4
                    act.wait_ge(S(f"unit{g % 2}"), 16 * (g // 2 + 1))
                    if p >= 2:
                        act.wait_ge(S("mm"), p - 1)
                    a_(in_hi(p), ring[:, g % 2, :, j * P:(j + 1) * P], ACT.Copy).then_inc(S("w_hi"), 1)

            w_hi_in(0)
            w_hi_in(1)
            act.wait_ge(S("if_ev"), 2)
            a_(gr[2], gr[1], ACT.Abs).then_inc(S("ga"), 1)
            act.wait_ge(S("ga"), 1)
            a_(gr[2], gr[2], ACT.Exp, scale=-1.0).then_inc(S("ga"), 1)
            act.wait_ge(S("ga"), 2)
            a_(gr[2], gr[2], ACT.Ln, bias=eps[0:4, 2:3]).then_inc(S("ga"), 1)

            for g in range(10):
                for j in range(4):
                    w_hi_in(4 * g + j + 2)
                    act.wait_ge(S("mm"), TILE_DONE[g][j])
                    a_(A[:, 4 * g + j, :], PS[:, 4 * (g % 2) + j, :], ACT.Copy if g in (0, 2, 3, 4) else ACT.Sigmoid).then_inc(S("ev_act"), 1)
                if g == 0:
                    act.wait_ge(S("g_rows"), 2)
                    a_(gr[7], gr[7], ACT.Exp).then_inc(S("em"), 1)
            act.wait_ge(S("gT_mm"), 1)
            a_(A[:, 16:20, :], PS[:, 4:8, :], ACT.Copy).then_inc(S("ev_act"), 1)
            for m in range(8):
                act.wait_ge(S("qk_cv"), m + 1)
                a_(A[:, 44 + m, :], A[:, 44 + m, :], ACT.Silu).then_inc(S("qk"), 1)
            for i in range(CT):
                act.wait_ge(S("cl_d"), i + 1)
                a_(A[:, 4 + i, :], A[:, 40 + i, :], ACT.Square).then_inc(S("cl_sq"), 1)
            act.wait_ge(S("cl_mm"), 2)
            inv_sqrt(rstd[:], PS[:, 2, :], 1, 1.0 / DC).then_inc(S("cl_ev"), 1)
            for i in range(CT):
                act.wait_ge(S("cl_n"), i + 1)
                a_(A[:, 40 + i, :], A[:, 40 + i, :], ACT.Silu, bias=V("conv_ln_b", i)).then_inc(S("ya_in"), 1)
            act.wait_ge(S("gT_ev"), 1)
            for hd in range(MH):
                act.wait_ge(S("ml_m"), 2 * hd + 2)
                if hd:
                    act.wait_ge(S("ml_n"), hd)
                for s in range(NT):
                    bias = gT[:, s, hd:hd + 1]
                    w = a_(A[:, 52 + s, s * P:(s + 1) * P], A[:, 1, s * P:(s + 1) * P], ACT.Exp, bias=bias)
                    w.then_inc(S("ml_w"), 1)
                    if s < NT - 1:
                        a_(A[:, 52 + s, (s + 1) * P:T], A[:, 0, (s + 1) * P:T], ACT.Exp, bias=bias).then_inc(S("ml_w"), 1)
                act.wait_ge(S("ml_n"), hd + 1)
                a_(A[:, 2, :], PS[:, 7, :], ACT.Abs).then_inc(S("ml_ad"), 1)
            for hd in range(MH):
                act.wait_ge(S("ml_d"), hd + 1)
                a_(A[:, 12 + hd, :], A[:, 8 + hd, :], ACT.Square).then_inc(S("ml_sq"), 1)
            for hd in range(MH):
                act.wait_ge(S("ml_var"), hd + 1)
                last = a_(A[:, 4 + hd, :], PS[:, 4 + hd, :], ACT.Ln, bias=eps[:, 1:2], scale=1.0 / P)
            link(last)
            for hd in range(MH):
                a_(A[:, 4 + hd, :], A[:, 4 + hd, :], ACT.Exp, scale=-0.5).then_inc(S("ml_std"), 1)
            norm(1)
            for k in range(KD):
                act.wait_ge(S("h_pre"), KD + k + 1)
                a_(h[:, k, :], h[:, k, :], ACT.Identity, bias=mod[:, 24 + k:25 + k]).then_inc(S("h"), 1)

            for t in range(NT):
                act.wait_ge(S("ht_mm"), t + 1)
                a_(A[:, 2 * t:2 * t + 2, :], PS[:, 2 + 2 * (t % 2):4 + 2 * (t % 2), :], ACT.Copy).then_inc(S("ht_ev"), 1)
            act.wait_ge(S("rg"), 1)
            a_(r4[0], r4[0], ACT.Exp).then_inc(S("rexp"), 1)
            act.wait_ge(S("rg"), 2)
            a_(rs[8], rs[8], ACT.Exp).then_inc(S("rexp"), 1)
            n = pairs(act)

            def rows_hi(j, count):
                act.wait_ge(S("m_tr"), count)
                a_(xT_hi[j], PS[:, 0:2, :], ACT.Copy).then_inc(S("m_xh"), 1)

            def hidden_hi_T(j, i):
                act.wait_ge(S("m_tr"), m_turn(i, 2 + j))
                a_(hT_hi[j], PS[:, 0, :], ACT.Copy).then_inc(S("m_xh"), 1)

            def y_out(j, used, scattered):
                act.wait_ge(S("m_pc"), used)
                rwait(act, S(f"sc{j}"), scattered)
                a_(yb[j], PS[:, 6 - 2 * j:8 - 2 * j, :], ACT.Copy).then_inc(S(f"m_y{j}"), 1)

            def silu_gate(j, i):
                act.wait_ge(S("m_pc"), m_used(i, 8 * j + 3))
                a_(hid[j], PS[:, 2 + 2 * j, :], ACT.Silu).then_inc(S("m_sg"), 1)

            rows_hi(0, 1)
            with act.Fori(0, n) as i:
                for p in range(PIECES):
                    j, part, k = piece(p)
                    if k == 0:
                        act.wait_ge(S(f"w{j}{part}"), 16 * i + 16)
                    act.wait_ge(S("m_pc"), m_used(i, p - DEPTH))
                    w, _, hi = m_weights(p)
                    a_(hi, w, ACT.Copy).then_inc(S("m_hi"), 1)
                    if p == 3:
                        y_out(1, m_used(i, PIECES - 1, back=1), 16 * i + 16 * (NT - 1))
                    if p == 7:
                        rows_hi(1, m_turn(i, 1))
                        silu_gate(0, i)
                    if p == 15:
                        silu_gate(1, i)
                    if p == 16:
                        hidden_hi_T(0, i)
                    if p == 21:
                        hidden_hi_T(1, i)
                y_out(0, m_used(i, 19), 16 * i + 16 * NT)
                rows_hi(0, m_turn(i, 4))
            rwait(act, S("m_pc"), m_used(n, PIECES - 1, back=1))
            rwait(act, S("sc1"), 16 * n + 16 * (NT - 1))
            a_(yb[1], PS[:, 4:6, :], ACT.Copy).then_inc(S("m_y1"), 1)
            norm(2)

            def w_hi(u, j, load_count=None, free_count=None, slot=None):
                slot = u % 2 if slot is None else slot
                act.wait_ge(S(f"unit{slot}"), 16 * (u // 2 + 1) if load_count is None else load_count)
                if free_count is not None or u > NU1:
                    act.wait_ge(S("mm"), tile_done(u - 1, j) if free_count is None else free_count)
                a_(w_hi_r[:, :, j * P:(j + 1) * P], ring[:, slot, :, j * P:(j + 1) * P], ACT.Copy).then_inc(S("w_hi"), 1)

            def h_hi(ready, count, src=None, dst=None):
                for k in range(KD):
                    act.wait_ge(S(ready), count - KD + k + 1)
                    a_((h_hi_r if dst is None else dst)[:, k, :], h[:, k, :] if src is None else A[:, src + k, :], ACT.Copy).then_inc(S("h_hi"), 1)

            norm(3)
            for j in range(4):
                w_hi(NU1, j)
            h_hi("h", KD * 3)
            for m in range(24):
                if m == 4:
                    act.wait_ge(S("ab_ev"), 2)
                    a_(dl[0][:], ab[:, :, 0:DH], ACT.Sigmoid).then_inc(S("ab_a"), 1)
                    link(a_(dl[1][:], ab[:, :, DH:2 * DH], ACT.Abs))
                    link(a_(dl[1][:], dl[1][:], ACT.Exp, scale=-1.0))
                    a_(dl[1][:], dl[1][:], ACT.Ln, bias=eps[:, 2:3]).then_inc(S("ab_a"), 1)
                    a_(glast[:], R("a_gate")[:, DH:2 * DH], ACT.Exp).then_inc(S("ab_a"), 1)
                w_hi(NU1 + 1 + m // 4, m % 4)
                act.wait_ge(S("ev_dve"), EMPTIED[G_AIN][1] - 4 + m + 1)
                u = A[:, m if m < 16 else 30 + m, :]
                a_(u, u, ACT.Silu).then_inc(S("a_silu"), 1)
            for g in (6, 7):
                for j in range(4):
                    if g == 6:
                        w_hi(NU1 + 7, j)
                    act.wait_ge(S("mm"), TILE_DONE[G_AIN + g][j])
                    a_(A[:, 16 + 4 * (g - 6) + j, :], PS[:, 4 * ((G_AIN + g) % 2) + j, :], ACT.Silu).then_inc(S("ev_act"), 1)
            act.wait_ge(S("a_silu"), 24)
            for half in range(2):
                for m in range(8 * half, 8 * half + 8):
                    if m >= 2:
                        act.wait_ge(S("l_mm"), m - 1)
                    a_(sq[:, m % 2, :], A[:, m, :], ACT.Square).then_inc(S("l_sq"), 1)
                for m in range(8 * half, 8 * half + 8):
                    act.wait_ge(S("l_mm"), m + 1)
                    a_(A[:, 30 + m, :], PS[:, m % 8, :], ACT.Ln, bias=eps[:, 0:1]).then_inc(S("l_ln"), 1)
            act.wait_ge(S("l_ln"), 16)
            for m in range(16):
                a_(A[:, 30 + m, :], A[:, 30 + m, :], ACT.Exp, scale=-0.5).then_inc(S("l_r"), 1)
            for t in range(NT):
                act.wait_ge(S("vk_mm"), 2 * t + 2)
                b = 4 * (t % 2) + 2
                a_(A[:, 32 + 2 * t:34 + 2 * t, :], PS[:, b:b + 2, :], ACT.Copy).then_inc(S("kt"), 1)
            act.wait_ge(S("gc"), 1)
            a_(dl[3][:], dl[2][:], ACT.Exp).then_inc(S("eg"), 1)
            for c in range(NT):
                act.wait_ge(S("d_mm"), 3 * c + 1)
                a_(A[:, 48:50, :], PS[:, 0:2, :], ACT.Exp).then_inc(S("d_eg"), 1)
                act.wait_ge(S("d_arg"), c + 1)
                a_(A[:, 42:44, :], A[:, 42:44, :], ACT.Exp).then_inc(S("d_et"), 1)
                for l in range(1, LEVELS):
                    for s in range(2):
                        act.wait_ge(S(f"d_p{s}"), LEVELS * c + l + 1)
                        a_(A[:, 54 + s, :], PS[:, s, :], ACT.Copy).then_inc(S(f"d_p1{s}"), 1)
                for s in range(2):
                    act.wait_ge(S("d_vn"), 2 * c + s + 1)
                    a_(A[:, 40 + s, :], PS[:, 2 + s, :], ACT.Copy).then_inc(S("d_vs"), 1)
                for s in range(2):
                    act.wait_ge(S("d_om"), 2 * c + s + 1)
                    a_(h[:, 4 * s:4 * s + 4, c * P:(c + 1) * P], PS[:, 4 + s, :].rearrange("p (a b) -> p a b", b=P), ACT.Copy).then_inc(S("d_o"), 1)
            act.wait_ge(S("d_o"), 2 * NT)
            act.wait_ge(S("d_S"), 2 * NT)
            u = UIDX["a_out0"]
            for j in range(4):
                w_hi(u, j)
            for hd in range(DH):
                if hd >= 2:
                    act.wait_ge(S("o_mm"), hd - 1)
                a_(sq[:, hd % 2, :], h[:, hd, :], ACT.Square).then_inc(S("o_sq"), 1)
            for hd in range(DH):
                act.wait_ge(S("o_mm"), hd + 1)
                last = a_(A[:, 46 + hd, :], PS[:, hd, :], ACT.Ln, bias=eps[:, 0:1], scale=1.0 / P)
            link(last)
            for hd in range(DH):
                a_(A[:, 46 + hd, :], A[:, 46 + hd, :], ACT.Exp, scale=-0.5).then_inc(S("o_r"), 1)
            h_hi("o", DH)
            for m in range(2):
                for j in range(4):
                    w_hi(u + m + 1, j)

            def ffn(layer, g_up):
                ev0 = EMPTIED[g_up][1] - 4
                u0 = UIDX[f"up{layer}_0"]

                def unit(u, par, i):
                    for j in range(4):
                        w_hi(u0 + par + 1, j, 16 * i + 16 * ((u0 + par + 1) // 2 + 1), 8 * i + tile_done(u0 + par, j))
                        if j < 2:
                            act.wait_ge(S("ev_dve"), 4 * u + ev0 + j + 1)
                            t = A[:, 22 + 4 * par + j, :]
                            a_(t, t, ACT.Silu).then_inc(S("f_act"), 1)

                def hidden(tiles):
                    for t in tiles:
                        act.wait_ge(S("f_hid"), FT * layer + t + 1)
                        a_(hidden_hi(t), A[:, t, :], ACT.Copy).then_inc(S("f_hi"), 1)

                with act.Fori(0, FU // 2) as i:
                    for j in range(2):
                        unit(2 * i + j, j, i)
                hidden(range(13))
                unit(FU - 1, 0, FU // 2)
                act.wait_ge(S("mm"), UNIT_USED[f"up{layer}_{FU - 1}"])
                hidden(range(13, FT))
                for u in range(6):
                    for j in range(4):
                        if UIDX[f"down{layer}_{u}"] + 1 < NU:
                            w_hi(UIDX[f"down{layer}_{u}"] + 1, j)

            norm(4)
            h_hi("h", KD * 4)
            ffn(0, G_UP0)
            norm(5)
            h_hi("h", KD * 5)
            h_hi("hb", KD, 46, hb_hi_r)
            for u in (UIDX["w_q0"], UIDX["w_q1"]):
                for j in range(4):
                    w_hi(u, j)

            def exps(n):
                b, m = n // 2, n % 2
                act.wait_ge(S("at_m"), 2 * n + 2)
                link(a_(sm[2][:, m, :], sm[2][:, m, :], ACT.Exp))
                for hh in range(8):
                    p = A[:, 20 + 4 * m + hh // 2, (hh % 2) * 256 + (0 if b else P):(hh % 2) * 256 + 256]
                    last = a_(p, p, ACT.Exp, bias=sm[0][:, m, hh:hh + 1], accum_out=sm[1][:, m, hh:hh + 1])
                last.then_inc(S("at_p"), 1)

            exps(0)
            for n in range(2 * NT):
                b, m = n // 2, n % 2
                act.wait_ge(S("at_t"), n + 1)
                if n >= 2:
                    act.wait_ge(S("at_pv"), n - 1)
                src, dst = PS[:, 4 * m:4 * m + 4, :], A[:, 28 + 4 * m:32 + 4 * m, :]
                if not b:
                    src, dst = (v.rearrange("p a (b c d) -> p (a b) c d", c=2, d=P)[:, :, 1, :] for v in (src, dst))
                a_(dst, src, ACT.Copy).then_inc(S("at_pt"), 1)
                if n + 1 < 2 * NT:
                    exps(n + 1)
            act.wait_ge(S("at_pv"), 2 * NT)
            for j in range(4):
                w_hi(UIDX["w_o0"], j)
            act.wait_ge(S("at_o"), 2 * NT)
            h_hi("at_o", 2 * NT)
            for m in range(2):
                for j in range(4):
                    w_hi(UIDX["w_o1"] + m, j)
            norm(6)
            h_hi("h", KD * 6)
            ffn(1, G_UP1)
            norm(7)

        @block.vector
        def _(dve):
            chain = [0]
            ts, tt, stt, cp = nc.vector.tensor_scalar, nc.vector.tensor_tensor, nc.vector.scalar_tensor_tensor, nc.vector.tensor_copy

            def link(ins):
                chain[0] += 1
                ins.then_inc(S("dve"), 1)
                dve.wait_ge(S("dve"), chain[0])

            for i, e in enumerate((1e-6, 1e-5, 1.0, 0.0)):
                nc.vector.memset(eps[:, i:i + 1], e).then_inc(S("eps"), 1)
            dve.wait_ge(S("x_in"), 16)
            dve.wait_ge(S("silc"), 1)

            STEPS = 4
            steps, pieces, pieces_to = [0], [0], [0]

            def w_lo_in(upto):
                while pieces[0] < upto:
                    p = pieces[0]
                    pieces[0] += 1
                    cols = slice((p % 4) * P, (p % 4 + 1) * P)
                    dve.wait_ge(S("w_hi"), p + 1)
                    tt(ring_r[:, p // 4 % 2, :, cols], ring[:, p // 4 % 2, :, cols], in_hi(p).bitcast(F32), ALU.subtract).then_inc(S("w_lo"), 1)

            def step():
                steps[0] += 1
                if steps[0] % STEPS == 0:
                    w_lo_in(min(pieces[0] + 1, pieces_to[0]))

            def ada_acc(a):
                dve.wait_ge(S(ada_sem(a)), 16 * (1 if a < 4 else a // 2))
                w = ada_place(a)
                acc = ada_sums(a)
                link(ts(acc, w[:, 0, :], silc[:, 0:1], None, ALU.mult))
                for k in range(1, KD):
                    ins = stt(acc, w[:, k, :], silc[:, k:k + 1], acc, ALU.mult, ALU.add)
                    if k < KD - 1:
                        link(ins)
                        step()
                ins.then_inc(S("ada_used"), 1)

            def mod_ev(n, bank):
                dve.wait_ge(S("ada_sum"), 4 * n + 4)
                tt(mod[:, 16 * n:16 * n + 16], PS[:, bank, 16 * n:16 * n + 16], V("b_ada", 16 * n, 16), ALU.add).then_inc(S("mod_ev"), 1)

            def gain(layer, gname, sc):
                link(ts(gm[:, layer, :], mod[:, sc:sc + KD], 1.0, None, ALU.add))
                link(tt(gm[:, layer, :], gm[:, layer, :], V(gname, 0, KD), ALU.mult))

            def norm(n, g, dst, done):
                dve.wait_ge(S("std"), n + 1)
                for k in range(KD):
                    stt(dst[:, k, :], x[:, k, :], g[:, k:k + 1], rstd[:], ALU.mult, ALU.mult).then_inc(S(done), 1)

            for a in range(4):
                ada_acc(a)
            dve.wait_ge(S("small2"), 48)
            link(cp(wif_hi, wif[:]))
            link(tt(wif_lo, wif[:], wif_hi.bitcast(F32), ALU.subtract))
            mod_ev(0, 1)
            dve.wait_ge(S("mod_ev"), 1)
            gain(0, "g_norm1", 8)
            norm(0, gm[:, 0, :], h, "h_pre")
            for k in range(KD):
                dve.wait_ge(S("h_hi"), k + 1)
                tt(h_r[:, k, :], h[:, k, :], x_r[:, k, :].bitcast(F32), ALU.subtract).then_inc(S("h_lo"), 1)
            w_lo_in(2)
            ada_acc(4)
            dve.wait_ge(S("if_mm"), 1)
            ts(gr[0], PS[0:4, 4, :], bif[0:4], None, ALU.add).then_inc(S("if_ev"), 1)
            ts(gr[1], PS[32:36, 4, :], bif[32:36], None, ALU.add).then_inc(S("if_ev"), 1)
            dve.wait_ge(S("if_ev"), 2)
            link(nc.vector.memset(gr[4], 1.0))
            link(ts(gr[6], gr[1], 0.0, None, ALU.min))
            dve.wait_ge(S("ga"), 3)
            link(tt(gr[2], gr[6], gr[2], ALU.subtract))
            link(nc.vector.tensor_tensor_scan(gr[3], gr[4], gr[2], 0.0, ALU.mult, ALU.add))
            tt(gr[5], gr[0], gr[3], ALU.subtract).then_inc(S("g_rows"), 1)
            dve.wait_ge(S("g_rows"), 1)
            link(nc.vector.tensor_tensor_scan(gr[6], gr[5], gr[5], 0.0, ALU.max, ALU.max))
            link(ts(gr[6], gr[6], -1.0, None, ALU.mult))
            tt(gr[7], gr[6], gr[3], ALU.subtract).then_inc(S("g_rows"), 1)

            pieces_to[0] = 12
            for a in range(5, 12):
                ada_acc(a)
            w_lo_in(8)
            mod_ev(1, 3)
            pieces_to[0] = 16
            for i in range(CT):
                dve.wait_ge(S("ev_act"), 4 + i + 1)
                link(tt(A[:, i, :], A[:, i, :], A[:, 4 + i, :], ALU.mult))

            def conv(dst, src, taps, w, b):
                if b is None:
                    link(ts(dst, src, w(taps - 1), None, ALU.mult))
                else:
                    link(ts(dst, src, w(taps - 1), b, ALU.mult, ALU.add))
                for j in range(taps - 2, -1, -1):
                    s = taps - 1 - j
                    ins = stt(dst[:, s:T], src[:, 0:T - s], w(j), dst[:, s:T], ALU.mult, ALU.add)
                    if j:
                        link(ins)
                        step()
                return ins

            def conv_u(i):
                conv(A[:, 40 + i, :], A[:, i, :], TAPS, lambda j: V("conv_dw_w", CT * j + i), V("conv_dw_b", i)).then_inc(S("cv"), 1)

            def conv_qk(m):
                dve.wait_ge(S("ev_act"), 8 + m + 1)
                conv(A[:, 44 + m, :], A[:, 8 + m, :], QTAPS, lambda j: V("qk_conv_w", 8 * j + m), V("qk_conv_b", m)).then_inc(S("qk_cv"), 1)

            for i in range(CT):
                conv_u(i)
                if i == 0:
                    w_lo_in(12)
                    mod_ev(2, 7)
                    pieces_to[0] = PIECES1
            for m in range(8):
                w_lo_in(9 + m)
                conv_qk(m)
            w_lo_in(PIECES1)
            dve.wait_ge(S("cl_mm"), 1)
            dve.wait_ge(S("cv"), CT)
            for i in range(CT):
                stt(A[:, 40 + i, :], PS[:, 0, :], -1.0 / DC, A[:, 40 + i, :], ALU.mult, ALU.add).then_inc(S("cl_d"), 1)
            dve.wait_ge(S("mod_ev"), 3)
            gain(1, "g_norm2", 32)
            dve.wait_ge(S("cl_ev"), 1)
            dve.wait_ge(S("cl_d"), CT)
            for i in range(CT):
                stt(A[:, 40 + i, :], A[:, 40 + i, :], V("conv_ln_g", i), rstd[:], ALU.mult, ALU.mult).then_inc(S("cl_n"), 1)
            dve.wait_ge(S("gT_mm"), 2)
            cp(gT[:], PS[:, 3, 0:16].rearrange("p (a b) -> p a b", b=MH)).then_inc(S("gT_ev"), 1)
            for hd in range(MH):
                dve.wait_ge(S("ml_s"), hd + 1)
                cp(A[:, 0, :], PS[:, 4, :]).then_inc(S("ml_m"), 1)
                tt(A[:, 1, :].rearrange("p (a b) -> p a b", b=P), PS[:, 4, :].rearrange("p (a b) -> p a b", b=P),
                   C("after").rearrange("p (a b) -> p a b", a=1).broadcast_to([P, NT, P]), ALU.add).then_inc(S("ml_m"), 1)
                for s in range(NT):
                    dve.wait_ge(S("ml_w"), 7 * hd + min(2 * s + 2, 7))
                    stt(A[:, 52 + s, s * P:T], PS[:, s, 0:T - s * P], float(P) ** -0.5, A[:, 52 + s, s * P:T], ALU.mult, ALU.mult).then_inc(S("ml_p"), 1)
                dve.wait_ge(S("ml_ad"), hd + 1)
                link(tt(A[:, 2, :], A[:, 2, :], PS[:, 5, :], ALU.max))
                link(nc.vector.reciprocal(A[:, 3, :], A[:, 2, :]))
                tt(A[:, 8 + hd, :], PS[:, 6, :], A[:, 3, :], ALU.mult).then_inc(S("ml_h"), 1)
            dve.wait_ge(S("ml_h"), MH)
            for hd in range(MH):
                dve.wait_ge(S("ml_mu"), hd + 1)
                stt(A[:, 8 + hd, :], PS[:, hd, :], -1.0 / P, A[:, 8 + hd, :], ALU.mult, ALU.add).then_inc(S("ml_d"), 1)
            for hd in range(MH):
                dve.wait_ge(S("ml_std"), hd + 1)
                link(stt(A[:, 8 + hd, :], A[:, 8 + hd, :], V("m_norm_g", hd), A[:, 4 + hd, :], ALU.mult, ALU.mult))
                tt(A[:, 8 + hd, :], A[:, 8 + hd, :], A[:, 20 + hd, :], ALU.mult).then_inc(S("hm"), 1)
            for m in range(2):
                for j in range(4):
                    dve.wait_ge(S("mm"), TILE_DONE[G_CONV + m][j])
                    b = 4 * ((G_CONV + m) % 2) + j
                    tt(A[:, 24 + 4 * m + j, :], A[:, 24 + 4 * m + j, :], PS[:, b, :], ALU.mult).then_inc(S("ev_dve"), 1)
            for m in range(2):
                for j in range(4):
                    dve.wait_ge(S("mm"), TILE_DONE[G_MOUT + m][j])
                    b = 4 * ((G_MOUT + m) % 2) + j
                    tt(A[:, 32 + 4 * m + j, :], A[:, 32 + 4 * m + j, :], PS[:, b, :], ALU.mult).then_inc(S("ev_dve"), 1)
                    dve.wait_ge(S("ev_dve"), 8 + 4 * m + j + 1)
                    tt(A[:, 24 + 4 * m + j, :], A[:, 24 + 4 * m + j, :], A[:, 32 + 4 * m + j, :], ALU.add).then_inc(S("merged"), 1)

            def residual(g, n_of, scale_of=None, bias_of=None, next_unit=NU):
                for j in range(4):
                    if next_unit < NU:
                        w_lo(next_unit, j)
                    k = 4 * n_of + j
                    dve.wait_ge(S("mm"), TILE_DONE[g][j])
                    src = PS[:, 4 * (g % 2) + j, :]
                    if scale_of is not None:
                        ins = stt(x[:, k, :], src, scale_of(k), x[:, k, :], ALU.mult, ALU.add)
                    elif bias_of is not None:
                        ins = stt(x[:, k, :], src, bias_of(k), x[:, k, :], ALU.add, ALU.add)
                    else:
                        ins = tt(x[:, k, :], src, x[:, k, :], ALU.add)
                    ins.then_inc(S("xt"), 1)

            dve.wait_ge(S("x_in"), 32)
            for m in range(2):
                residual(G_WOUT + m, m, scale_of=lambda k: mod[:, 16 + k:17 + k])
            norm(1, gm[:, 1, :], h, "h_pre")
            X3 = [P, NT, EPG]

            def b3(v, w):
                return v.rearrange("p (a b) -> p a b", b=1).broadcast_to([P, NT, w])

            def bnum(name, w):
                return C(name).rearrange("p (a b) -> p a b", a=1).broadcast_to([P, NT, w])

            def first_of(dst, vals, mx, num, w, t1):
                link(nc.vector.tensor_reduce(mx, vals, AX, ALU.max))
                link(tt(t1, vals, b3(mx, w), ALU.is_lt))
                link(stt(t1, t1, 1000.0, bnum(num, w), ALU.mult, ALU.add))
                link(nc.vector.tensor_reduce(rs[13], t1, AX, ALU.min))
                link(tt(dst, bnum(num, w), b3(rs[13], w), ALU.is_equal))

            dve.wait_ge(S("logits"), 1)
            link(tt(lg, PS[:, 0, 0:256].rearrange("p (a b) -> p a b", b=64)[:, :, 0:NG + E],
                    R("b_router").rearrange("p (a b) -> p a b", a=1).broadcast_to([P, NT, NG + E]), ALU.add))
            first_of(r4[1], lg[:, :, 0:NG], rs[0], "iota4", NG, r4[2])
            tt(r4[0], lg[:, :, 0:NG], b3(rs[0], NG), ALU.subtract).then_inc(S("rg"), 1)
            dve.wait_ge(S("rexp"), 1)
            link(nc.vector.tensor_reduce(rs[1], r4[0], AX, ALU.add))
            link(nc.vector.reciprocal(rs[2], rs[1]))
            for g in range(NG):
                le = lg[:, :, NG + g * EPG:NG + (g + 1) * EPG]
                og = r4[1][:, :, g:g + 1].broadcast_to(X3)
                if g == 0:
                    link(tt(r8[0], le, og, ALU.mult))
                else:
                    link(tt(r8[1], le, og, ALU.mult))
                    link(tt(r8[0], r8[0], r8[1], ALU.add))
            first_of(r8[2], r8[0], rs[3], "iota8", EPG, r8[1])
            link(stt(r8[3], r8[2], NEG, r8[0], ALU.mult, ALU.add))
            first_of(r8[4], r8[3], rs[4], "iota8", EPG, r8[1])
            tt(rs[8], rs[4], rs[3], ALU.subtract).then_inc(S("rg"), 1)
            dve.wait_ge(S("rexp"), 2)
            link(ts(rs[5], rs[8], 1.0, None, ALU.add))
            link(nc.vector.reciprocal(rs[6], rs[5]))
            link(tt(wtok[:, 0, :], rs[6], rs[2], ALU.mult))
            link(tt(wtok[:, 1, :], wtok[:, 0, :], rs[8], ALU.mult))
            for c in range(2):
                for g in range(NG):
                    link(tt(asg[c][:, :, g * EPG:(g + 1) * EPG], r8[2 + 2 * c], r4[1][:, :, g:g + 1].broadcast_to(X3), ALU.mult))
            tt(asg[2], asg[0], asg[1], ALU.add).then_inc(S("asg"), 1)
            dve.wait_ge(S("rank"), 1)
            link(cp(er[0], PS[:, 7, 0:E]))
            link(ts(er[1], er[0], 0.0, None, ALU.is_gt))
            for m in range(1, NT):
                link(ts(er[2], er[0], float(m * P), None, ALU.is_gt))
                link(tt(er[1], er[1], er[2], ALU.add))
            link(nc.vector.memset(er[3], 1.0))
            link(nc.vector.tensor_tensor_scan(er[4], er[3], er[1], 0.0, ALU.mult, ALU.add))
            link(tt(er[5], er[4], er[1], ALU.subtract))
            link(ts(er[5], er[5], float(P), None, ALU.mult))
            link(tt(asg[3], PS[:, 6, 0:NT * E].rearrange("p (a b) -> p a b", b=E), er[5].rearrange("p (a b) -> p a b", a=1).broadcast_to([P, NT, E]), ALU.add))
            for c in range(2):
                link(tt(asg[4], asg[3], asg[c], ALU.mult))
                link(nc.vector.tensor_reduce(rs[9 + c], asg[4], AX, ALU.add))
                cp(posi[:, c, :], rs[9 + c]).then_inc(S("posi"), 1)
            pend = er[4][0:1, :].rearrange("p (a b) -> p a b", a=1).broadcast_to([1, NB, E])
            link(tt(blk[0:1], pend, C("iotab")[0:1, :].rearrange("p (a b) -> p a b", b=1).broadcast_to([1, NB, E]), ALU.is_le))
            link(nc.vector.tensor_reduce(blkf[0:1, 0:NB], blk[0:1], AX, ALU.add))
            link(ts(blkf[0:1, 0:NB], blkf[0:1, 0:NB], float(E - 1), None, ALU.min))
            link(ts(blkf[0:1, NB:NB + 1], er[4][0:1, E - 1:E], 0.5, 0.25, ALU.mult, ALU.add))
            link(cp(blki[0:1, 0:NB], blkf[0:1, 0:NB]))
            cp(blki[0:1, NB:NB + 1], blkf[0:1, NB:NB + 1]).then_inc(S("blocks"), 1)
            nc.vector.memset(dl[5][:], 0.0).then_inc(S("m_y0"), 1)
            nc.vector.memset(dl[4][:], 0.0).then_inc(S("m_pc"), DEPTH)
            n = pairs(dve)

            def rows_lo(j, count):
                dve.wait_ge(S("m_xh"), count)
                tt(xT_lo[j], PS[:, 0:2, :], xT_hi[j].bitcast(F32), ALU.subtract).then_inc(S("m_xl"), 1)

            def hidden_lo_T(j, i):
                dve.wait_ge(S("m_xh"), m_turn(i, 2 + j))
                tt(hT_lo[j], PS[:, 0, :], hT_hi[j].bitcast(F32), ALU.subtract).then_inc(S("m_xl"), 1)

            def hidden_rows(j, i):
                dve.wait_ge(S("m_sg"), 2 * i + j + 1)
                dve.wait_ge(S("m_pc"), m_used(i, 8 * j + 7))
                tt(hid[j], hid[j], PS[:, 3 + 2 * j, :], ALU.mult).then_inc(S("m_h"), 1)

            rows_lo(0, 1)
            with dve.Fori(0, n) as i:
                for p in range(PIECES):
                    dve.wait_ge(S("m_hi"), PIECES * i + p + 1)
                    w, lo, hi = m_weights(p)
                    tt(lo, w, hi.bitcast(F32), ALU.subtract).then_inc(S("m_lo"), 1)
                    if p == 7:
                        rows_lo(1, m_turn(i, 1))
                    if p == 10:
                        hidden_rows(0, i)
                    if p == 16:
                        hidden_lo_T(0, i)
                    if p == 18:
                        hidden_rows(1, i)
                    if p == 21:
                        hidden_lo_T(1, i)
                rows_lo(0, m_turn(i, 4))
            dve.wait_ge(S("y2"), 16 * NT)
            for t in range(NT):
                y2 = A[:, 4 * t:4 * t + 4, :].rearrange("p a b -> p (a b)")
                yy = A[:, 16 + 2 * t:18 + 2 * t, :].rearrange("p a b -> p (a b)")
                link(ts(yy, y2[:, D:2 * D], wtok[:, 1, t:t + 1], None, ALU.mult))
                stt(yy, y2[:, 0:D], wtok[:, 0, t:t + 1], yy, ALU.mult, ALU.add).then_inc(S("y_sum"), 1)
            for k in range(KD):
                dve.wait_ge(S("yT"), k + 1)
                stt(x[:, k, :], PS[:, k, :], mod[:, 40 + k:41 + k], x[:, k, :], ALU.mult, ALU.add).then_inc(S("xt"), 1)
            norm(2, V("g_final", 0, KD), x, "xt")

            def w_lo(u, j, count=None, slot=None):
                slot = u % 2 if slot is None else slot
                dve.wait_ge(S("w_hi"), split_count(u, j) if count is None else count)
                cols = slice(j * P, (j + 1) * P)
                tt(ring_r[:, slot, :, cols], ring[:, slot, :, cols], w_hi_r[:, :, cols].bitcast(F32), ALU.subtract).then_inc(S("w_lo"), 1)

            h_sets = [1]

            def h_lo(src=None):
                for k in range(KD):
                    dve.wait_ge(S("h_hi"), KD * h_sets[0] + k + 1)
                    v, r, top = (h[:, k, :], h_r[:, k, :], h_hi_r[:, k, :]) if src is None else (A[:, src + k, :], top_r[:, k, :], hb_hi_r[:, k, :])
                    tt(r, v, top.bitcast(F32), ALU.subtract).then_inc(S("h_lo"), 1)
                h_sets[0] += 1

            dve.wait_ge(S("small3"), 32)
            link(cp(wab_hi, wab[:]))
            link(tt(wab_lo, wab[:], wab_hi.bitcast(F32), ALU.subtract))
            norm(3, V("a_norm", 0, KD), h, "h")
            for j in range(4):
                w_lo(NU1, j)
            h_lo()
            dve.wait_ge(S("ab_mm"), 1)
            cp(ab_rows, PS[0:2 * DH, 4, :]).then_inc(S("ab_ev"), 1)
            for m in range(24):
                g = G_AIN + m // 4
                if m == 4:
                    dve.wait_ge(S("ab_mm"), 2)
                    pab = PS[:, 7, 0:64].rearrange("p (a b) -> p a b", b=16)
                    link(cp(ab[:, :, 0:DH], pab[:, :, 0:DH]))
                    tt(ab[:, :, DH:2 * DH], pab[:, :, DH:2 * DH], R("a_gate")[:, 0:DH].rearrange("p (a b) -> p a b", a=1).broadcast_to([P, NT, DH]),
                       ALU.add).then_inc(S("ab_ev"), 1)
                if m == 8:
                    dve.wait_ge(S("ab_ev"), 2)
                    link(ts(dl[5][:], ab[:, :, DH:2 * DH], 0.0, None, ALU.max))
                    dve.wait_ge(S("ab_a"), 3)
                    link(tt(dl[1][:], dl[1][:], dl[5][:], ALU.add))
                    stt(dl[1][:], dl[1][:], -1.0, glast[:].rearrange("p (a b) -> p a b", a=1).broadcast_to([P, NT, DH]), ALU.mult, ALU.mult).then_inc(S("g"), 1)
                w_lo(NU1 + 1 + m // 4, m % 4)
                dve.wait_ge(S("mm"), TILE_DONE[g][m % 4])
                dst = A[:, m if m < 16 else 30 + m, :]
                src = PS[:, 4 * (g % 2) + m % 4, :]
                conv(dst, src, 4, lambda j: V("a_conv_w", 24 * j + m), None).then_inc(S("ev_dve"), 1)
            for j in range(4):
                w_lo(NU1 + 7, j)
            for m in range(16):
                dve.wait_ge(S("l_r"), m + 1)
                r = A[:, 30 + m, :]
                if m < 8:
                    stt(A[:, m, :], A[:, m, :], float(P) ** -0.5, r, ALU.mult, ALU.mult).then_inc(S("l_n"), 1)
                else:
                    tt(A[:, m, :], A[:, m, :], r, ALU.mult).then_inc(S("l_n"), 1)

            def per_head(v, n=DH):
                return v.rearrange("p (a b) -> p a b", b=1).broadcast_to([P, n, P])

            def h3(v):
                return v.rearrange("p a (b c) -> p (a b) c", c=P)

            def m4(v):
                return v.rearrange("p (a b) -> p a b", b=P)

            for t in range(NT):
                dve.wait_ge(S("vk_mm"), 2 * t + 1)
                b = 4 * (t % 2)
                v_t = A[:, 24 + 2 * t:26 + 2 * t, :].rearrange("p a (b c) -> p (a b) c", c=P)
                tt(v_t, h3(PS[:, b:b + 2, :]), per_head(dl[0][:, t, :]), ALU.mult).then_inc(S("vt"), 1)
            dve.wait_ge(S("gc_mm"), 1)
            cp(dl[2][:], PS[:, 0, 0:32].rearrange("p (a b) -> p a b", b=DH)).then_inc(S("gc"), 1)
            dve.wait_ge(S("eg"), 1)
            link(stt(dl[4][:], dl[0][:], -1.0, dl[3][:], ALU.mult, ALU.mult))
            identb = ident.rearrange("p (a b) -> p a b", a=1).broadcast_to([P, 4, P])
            for c in range(NT):
                cols = slice(c * P, (c + 1) * P)
                dve.wait_ge(S("d_eg"), c + 1)
                for hd in range(DH):
                    part = slice((hd % 4) * P, (hd % 4 + 1) * P)
                    last = stt(A[:, 42 + hd // 4, part], PS[:, hd // 4, part], dl[2][:, c, hd:hd + 1], C("after"), ALU.subtract, ALU.add)
                last.then_inc(S("d_arg"), 1)
                link(cp(glast[:], h3(A[:, 48:50, :])[:, :, P - 1]))
                dve.wait_ge(S("d_mm"), 3 * c + 3)
                link(tt(A[:, 0:8, cols], A[:, 0:8, cols], h3(A[:, 48:50, :]), ALU.mult))
                dve.wait_ge(S("d_et"), c + 1)
                link(tt(A[:, 44:46, :], PS[:, 4:6, :], A[:, 42:44, :], ALU.mult))
                link(tt(A[:, 46:48, :], PS[:, 2:4, :], A[:, 42:44, :], ALU.mult))
                link(tt(A[:, 46:48, :], A[:, 46:48, :], PS[:, 6:8, :], ALU.mult))
                kd = h3(A[:, 32 + 2 * c:34 + 2 * c, :])
                tt(kd, kd, h3(A[:, 42:44, :])[:, :, P - 1:P].broadcast_to([P, DH, P]), ALU.mult).then_inc(S("d_pre"), 1)

                def nl(l, s):
                    tt(m4(A[:, 48 + s, :]), m4(A[:, 46 + s, :]), levels[:, l:l + 1, :].broadcast_to([P, 4, P]), ALU.mult).then_inc(S(f"d_nl{s}"), 1)

                for s in range(2):
                    nl(0, s)
                for l in range(LEVELS):
                    n = LEVELS * c + l
                    if l == 0:
                        for s in range(2):
                            dve.wait_ge(S(f"d_nl{s}"), n + 1)
                            link(tt(m4(A[:, 50 + s, :]), m4(A[:, 48 + s, :]), identb, ALU.add))
                            dve.wait_ge(S(f"d_p{s}"), n + 1)
                            tt(m4(A[:, 52 + s, :]), m4(PS[:, s, :]), identb, ALU.add).then_inc(S(f"d_X{s}"), 1)
                            nl(1, s)
                        continue
                    if l + 1 < LEVELS:
                        for s in range(2):
                            dve.wait_ge(S(f"d_p{s}"), n + 1)
                            nl(l + 1, s)
                    for s in range(2):
                        dve.wait_ge(S(f"d_dx{s}"), c * (LEVELS - 1) + l)
                        if l < LEVELS - 1:
                            link(tt(A[:, 52 + s, :], A[:, 52 + s, :], PS[:, 2 + s, :], ALU.add))
                        tt(A[:, 50 + s, :], A[:, 50 + s, :], PS[:, 4 + s, :], ALU.add).then_inc(S(f"d_X{s}"), 1)
                if c:
                    for s in range(2):
                        dve.wait_ge(S("d_ks"), 2 * (c - 1) + s + 1)
                        link(tt(m4(A[:, 54 + s, :]), m4(PS[:, s, :]), per_head(dl[4][:, c, 4 * s:4 * s + 4], 4), ALU.mult))
                        tt(A[:, 54 + s, :], A[:, 54 + s, :], A[:, 24 + 2 * c + s, :], ALU.add).then_inc(S("d_R"), 1)
                for s in range(2):
                    dve.wait_ge(S("d_sm"), 2 * c + s + 1)
                    if c:
                        link(tt(m4(A[:, 56 + s, :]), m4(A[:, 56 + s, :]), per_head(glast[:, 4 * s:4 * s + 4], 4), ALU.mult))
                        tt(A[:, 56 + s, :], A[:, 56 + s, :], PS[:, 6 + s, :], ALU.add).then_inc(S("d_S"), 1)
                    else:
                        cp(A[:, 56 + s, :], PS[:, 6 + s, :]).then_inc(S("d_S"), 1)
            for j in range(4):
                w_lo(UIDX["a_out0"], j)
            for hd in range(DH):
                dve.wait_ge(S("o_r"), hd + 1)
                link(stt(h[:, hd, :], h[:, hd, :], V("a_onorm"), A[:, 46 + hd, :], ALU.mult, ALU.mult))
                tt(h[:, hd, :], h[:, hd, :], A[:, 16 + hd, :], ALU.mult).then_inc(S("o"), 1)
            h_lo()
            for m in range(2):
                residual(G_AOUT + m, m, next_unit=UIDX["a_out0"] + m + 1)

            def ffn(layer, g_up, g_dn):
                ev0 = EMPTIED[g_up][1] - 4
                mm0 = TILE_DONE[g_up][0]
                LINKS = 8
                u0 = UIDX[f"up{layer}_0"]

                def unit(u, par, i):
                    done = [0]

                    def flink(ins):
                        done[0] += 1
                        ins.then_inc(S("dve_f"), 1)
                        dve.wait_ge(S("dve_f"), LINKS * u + (LINKS * FU * layer + done[0]))

                    for j in range(4):
                        w_lo(u0 + par + 1, j, 8 * i + split_count(u0 + par + 1, j))
                        dve.wait_ge(S("mm"), 4 * u + (mm0 + j))
                        t = A[:, 22 + 4 * par + j, :]
                        src = PS[:, 4 * ((g_up + par) % 2) + j, :]
                        tile = (j % 2) + (FT if j >= 2 else 0)

                        def col(name, base):
                            return vec[:, bass.ds(2 * u + (VOFF[name] + base + tile), 1)]

                        flink(ts(t, src, col("f_conv_w", (3 * layer + 2) * 2 * FT), col("f_conv_b", 2 * FT * layer), ALU.mult, ALU.add))
                        flink(stt(t[:, 1:T], src[:, 0:T - 1], col("f_conv_w", (3 * layer + 1) * 2 * FT), t[:, 1:T], ALU.mult, ALU.add))
                        stt(t[:, 2:T], src[:, 0:T - 2], col("f_conv_w", 3 * layer * 2 * FT), t[:, 2:T], ALU.mult, ALU.add).then_inc(S("ev_dve"), 1)
                    assert done[0] == LINKS
                    dve.wait_ge(S("ev_dve"), 4 * u + (ev0 + 4))
                    for j in range(2):
                        dve.wait_ge(S("f_act"), 2 * u + (FT * layer + j + 1))
                        tt(A[:, bass.ds(2 * u + j, 1), :].rearrange("p a b -> p (a b)"), A[:, 22 + 4 * par + j, :], A[:, 24 + 4 * par + j, :],
                           ALU.mult).then_inc(S("f_hid"), 1)

                def hidden(tiles):
                    for t in tiles:
                        dve.wait_ge(S("f_hi"), FT * layer + t + 1)
                        tt(hid_r[:, t, :], A[:, t, :], hidden_hi(t).bitcast(F32), ALU.subtract).then_inc(S("f_lo"), 1)

                with dve.Fori(0, FU // 2) as i:
                    for j in range(2):
                        unit(2 * i + j, j, i)
                hidden(range(13))
                unit(FU - 1, 0, FU // 2)
                hidden(range(13, FT))
                for m in range(2):
                    u = UIDX[f"down{layer}_{3 * m}"]
                    for j in range(8):
                        w_lo(u + 1 + j // 4, j % 4)
                    residual(g_dn + m, m, next_unit=u + 3)


            norm(4, V("f_norm", 0, KD), h, "h")
            h_lo()
            ffn(0, G_UP0, G_DN0)

            norm(5, V("kv_norm", 0, KD), h, "h")
            h_lo()
            for k in range(KD):
                stt(A[:, 46 + k, :], x[:, k, :], V("b_norm", k), rstd[:], ALU.mult, ALU.mult).then_inc(S("hb"), 1)
            h_lo(46)
            for j in range(4):
                if j < 2:
                    w_lo(UIDX["w_q0"], j)
                dve.wait_ge(S("mm"), TILE_DONE[G_KV][j])
                src = PS[:, 4 * (G_KV % 2) + j, :]
                if j < 2:
                    ts(A[:, 8 + j, :], src, V("kv_b", j), None, ALU.add).then_inc(S("ev_dve"), 1)
                else:
                    tt(A[:, 8 + j, :].rearrange("p (a b) -> p a b", b=256), src.rearrange("p (a b) -> p a b", b=256),
                       R("kv_b_v").rearrange("p (a b) -> p a b", a=1).broadcast_to([P, 2, 256]), ALU.add).then_inc(S("ev_dve"), 1)
            for j in (2, 3):
                w_lo(UIDX["w_q0"], j)
            for m in range(2):
                for j in range(4):
                    if m == 0:
                        w_lo(UIDX["w_q1"], j)
                    dve.wait_ge(S("mm"), TILE_DONE[G_WQ + m][j])
                    ts(A[:, 4 * m + j, :], PS[:, 4 * ((G_WQ + m) % 2) + j, :], V("b_b_q", 4 * m + j), float(HD) ** -0.5, ALU.add, ALU.mult).then_inc(S("ev_dve"), 1)

            def ph(m, b):
                v = A[:, 20 + 4 * m:24 + 4 * m, :].rearrange("p a (b c) -> p (a b) c", c=256)
                return v if b else v[:, :, P:256]

            def maxima(n):
                b, m = n // 2, n % 2
                dve.wait_ge(S("at_s"), n + 1)
                if n >= 2:
                    dve.wait_ge(S("at_t"), n - 1)
                src = PS[:, 4 * m:4 * m + 4, :].rearrange("p a (b c) -> p (a b) c", c=256)
                bias = A[:, 12 + 4 * m:16 + 4 * m, :].rearrange("p a (b c) -> p (a b) c", c=256)
                if not b:
                    src, bias = src[:, :, P:256], bias[:, :, P:256]
                link(tt(ph(m, b), src, bias, ALU.add))
                link(nc.vector.tensor_reduce(sm[3][:, m, :], ph(m, b), AX, ALU.max))
                sink = R("sinks")[:, 8 * m:8 * m + 8]
                link(tt(sm[3][:, m, :], sm[3][:, m, :], sink, ALU.max))
                ts(sm[0][:, m, :], sm[3][:, m, :], -1.0, None, ALU.mult).then_inc(S("at_m"), 1)
                tt(sm[2][:, m, :], sink, sm[3][:, m, :], ALU.subtract).then_inc(S("at_m"), 1)

            dve.wait_ge(S("bias"), 16)
            maxima(0)
            for n in range(2 * NT):
                b, m = n // 2, n % 2
                dve.wait_ge(S("at_p"), n + 1)
                link(tt(sm[1][:, m, :], sm[1][:, m, :], sm[2][:, m, :], ALU.add))
                link(nc.vector.reciprocal(sm[1][:, m, :], sm[1][:, m, :]))
                tt(ph(m, b), ph(m, b), sm[1][:, m, :].rearrange("p (a b) -> p a b", b=1).broadcast_to([P, 8, 256 if b else P]), ALU.mult).then_inc(S("at_pn"), 1)
                if n + 1 < 2 * NT:
                    maxima(n + 1)
                dve.wait_ge(S("at_pv"), n + 1)
                cp(h[:, 4 * m:4 * m + 4, b * P:(b + 1) * P], m4(PS[:, 4 * m, :])).then_inc(S("at_o"), 1)
            for j in range(4):
                w_lo(UIDX["w_o0"], j)
            h_lo()
            for m in range(2):
                residual(G_WO + m, m, bias_of=lambda k: V("b_b_o", k), next_unit=UIDX["w_o1"] + m)
            norm(6, V("f_norm", KD, KD), h, "h")
            h_lo()
            ffn(1, G_UP1, G_DN1)
            norm(7, V("final_norm", 0, KD), h, "h")

        @block.gpsimd
        def _(pool):
            pool.wait_ge(S("slots0"), 16)
            pool.wait_ge(S("small2"), 48)
            pool.wait_ge(S("posi"), 2)
            for t in range(NT):
                for c in range(2):
                    pool.indirect_dma_start(slots, bass.IndirectOffsetOnAxis(ap=posi[:, c, t:t + 1], axis=0),
                                            tok[:, 2 * t + c, :], None).then_inc(S(f"sc{c}"), 16)
            n = pairs(pool)
            for c in range(2):
                pool.wait_ge(S(f"sc{c}"), 16 * NT)
            pool.wait_ge(S("f_tok"), 16 * NT)

            def gather(b, j):
                pool.dma_start(idx[:, j, :], slots[bass.ds(b * P, P), :]).then_inc(S(f"idx{j}"), 16)

            def gather2(j, count):
                rwait(pool, S(f"idx{j}"), count)
                pool.indirect_dma_start(xg[j].rearrange("p a b -> p (a b)"), None, f_tok,
                                        bass.IndirectOffsetOnAxis(ap=idx[:, j, 0:1], axis=0)).then_inc(S(f"xg{j}"), 16)

            for j in range(2):
                gather(j, j)
            for j in range(2):
                gather2(j, 16)
            with pool.Fori(0, n) as i:
                for j in range(2):
                    rwait(pool, S(f"sc{j}"), 16 * i + 16 * NT)
                    rwait(pool, S(f"idx{j}"), 16 * i + 16)
                    nc.gpsimd.tensor_copy(sidx[:, j, :], idx[:, j, :]).then_inc(S("sidx"), 1)
                    rwait(pool, S("sidx"), 2 * i + j + 1)
                    rwait(pool, S(f"xg{j}"), 16 * i + 16)
                    gather(2 * i + 2 + j, j)
                    rwait(pool, S("m_tr"), m_turn(i, j))
                    gather2(j, 16 * i + 32)
                for j in range(2):
                    rwait(pool, S(f"m_y{j}"), i + 2)
                    pool.indirect_dma_start(y_asg, bass.IndirectOffsetOnAxis(ap=sidx[:, j, 1:2], axis=0),
                                            yb[j].rearrange("p a b -> p (a b)"), None, bounds_check=2 * T - 1,
                                            oob_is_err=False).then_inc(S(f"sc{j}"), 16)
            for j in range(2):
                rwait(pool, S(f"xg{j}"), 16 * n + 16)
                rwait(pool, S(f"idx{j}"), 16 * n + 16)


NORM_BANK = [0, 0, 0, 0, 0, 4, 0, 4]


def slab(w, k0, nk, c0, nc_=512):
    return w[k0 * P:(k0 + nk) * P, c0:c0 + nc_].reshape(nk, P, nc_).transpose(1, 0, 2)


def feat(v):
    return np.ascontiguousarray(v.reshape(-1, P).T)


def pack(I):
    g = {k: np.asarray(v) for k, v in I.items()}
    w_in, ada = g["w_in"][0], g["w_ada"][0]
    wall = np.zeros((NU, P, 8, 512), np.float32)

    def put(name, *slabs):
        o = 0
        for s in slabs:
            wall[UIDX[name], :, o:o + s.shape[1]] = s
            o += s.shape[1]

    wada = np.stack([slab(ada, 0, 8, 512 * a) for a in range(12)])
    for i in range(10):
        put(f"in{i}", slab(w_in, 0, 8, 512 * i if i < 6 else 512 * i + 2 * MH))
    for n in ("conv_out", "m_out"):
        w = g["w_" + n][0]
        put(n, slab(w, 0, 4, 0), slab(w, 0, 4, 512))
    for m in range(2):
        put(f"w_out{m}", slab(g["w_out"][0], 0, 8, 512 * m))
        put(f"a_out{m}", slab(g["a_w_out_2"][0], 0, 8, 512 * m))
        put(f"w_o{m}", slab(g["b_w_o_2"][0], 0, 8, 512 * m))
        wq = g["b_w_q_2"][0].reshape(D, 2, 2, 4, HD)[:, m].transpose(0, 2, 1, 3).reshape(D, 512)
        put(f"w_q{m}", slab(wq, 0, 8, 0))
    for i in range(8):
        put(f"a_in{i}", slab(g["a_w_in_2"][0], 0, 8, 512 * i))
    put("kv", slab(g["kv_w_2"], 0, 8, 0))
    for l in range(2):
        up, dn = g["f_w_up_2"][l], g["f_w_down_2"][l]
        for i in range(FU):
            u = np.concatenate([slab(up, 0, 8, 256 * i, 256), slab(up, 0, 8, FF + 256 * i, 256)], 2)
            put(f"up{l}_{i}", u)
        for m in range(2):
            for i in range(3):
                put(f"down{l}_{3 * m + i}", slab(dn, 8 * i, 8 if i < 2 else FT - 16, 512 * m))
    we = np.empty((E, 3, P, 8, 512), np.float32)
    we[:, 0] = g["w_e_gate"][0].reshape(E, 8, P, 512).transpose(0, 2, 1, 3)
    we[:, 1] = g["w_e_up"][0].reshape(E, 8, P, 512).transpose(0, 2, 1, 3)
    we[:, 2] = g["w_e_down"][0].reshape(E, 4, P, 2, 512).transpose(0, 2, 3, 1, 4).reshape(E, P, 8, 512)
    wif = np.zeros((P, KD, 64), np.float32)
    wi = w_in[:, 3072:3072 + 2 * MH].reshape(KD, P, 2 * MH).transpose(1, 0, 2)
    wif[:, :, 0:4], wif[:, :, 32:36] = wi[:, :, 0:4], wi[:, :, 4:8]
    wr = np.concatenate([g["w_rg"][0], g["w_re"][0]], 1).reshape(KD, P, NG + E).transpose(1, 0, 2)
    wab = g["a_w_in_2"][0][:, 4096:].reshape(KD, P, 2 * DH).transpose(1, 0, 2)
    bq = g["b_b_q_2"][0].reshape(2, 2, 4, HD).transpose(0, 2, 1, 3)
    src = dict(c=g["c"], b_ada=g["b_ada"], g_norm1=g["g_norm1"], conv_dw_w=g["conv_dw_w"], conv_dw_b=g["conv_dw_b"],
               conv_ln_g=g["conv_ln_g"], conv_ln_b=g["conv_ln_b"], qk_conv_w=g["qk_conv_w"], qk_conv_b=g["qk_conv_b"],
               m_norm_g=g["m_norm_g"], g_norm2=g["g_norm2"], g_final=g["g_final"], a_norm=g["a_norm_2"],
               a_conv_w=g["a_conv_w_2"], a_onorm=g["a_onorm_2"], kv_norm=g["kv_norm_2"], kv_b=g["kv_b_2"][:256],
               b_norm=g["b_norm_2"], b_b_q=bq, b_b_o=g["b_b_o_2"], f_norm=g["f_norm_2"], f_conv_w=g["f_conv_w_2"],
               f_conv_b=g["f_conv_b_2"], final_norm=g["final_norm_2"])
    vecs = np.concatenate([feat(np.ascontiguousarray(src[n])) for n, _ in VECS], 1)
    assert vecs.shape == (P, NVEC)
    rows = np.concatenate([g["b_rg"][0], g["b_re"][0], g["a_dt_bias_2"][0], g["a_A_log_2"][0], g["kv_b_2"][256:], g["b_sinks_2"][0]])
    p, f = np.arange(P)[:, None], np.arange(P)[None, :]
    lev = []
    for l in range(LEVELS):
        lev.append(-(((f >> l) == (p >> l) + 1) & ((f >> l) % 2 == 1)).astype(np.float32))
    zero = np.zeros((P, 1), np.float32)
    cst = np.concatenate([np.eye(P), np.ones((P, P)), np.where(f < p, NEG, 0.0), (p < f) * 1.0, (p <= f) * 1.0,
                          zero + np.arange(NG), zero + np.arange(EPG), zero + np.arange(NB)], 1).astype(np.float32)
    t = np.arange(P)[:, None, None] + P * np.arange(NT)[None, :, None] + 0 * np.arange(2)[None, None, :]
    tokens = np.stack([t, 2 * t + np.arange(2)], -1).reshape(P, -1)
    none = np.tile(np.array([0, 2 * T], np.int64), (P, NB + 2))
    ints = np.concatenate([tokens, none], 1).astype(np.int32)
    dist = p + P - np.arange(2 * P)[None, :]
    slopes = 2.0 ** (-8.0 * np.arange(1, AH + 1, dtype=np.float32) / AH)
    ok = (dist >= 0) & (dist < P)
    att = np.where(ok[:, None, :], -slopes[None, :, None] * dist[:, None, :], NEG).astype(np.float32)
    xt = np.ascontiguousarray(g["x"][0].T.reshape(KD, P, T).transpose(1, 0, 2))
    return dict(xt_in=xt, wada=wada, wall=wall, wexp=we, w_if=wif, w_router=np.ascontiguousarray(wr), w_ab=np.ascontiguousarray(wab),
                vecs=vecs, rows=rows, b_if=np.ascontiguousarray(g["b_if"].reshape(8, 1)), cst_in=cst, ints=ints, att_bias=att,
                levels_in=np.concatenate(lev, 1))


def kernel(**inputs):
    import concourse.bacc as bacc
    from concourse.bass_utils import run_bass_kernel_spmd

    arrays = {name: np.ascontiguousarray(v) for name, v in pack(inputs).items()}
    nc = bacc.Bacc("TRN2", target_bir_lowering=False, num_devices=1)
    handles = {name: nc.dram_tensor(name, list(v.shape), mybir.dt.from_np(v.dtype), kind="ExternalInput").ap() for name, v in arrays.items()}
    out_t = nc.dram_tensor("out_t", [P, KD, T], F32, kind="ExternalOutput").ap()
    build(nc, out_t=out_t, **handles)
    result = run_bass_kernel_spmd(nc, [arrays], core_ids=[0])
    return np.ascontiguousarray(result.results[0]["out_t"].transpose(1, 0, 2).reshape(D, T).T[None])
```
